# Optimizing a Trainium2 kernel written in Bass

```python
import jax, jax.numpy as jnp
from jax import lax
import numpy as np

D_MODEL = 1024
BATCH = 1
SEQ = 1024
DEPTH = 1

RWKV_HEADS = 8
RWKV_HEAD_DIM = 64
RWKV_DIM = RWKV_HEADS * RWKV_HEAD_DIM
DECAY_LORA = 64
ICLR_LORA = 64
GATE_LORA = 128
RWKV_GN_EPS = 64e-5
FOX_HEADS = 8
FOX_HEAD_DIM = 64
FOX_DIM = FOX_HEADS * FOX_HEAD_DIM
Q_BLOCK = 128
SSM_HEADS = 16
SSM_HEAD_DIM = 64
SSM_DIM = SSM_HEADS * SSM_HEAD_DIM
SSM_GROUPS = 2
SSM_STATE = 128
CONV_WIDTH = 4
SSD_CHUNK = 128
SSM_CONV_DIM = SSM_DIM + 2 * SSM_GROUPS * SSM_STATE
NORM_EPS = 1e-5
N_BRANCHES = 3
RWKV_COLS = 3 * RWKV_DIM + DECAY_LORA + ICLR_LORA + GATE_LORA
FOX_COLS = 3 * FOX_DIM + FOX_HEADS
SSM_COLS = SSM_DIM + SSM_CONV_DIM + SSM_HEADS
GATE_COLS = N_BRANCHES * D_MODEL
OFF_FOX = RWKV_COLS
OFF_SSM = OFF_FOX + FOX_COLS
OFF_GATE = OFF_SSM + SSM_COLS
IN_COLS = OFF_GATE + GATE_COLS
N_EXPERTS = 32
N_EXPERT_GROUPS = 4
EXPERTS_PER_GROUP = N_EXPERTS // N_EXPERT_GROUPS
TOP_K = 2
D_EXPERT = 512
DISPATCH_BLOCK = 128
DEEPNORM_ALPHA = (2 * DEPTH) ** 0.25
DEEPNORM_BETA = (8 * DEPTH) ** -0.25
LN_EPS = 1e-5

kernel_name = "hybrid_rwkv7_fox_mamba2_groupmoe_deepnorm"

def layer_norm(x, g, b):
    xf = x.astype(jnp.float32)
    mu = jnp.mean(xf, axis=-1, keepdims=True)
    var = jnp.mean(jnp.square(xf - mu), axis=-1, keepdims=True)
    y = (xf - mu) * lax.rsqrt(var + LN_EPS) * g.astype(jnp.float32) + b.astype(jnp.float32)
    return y.astype(x.dtype)

def token_shift(p):
    return jnp.pad(p[:, :-1], ((0, 0), (1, 0), (0, 0)))

def rwkv7_recurrence(r, w, k, v, a, b):
    Bsz, S, H, N = r.shape

    def step(state, inp):
        r_t, w_t, k_t, v_t, a_t, b_t = inp
        sa = jnp.einsum('bhij,bhj->bhi', state, a_t)
        state = (state * w_t[:, :, None, :] + sa[..., None] * b_t[:, :, None, :]
                 + v_t[..., None] * k_t[:, :, None, :])
        return state, jnp.einsum('bhij,bhj->bhi', state, r_t)

    xs = tuple(t.transpose(1, 0, 2, 3) for t in (r, w, k, v, a, b))
    _, y = lax.scan(step, jnp.zeros((Bsz, H, N, N), jnp.float32), xs)
    return y.transpose(1, 0, 2, 3)

def rwkv7_mixer(p, mu, w0, w_up, a0, a_up, g_up, k_k, k_a, r_k, gn_g, gn_b):
    Bsz, S, _ = p.shape
    f32 = jnp.float32
    p = p + mu * (token_shift(p) - p)
    R = RWKV_DIM
    r, k, v, wd, ad, gd = jnp.split(p, [R, 2 * R, 3 * R, 3 * R + DECAY_LORA,
                                        3 * R + DECAY_LORA + ICLR_LORA], axis=-1)
    w_raw = -jax.nn.softplus(-(w0 + jnp.tanh(wd) @ w_up)) - 0.5
    decay = jnp.exp(-jnp.exp(w_raw.astype(f32)))
    a = jax.nn.sigmoid(a0 + ad @ a_up)
    g = jax.nn.sigmoid(gd) @ g_up
    hs = lambda t: t.astype(f32).reshape(Bsz, S, RWKV_HEADS, RWKV_HEAD_DIM)
    hv = lambda t: t.astype(f32).reshape(RWKV_HEADS, RWKV_HEAD_DIM)
    r, k, v, a, decay = hs(r), hs(k), hs(v), hs(a), hs(decay)
    kk = k * hv(k_k)
    kk = kk / jnp.maximum(jnp.sqrt(jnp.sum(kk * kk, axis=-1, keepdims=True)), 1e-12)
    k = k * (1.0 + (a - 1.0) * hv(k_a))
    y = rwkv7_recurrence(r, decay, k, v, -kk, kk * a)
    mean = jnp.mean(y, axis=-1, keepdims=True)
    var = jnp.mean(jnp.square(y - mean), axis=-1, keepdims=True)
    y = (y - mean) * lax.rsqrt(var + RWKV_GN_EPS)
    y = y * hv(gn_g) + hv(gn_b)
    y = y + jnp.sum(r * k * hv(r_k), axis=-1, keepdims=True) * v
    y = y.reshape(Bsz, S, RWKV_DIM) * g.astype(f32)
    return y.astype(p.dtype)

def fox_mixer(p, f_bias):
    Bsz, S, _ = p.shape
    f32 = jnp.float32
    q, k, v, f = jnp.split(p, [FOX_DIM, 2 * FOX_DIM, 3 * FOX_DIM], axis=-1)
    hs = lambda t: t.astype(f32).reshape(Bsz, S, FOX_HEADS, FOX_HEAD_DIM)
    q, k, v = hs(q), hs(k), hs(v)
    log_f = jax.nn.log_sigmoid(f.astype(f32) + f_bias.astype(f32))
    c = jnp.cumsum(log_f, axis=1)
    c_key = c.transpose(0, 2, 1)
    nb = S // Q_BLOCK
    qb = q.reshape(Bsz, nb, Q_BLOCK, FOX_HEADS, FOX_HEAD_DIM).transpose(1, 0, 2, 3, 4)
    cb = c.reshape(Bsz, nb, Q_BLOCK, FOX_HEADS).transpose(1, 0, 3, 2)
    kpos = jnp.arange(S)
    scale = FOX_HEAD_DIM ** -0.5

    def block(args):
        qi, ci, i = args
        s = jnp.einsum('bqhe,bkhe->bhqk', qi, k) * scale
        s = s + ci[..., None] - c_key[:, :, None, :]
        qpos = i * Q_BLOCK + jnp.arange(Q_BLOCK)
        s = jnp.where(kpos[None, :] <= qpos[:, None], s, -jnp.inf)
        return jnp.einsum('bhqk,bkhe->bqhe', jax.nn.softmax(s, axis=-1), v)

    o = lax.map(block, (qb, cb, jnp.arange(nb)))
    return o.transpose(1, 0, 2, 3, 4).reshape(Bsz, S, FOX_DIM).astype(p.dtype)

def causal_depthwise_conv(u, w, b):
    out = lax.conv_general_dilated(u, w[:, None, :], window_strides=(1,),
                                   padding=[(CONV_WIDTH - 1, 0)],
                                   dimension_numbers=('NWC', 'WIO', 'NWC'),
                                   feature_group_count=u.shape[-1])
    return out + b

def segsum(a):
    T = a.shape[-1]
    cs = jnp.cumsum(a, axis=-1)
    diff = cs[..., :, None] - cs[..., None, :]
    return jnp.where(jnp.tril(jnp.ones((T, T), bool)), diff, -jnp.inf)

def ssd(x, dt, A, Bm, Cm):
    Bsz, S, H, P = x.shape
    G, N = Bm.shape[2], Bm.shape[3]
    E = H // G
    L = SSD_CHUNK
    nc = S // L
    X = (x * dt[..., None]).reshape(Bsz, nc, L, G, E, P)
    dA = (dt * A).reshape(Bsz, nc, L, G, E).transpose(0, 3, 4, 1, 2)
    Bc = Bm.reshape(Bsz, nc, L, G, N)
    Cc = Cm.reshape(Bsz, nc, L, G, N)
    A_cs = jnp.cumsum(dA, axis=-1)
    Lmat = jnp.exp(segsum(dA))
    CB = jnp.einsum('bclgn,bcsgn->bcgls', Cc, Bc)
    y_diag = jnp.einsum('bcgls,bgecls,bcsgep->bclgep', CB, Lmat, X)
    decay_states = jnp.exp(A_cs[..., -1:] - A_cs)
    states = jnp.einsum('bclgn,bgecl,bclgep->bcgepn', Bc, decay_states, X)
    states = jnp.concatenate([jnp.zeros_like(states[:, :1]), states], axis=1)
    chunk_decay = jnp.exp(segsum(jnp.pad(A_cs[..., -1], ((0, 0), (0, 0), (0, 0), (1, 0)))))
    states = jnp.einsum('bgezc,bcgepn->bzgepn', chunk_decay, states)[:, :-1]
    y_off = jnp.einsum('bclgn,bcgepn,bgecl->bclgep', Cc, states, jnp.exp(A_cs))
    return (y_diag + y_off).reshape(Bsz, S, H, P)

def mamba2_mixer(p, conv_w, conv_b, dt_bias, a_log, d_skip, norm_g):
    Bsz, S, _ = p.shape
    f32 = jnp.float32
    z, xbc, dt = jnp.split(p, [SSM_DIM, SSM_DIM + SSM_CONV_DIM], axis=-1)
    xbc = jax.nn.silu(causal_depthwise_conv(xbc, conv_w, conv_b)).astype(f32)
    xs, Bm, Cm = jnp.split(xbc, [SSM_DIM, SSM_DIM + SSM_GROUPS * SSM_STATE], axis=-1)
    xs = xs.reshape(Bsz, S, SSM_HEADS, SSM_HEAD_DIM)
    Bm = Bm.reshape(Bsz, S, SSM_GROUPS, SSM_STATE)
    Cm = Cm.reshape(Bsz, S, SSM_GROUPS, SSM_STATE)
    dt = jax.nn.softplus(dt.astype(f32) + dt_bias.astype(f32))
    A = -jnp.exp(a_log.astype(f32))
    y = ssd(xs, dt, A, Bm, Cm) + d_skip.astype(f32)[:, None] * xs
    y = y.reshape(Bsz, S, SSM_DIM) * jax.nn.silu(z.astype(f32))
    y = y.reshape(Bsz, S, SSM_GROUPS, SSM_DIM // SSM_GROUPS)
    y = y * lax.rsqrt(jnp.mean(y * y, axis=-1, keepdims=True) + NORM_EPS)
    y = y.reshape(Bsz, S, SSM_DIM) * norm_g.astype(f32)
    return y.astype(p.dtype)

def hybrid_mixer(x, w_in, rwkv_mu, rwkv_w0, rwkv_w_up, rwkv_a0, rwkv_a_up, rwkv_g_up,
                 rwkv_k_k, rwkv_k_a, rwkv_r_k, rwkv_gn_g, rwkv_gn_b, fox_f_bias,
                 ssm_conv_w, ssm_conv_b, ssm_dt_bias, ssm_a_log, ssm_d, ssm_norm_g,
                 gate_bias, w_br_rwkv, w_br_fox, w_br_ssm, w_out):
    Bsz, S, D = x.shape
    proj = x @ w_in
    p_rwkv = proj[..., :OFF_FOX]
    p_fox = proj[..., OFF_FOX:OFF_SSM]
    p_ssm = proj[..., OFF_SSM:OFF_GATE]
    p_gate = proj[..., OFF_GATE:].reshape(Bsz, S, N_BRANCHES, D)
    o_r = rwkv7_mixer(p_rwkv, rwkv_mu, rwkv_w0, rwkv_w_up, rwkv_a0, rwkv_a_up, rwkv_g_up,
                      rwkv_k_k, rwkv_k_a, rwkv_r_k, rwkv_gn_g, rwkv_gn_b)
    o_f = fox_mixer(p_fox, fox_f_bias)
    o_m = mamba2_mixer(p_ssm, ssm_conv_w, ssm_conv_b, ssm_dt_bias, ssm_a_log, ssm_d, ssm_norm_g)
    gates = jax.nn.sigmoid(p_gate + gate_bias)
    merged = (gates[:, :, 0] * (o_r @ w_br_rwkv) + gates[:, :, 1] * (o_f @ w_br_fox)
              + gates[:, :, 2] * (o_m @ w_br_ssm))
    return merged @ w_out

def moe_ffn(x, router_w, router_bias, w_gate, w_up, w_down):
    Bsz, S, D = x.shape
    N = Bsz * S
    x2 = x.reshape(N, D)
    f32 = jnp.float32
    aff = jax.nn.sigmoid(x2.astype(f32) @ router_w.astype(f32))
    sel = aff + router_bias.astype(f32)
    grp_score = lax.top_k(sel.reshape(N, N_EXPERT_GROUPS, EXPERTS_PER_GROUP), TOP_K)[0].sum(-1)
    top_grp = jnp.argmax(grp_score, axis=-1)
    in_grp = (jnp.arange(N_EXPERTS) // EXPERTS_PER_GROUP)[None, :] == top_grp[:, None]
    _, idx = lax.top_k(jnp.where(in_grp, sel, -jnp.inf), TOP_K)
    w_sel = jnp.take_along_axis(aff, idx, axis=-1)
    gate = w_sel / jnp.sum(w_sel, axis=-1, keepdims=True)
    M = N * TOP_K
    BLK = DISPATCH_BLOCK
    flat_e = idx.reshape(M)
    flat_tok = jnp.broadcast_to(jnp.arange(N, dtype=jnp.int32)[:, None], (N, TOP_K)).reshape(M)
    flat_gate = gate.reshape(M)
    order = jnp.argsort(flat_e)
    e_sorted, tok_sorted, gate_sorted = flat_e[order], flat_tok[order], flat_gate[order]
    counts = jnp.bincount(flat_e, length=N_EXPERTS)
    padded = (counts + BLK - 1) // BLK * BLK
    pad_end = jnp.cumsum(padded)
    pad_start = pad_end - padded
    start = jnp.cumsum(counts) - counts
    dest = pad_start[e_sorted] + jnp.arange(M) - start[e_sorted]
    n_blocks = -(-M // BLK) + N_EXPERTS
    buf_tok = jnp.zeros((n_blocks * BLK,), jnp.int32).at[dest].set(tok_sorted)
    block_expert = jnp.minimum(jnp.searchsorted(pad_end, jnp.arange(n_blocks) * BLK, side='right'),
                               N_EXPERTS - 1)
    xb = x2[buf_tok].reshape(n_blocks, BLK, D)

    def expert_block(args):
        xblk, e = args
        h = jax.nn.silu(xblk @ w_gate[e]) * (xblk @ w_up[e])
        return h @ w_down[e]

    yb = lax.map(expert_block, (xb, block_expert)).reshape(n_blocks * BLK, D)
    y = jnp.zeros((N, D), x.dtype).at[tok_sorted].add(yb[dest] * gate_sorted[:, None].astype(x.dtype))
    return y.reshape(Bsz, S, D)

def setup_inputs(seed: int = 0) -> dict:
    key = jax.random.key(seed)
    keys = list(jax.random.split(key, 48))
    cnt = [0]
    f32 = jnp.float32

    def nk():
        cnt[0] += 1
        return keys[cnt[0] - 1]

    def normal(shape, scale):
        return jax.random.normal(nk(), shape, f32) * scale

    def uniform(shape, lo, hi):
        return jax.random.uniform(nk(), shape, f32, lo, hi)

    L, D = DEPTH, D_MODEL
    x = normal((BATCH, SEQ, D), 1.0)
    w_in = normal((L, D, IN_COLS), D ** -0.5)
    rwkv_mu = uniform((L, RWKV_COLS), 0.0, 1.0)
    rwkv_w0 = uniform((L, RWKV_DIM), -6.5, -1.5)
    rwkv_w_up = normal((L, DECAY_LORA, RWKV_DIM), 0.1 * DECAY_LORA ** -0.5)
    rwkv_a0 = normal((L, RWKV_DIM), 0.1)
    rwkv_a_up = normal((L, ICLR_LORA, RWKV_DIM), ICLR_LORA ** -0.5)
    rwkv_g_up = normal((L, GATE_LORA, RWKV_DIM), GATE_LORA ** -0.5)
    rwkv_k_k = 0.85 + normal((L, RWKV_DIM), 0.05)
    rwkv_k_a = 1.0 + normal((L, RWKV_DIM), 0.05)
    rwkv_r_k = normal((L, RWKV_DIM), 0.1)
    rwkv_gn_g = 1.0 + normal((L, RWKV_DIM), 0.05)
    rwkv_gn_b = normal((L, RWKV_DIM), 0.02)
    fox_f_bias = uniform((L, FOX_HEADS), 1.0, 4.0)
    ssm_conv_w = normal((L, CONV_WIDTH, SSM_CONV_DIM), CONV_WIDTH ** -0.5)
    ssm_conv_b = normal((L, SSM_CONV_DIM), 0.02)
    dt0 = jnp.exp(uniform((L, SSM_HEADS), float(np.log(1e-3)), float(np.log(1e-1))))
    ssm_dt_bias = dt0 + jnp.log(-jnp.expm1(-dt0))
    ssm_a_log = jnp.log(uniform((L, SSM_HEADS), 1.0, 16.0))
    ssm_d = 1.0 + normal((L, SSM_HEADS), 0.1)
    ssm_norm_g = 1.0 + normal((L, SSM_DIM), 0.05)
    gate_bias = normal((L, N_BRANCHES, D), 0.02)
    w_br_rwkv = normal((L, RWKV_DIM, D), RWKV_DIM ** -0.5)
    w_br_fox = normal((L, FOX_DIM, D), FOX_DIM ** -0.5)
    w_br_ssm = normal((L, SSM_DIM, D), SSM_DIM ** -0.5)
    w_out = normal((L, D, D), DEEPNORM_BETA * D ** -0.5)
    ln1_g = 1.0 + normal((L, D), 0.05)
    ln1_b = normal((L, D), 0.02)
    router_w = normal((D, N_EXPERTS), D ** -0.5)
    router_bias = normal((N_EXPERTS,), 0.01)
    exp_w_gate = normal((L, N_EXPERTS, D, D_EXPERT), D ** -0.5)
    exp_w_up = normal((L, N_EXPERTS, D, D_EXPERT), D ** -0.5)
    exp_w_down = normal((L, N_EXPERTS, D_EXPERT, D), DEEPNORM_BETA * D_EXPERT ** -0.5)
    ln2_g = 1.0 + normal((L, D), 0.05)
    ln2_b = normal((L, D), 0.02)
    return {"x": x, "w_in": w_in, "rwkv_mu": rwkv_mu, "rwkv_w0": rwkv_w0,
            "rwkv_w_up": rwkv_w_up, "rwkv_a0": rwkv_a0, "rwkv_a_up": rwkv_a_up,
            "rwkv_g_up": rwkv_g_up, "rwkv_k_k": rwkv_k_k, "rwkv_k_a": rwkv_k_a,
            "rwkv_r_k": rwkv_r_k, "rwkv_gn_g": rwkv_gn_g, "rwkv_gn_b": rwkv_gn_b,
            "fox_f_bias": fox_f_bias, "ssm_conv_w": ssm_conv_w, "ssm_conv_b": ssm_conv_b,
            "ssm_dt_bias": ssm_dt_bias, "ssm_a_log": ssm_a_log, "ssm_d": ssm_d,
            "ssm_norm_g": ssm_norm_g, "gate_bias": gate_bias, "w_br_rwkv": w_br_rwkv,
            "w_br_fox": w_br_fox, "w_br_ssm": w_br_ssm, "w_out": w_out,
            "ln1_g": ln1_g, "ln1_b": ln1_b, "router_w": router_w, "router_bias": router_bias,
            "exp_w_gate": exp_w_gate, "exp_w_up": exp_w_up, "exp_w_down": exp_w_down,
            "ln2_g": ln2_g, "ln2_b": ln2_b}

def reference(x, w_in, rwkv_mu, rwkv_w0, rwkv_w_up, rwkv_a0, rwkv_a_up, rwkv_g_up,
              rwkv_k_k, rwkv_k_a, rwkv_r_k, rwkv_gn_g, rwkv_gn_b, fox_f_bias,
              ssm_conv_w, ssm_conv_b, ssm_dt_bias, ssm_a_log, ssm_d, ssm_norm_g,
              gate_bias, w_br_rwkv, w_br_fox, w_br_ssm, w_out, ln1_g, ln1_b,
              router_w, router_bias, exp_w_gate, exp_w_up, exp_w_down, ln2_g, ln2_b):
    for l in range(DEPTH):
        mix = hybrid_mixer(x, w_in[l], rwkv_mu[l], rwkv_w0[l], rwkv_w_up[l], rwkv_a0[l],
                           rwkv_a_up[l], rwkv_g_up[l], rwkv_k_k[l], rwkv_k_a[l], rwkv_r_k[l],
                           rwkv_gn_g[l], rwkv_gn_b[l], fox_f_bias[l], ssm_conv_w[l],
                           ssm_conv_b[l], ssm_dt_bias[l], ssm_a_log[l], ssm_d[l],
                           ssm_norm_g[l], gate_bias[l], w_br_rwkv[l], w_br_fox[l],
                           w_br_ssm[l], w_out[l])
        x = layer_norm(DEEPNORM_ALPHA * x + mix, ln1_g[l], ln1_b[l])
        ffn = moe_ffn(x, router_w, router_bias, exp_w_gate[l], exp_w_up[l], exp_w_down[l])
        x = layer_norm(DEEPNORM_ALPHA * x + ffn, ln2_g[l], ln2_b[l])
    return x


_drawn_inputs = setup_inputs


def setup_inputs(seed=0):
    import zlib

    import numpy as np

    out = dict(_drawn_inputs(seed))
    spreads = {}
    factors = {'rwkv_w_up': 24.04,
     'rwkv_gn_b': 3.598,
     'gate_bias': 4.389,
     'ln2_b': 2.843,
     'rwkv_a0': 2.761,
     'rwkv_k_a': 3.044,
     'rwkv_gn_g': 2.82}
    for name, (base, spread) in spreads.items():
        noise = np.random.default_rng([zlib.crc32(name.encode()), seed]).standard_normal(out[name].shape)
        drawn = base * np.exp(spread * noise) if base else spread * noise
        out[name] = __import__('jax').numpy.asarray(drawn.astype(out[name].dtype))
    for name, factor in factors.items():
        out[name] = (out[name] * factor).astype(out[name].dtype)
    return out
```

```python
from contextlib import ExitStack

import numpy as np
import concourse.bass as bass
from concourse import mybir

F32 = mybir.dt.float32
BF16 = mybir.dt.bfloat16
I32 = mybir.dt.int32
U32 = mybir.dt.uint32
ALU = mybir.AluOpType
ACT = mybir.ActivationFunctionType
AX = mybir.AxisListType

P = 128
D = 1024
T = 1024
KD = D // P
NT = T // P
HALF = 512
RH, HD = 8, 64
RT = RH * HD // P
FH = 8
SH, SG, SN = 16, 2, 128
ST = SH * HD // P
NCONV = 12
TAPS = 4
E, EG, EPG = 32, 4, 8
DE = 512
FF = DE // P
OVER = 15
N_BLOCKS = E + OVER
KAPPA = float(np.exp(-0.5))
RWKV_EPS, NORM_EPS, LN_EPS = 64e-5, 1e-5, 1e-5
ALPHA = 2.0 ** 0.25
NEG = -1.0e30

T_R, T_K, T_V, T_WA, T_G = 0, 4, 8, 12, 13
T_FQ, T_FK = 14, 18
T_Z, T_XBC = 22, 30
T_GATE = 42
N_TILES = 66

COLS = {}
_at = 0
for _name, _n in (("mu", 14), ("w0", RT), ("a0", RT), ("k_k", RT), ("k_a", RT), ("r_k", RT), ("gn_g", RT), ("gn_b", RT),
                  ("conv_w", TAPS * NCONV), ("conv_b", NCONV), ("ssm_d", ST), ("norm_g", ST), ("gate_bias", 3 * KD)):
    COLS[_name] = _at
    _at += _n
N_COLS = _at

MATS = {}
_at = 0
for _name, _n in (("ident", P), ("ones", P), ("head_ones", P), ("before", P), ("before_or_at", P), ("after", P),
                  ("levels", 7 * P), ("level0_t", P), ("reset", T), ("experts", E),
                  ("group_of", E), ("slot0", E), ("row0", 16), ("over_ids", 16)):
    MATS[_name] = _at
    _at += _n
N_MATS = _at


def constant_matrices():
    m = np.zeros((P, N_MATS), np.float32)
    i, j = np.arange(P)[:, None], np.arange(P)[None, :]

    def put(name, what):
        m[:, MATS[name]:MATS[name] + what.shape[1]] = what

    put("ident", (i == j) * 1.0)
    put("ones", np.ones((P, P)))
    put("head_ones", (i // HD == j // HD) * 1.0)
    put("before", (i < j) * 1.0)
    put("before_or_at", (i <= j) * 1.0)
    put("after", (i > j) * 1.0)
    for n in range(7):
        b = 1 << n
        level = (i // (2 * b) == j // (2 * b)) & (i % (2 * b) >= b) & (j % (2 * b) < b)
        m[:, MATS["levels"] + n * P:MATS["levels"] + (n + 1) * P] = level if n == 0 else level + (i == j)
        if n == 0:
            put("level0_t", level.T * 1.0)
    put("reset", np.broadcast_to(np.arange(T) % P != 0, (P, T)) * 1.0)
    e = np.broadcast_to(np.arange(E), (P, E))
    put("experts", e * 1.0)
    put("group_of", e // EPG * 1.0)
    put("slot0", e * float(P))
    put("row0", np.broadcast_to(i, (P, 16)) * 1.0)
    put("over_ids", np.broadcast_to(np.arange(16), (P, 16)) * 1.0)
    return m


def head_rows():
    return np.ascontiguousarray(np.broadcast_to(np.eye(SH, dtype=np.float32)[:, :, None], (SH, SH, P)))


class Chain:

    def __init__(self, eng, sem, per_round=0):
        self.eng, self.sem, self.n, self.base, self.per_round = eng, sem, 0, 0, per_round

    def round(self, i):
        assert self.n in (0, self.per_round) or self.base is None, (self.n, self.per_round)
        self.base, self.n = i * self.per_round, 0

    def __call__(self, ins):
        self.n += 1
        ins.then_inc(self.sem, 1)
        self.eng.wait_ge(self.sem, self.base + self.n)

    def done(self):
        assert self.n == self.per_round, (self.n, self.per_round)


class Space:

    def __init__(self, nc, stage):
        self.nc, self.stage, self.ctx, self.sems = nc, stage, ExitStack(), []

    def __enter__(self):
        return self

    def __exit__(self, *a):
        if a[0] is None:
            self.nc.clear_and_free_semaphores(self.sems)
            self.nc.all_engine_barrier()
        return self.ctx.__exit__(*a)

    def sb(self, name, shape, dt=F32):
        return self.ctx.enter_context(self.nc.sbuf_tensor(f"{self.stage}_sb_{name}", shape, dt))

    def ps(self, name, shape, dt=F32):
        return self.ctx.enter_context(self.nc.psum_tensor(f"{self.stage}_ps_{name}", shape, dt))

    def sem(self, name):
        self.sems.append(self.nc.alloc_semaphore(f"{self.stage}_{name}"))
        return self.sems[-1]

    def block(self):
        return self.nc.Block()


def wait_apart(eng, sem, value, stood):
    eng.wait_ge(sem, value)
    eng.sem_inc(stood, 1)


def col(k, name, i=0):
    return k.cols[:, bass.ds(i + COLS[name], 1)]


def mat(k, name, n=P, at=0):
    return k.mats[:, MATS[name] + at:MATS[name] + at + n]


def project(nc, out, w, xT, halves=(0, 1)):
    for half in halves:
        for k in range(KD):
            last = nc.tensor.matmul(out[:, half, :], w[:, k, :], xT[:, k, half * HALF:(half + 1) * HALF],
                                    start=(k == 0), stop=(k == KD - 1))
    return last


def transpose_x(nc, k):
    with Space(nc, "xt") as s:
        xs = [s.sb(f"x{b}", [P, D]) for b in range(2)]
        ps = [s.ps(f"t{b}", [P, KD, P]) for b in range(2)]
        consts_in = s.sem("consts_in")
        x_in = [s.sem(f"x_in{b}") for b in range(2)]
        turned = s.sem("turned")
        copied = [s.sem(f"copied{h}") for h in range(2)]
        x_rows = k.x.rearrange("a (n p) d -> (a n) p d", p=P)
        with s.block() as block:
            @block.sync
            def _(sp):
                sp.dma_start(k.mats[:, :], k.mats_d).then_inc(consts_in, 16)
                sp.dma_start(k.cols[:, :], k.cols_d).then_inc(consts_in, 16)
                with sp.Fori(0, NT // 2) as i:
                    for b in range(2):
                        sp.wait_ge(turned, 2 * i + b + 1)
                        sp.dma_start(xs[b][:, :], x_rows[bass.ds(2 * i + b, 1)].rearrange("a p d -> (a p) d")
                                     ).then_inc(x_in[b], 16)
                sp.wait_ge(consts_in, 32)

            @block.tensor
            def _(pe):
                pe.sem_inc(turned, 2)
                pe.wait_ge(consts_in, 32)
                with pe.Fori(0, NT // 2) as i:
                    for b in range(2):
                        pe.wait_ge(x_in[b], 16 * i + 16)
                        for h in range(2):
                            pe.wait_ge(copied[h], 2 * i + b + 1)
                        for c in range(KD):
                            last = nc.tensor.transpose(ps[b][:, c, :], xs[b][:, c * P:(c + 1) * P], mat(k, "ident"))
                        last.then_inc(turned, 1)

            def copy_half(eng, op, half):
                eng.sem_inc(copied[half], 2)
                with eng.Fori(0, NT // 2) as i:
                    for b in range(2):
                        eng.wait_ge(turned, 2 * i + b + 3)
                        op(k.xT[:, half * 4:half * 4 + 4, bass.ts(2 * i + b, P)],
                           ps[b][:, half * 4:half * 4 + 4, :]).then_inc(copied[half], 1)

            @block.scalar
            def _(act):
                copy_half(act, nc.scalar.copy, 0)

            @block.vector
            def _(dve):
                copy_half(dve, nc.vector.tensor_copy, 1)


def rwkv_inputs(nc, k):
    with Space(nc, "ri") as s:
        w_k, w_v, w_r = s.sb("w_k", [P, KD, P]), s.sb("w_v", [P, KD, P]), s.sb("w_r", [P, KD, P])
        w_up = s.sb("w_up", [P, P])
        raw_k, raw_v, raw_r = (s.sb(f"raw_{n}", [P, T + 4]) for n in "kvr")
        diff = s.sb("diff", [P, T])
        wa = s.sb("wa", [P, T])
        kx, vx, rx = s.sb("kx", [P, T]), s.sb("vx", [P, T]), s.sb("rx", [P, T])
        kk, sq, norm = s.sb("kk", [P, T]), s.sb("sq", [P, T]), s.sb("norm", [P, T])
        sg, cum, cc, cx = s.sb("sg", [P, T]), s.sb("cum", [P, T]), s.sb("cc", [P, T]), s.sb("cx", [P, T])
        rate, k2, b, rkk = s.sb("rate", [P, T]), s.sb("k2", [P, T]), s.sb("b", [P, T]), s.sb("rkk", [P, T])
        e_pos, e_neg, e_ex = s.sb("e_pos", [P, T]), cc, cx
        ch = k.spare.rearrange("p a t -> p (a t)").rearrange("p (c n t) -> p c n t", c=NT, n=4)
        tok = s.sb("tok", [P, 3, NT, P])
        span = s.sb("span", [P, NT])
        ka1 = s.sb("ka1", [P, RT])
        ps_a, ps_b = s.ps("a", [P, 2, HALF]), s.ps("b", [P, 2, HALF])
        ps_x, ps_t = s.ps("x", [P, 2, HALF]), s.ps("t", [P, NT, P])
        (k_loaded, v_loaded, r_loaded, up_loaded, ch_out, tok_out) = (
            s.sem(n) for n in ("k_loaded", "v_loaded", "r_loaded", "up_loaded", "ch_out", "tok_out"))
        (inner_proj, k_proj, v_proj, r_proj, lora_w, lora_a, norm_sum, bonus_sum, turned) = (
            s.sem(n) for n in ("inner_proj", "k_proj", "v_proj", "r_proj", "lora_w", "lora_a", "norm_sum", "bonus_sum",
                               "turned"))
        (inner_raw, inner_done, k_raw, v_raw, r_raw, sg_ready, rate_ready, sq_ready, norm_ready, exps_ready, tok_ready) = (
            s.sem(n) for n in ("inner_raw", "inner_done", "k_raw", "v_raw", "r_raw", "sg_ready", "rate_ready",
                               "sq_ready", "norm_ready", "exps_ready", "tok_ready"))
        (inner_mixed, pads, k_mixed, v_mixed, r_mixed, kk_ready, cc_ready, ch_ready, rkk_ready, bonus_ready, dve_last) = (
            s.sem(n) for n in ("inner_mixed", "pads", "k_mixed", "v_mixed", "r_mixed", "kk_ready", "cc_ready",
                               "ch_ready", "rkk_ready", "bonus_ready", "dve_last"))
        norm_floored, tok_free = s.sem("norm_floored"), s.sem("tok_free")

        def w_tile(i):
            return k.w_tiles[bass.ds(i, 1)].rearrange("a p k c -> (a p) k c")

        def up_tile(w, i):
            return w[:, bass.ts(i, P)]

        def rounds(eng, body):
            body(0, True)
            with eng.Fori(1, RT) as i:
                body(i, False)

        with s.block() as block:
            @block.sync
            def _(sp):
                sp.dma_start(w_k[:, :, :], k.w_tiles[T_WA]).then_inc(k_loaded, 16)
                sp.dma_start(w_v[:, :, :], k.w_tiles[T_G]).then_inc(v_loaded, 16)

                def load(i, first):
                    sp.wait_ge(inner_proj, 1) if first else sp.wait_ge(k_proj, i)
                    sp.dma_start(w_k[:, :, :], w_tile(i + T_K)).then_inc(k_loaded, 16)
                    sp.wait_ge(inner_proj, 2) if first else sp.wait_ge(v_proj, i)
                    sp.dma_start(w_v[:, :, :], w_tile(i + T_V)).then_inc(v_loaded, 16)
                    if not first:
                        sp.wait_ge(lora_a, i)
                    sp.dma_start(w_up[0:HD, :], up_tile(k.rwkv_w_up, i)).then_inc(up_loaded, 16)
                    sp.dma_start(w_up[HD:P, :], up_tile(k.rwkv_a_up, i)).then_inc(up_loaded, 16)
                    if not first:
                        sp.wait_ge(r_proj, i)
                    sp.dma_start(w_r[:, :, :], w_tile(i + T_R)).then_inc(r_loaded, 16)

                rounds(sp, load)

            @block.gpsimd
            def _(pool):
                def store(i, first):
                    if not first:
                        pool.wait_ge(tok_out, 48 * i)
                    pool.sem_inc(tok_free, 1)
                    pool.wait_ge(ch_ready, i + 1)
                    pool.dma_start(k.chunk_ch[:, :, bass.ds(i, 1)].rearrange("c p o a b -> p c (o a b)"),
                                   ch[:, :, :, :].rearrange("p c a b -> p c (a b)")).then_inc(ch_out, 16)
                    for n in range(3):
                        pool.wait_ge(tok_ready, 3 * i + n + 2)
                        pool.dma_start(k.chunk_tok[n, :, :, bass.ds(i, 1)].rearrange("c p o b -> p c (o b)"),
                                       tok[:, n, :, :]).then_inc(tok_out, 16)

                rounds(pool, store)
                pool.wait_ge(ch_out, 16 * RT)
                pool.wait_ge(tok_out, 48 * RT)

            @block.tensor
            def _(pe):
                pe.wait_ge(k_loaded, 16)
                project(nc, ps_a, w_k, k.xT).then_inc(inner_proj, 1)
                pe.wait_ge(v_loaded, 16)
                project(nc, ps_b, w_v, k.xT).then_inc(inner_proj, 1)

                def both(out, lhsT, rhs, lo=0, hi=P):
                    for h in range(2):
                        last = nc.tensor.matmul(out[:, h, :], lhsT, rhs[lo:hi, h * HALF:(h + 1) * HALF],
                                                start=True, stop=True)
                    return last

                def finish(i):
                    pe.wait_ge(rkk_ready, i)
                    pe.wait_ge(norm_ready, i)
                    both(ps_x, mat(k, "head_ones"), rkk).then_inc(bonus_sum, 1)
                    pe.wait_ge(ch_ready, i)
                    pe.wait_ge(v_mixed, i)
                    for n in range(3):
                        pe.wait_ge(tok_ready, 3 * i + n - 3 + 1)
                        for c in range(NT):
                            src = vx[:, c * P:(c + 1) * P] if n == 0 else ch[:, c, 1 + n, :]
                            last = nc.tensor.transpose(ps_t[:, c, :], src, mat(k, "ident"))
                        last.then_inc(turned, 1)

                def body(i, first):
                    pe.wait_ge(k_loaded, 16 * i + 32)
                    if first:
                        pe.wait_ge(inner_raw, 1)
                    else:
                        pe.wait_ge(r_raw, i)
                    project(nc, ps_a, w_k, k.xT).then_inc(k_proj, 1)
                    if not first:
                        finish(i)
                    pe.wait_ge(v_loaded, 16 * i + 32)
                    if first:
                        pe.wait_ge(inner_raw, 2)
                    else:
                        pe.wait_ge(v_raw, i)
                    project(nc, ps_b, w_v, k.xT).then_inc(v_proj, 1)
                    pe.wait_ge(up_loaded, 32 * i + 32)
                    if first:
                        pe.wait_ge(inner_done, 3)
                    else:
                        pe.wait_ge(bonus_ready, i)
                    both(ps_x, w_up[0:HD, :], wa, 0, HD).then_inc(lora_w, 1)
                    pe.wait_ge(sg_ready, i + 1)
                    both(ps_x, w_up[HD:P, :], wa, HD, P).then_inc(lora_a, 1)
                    pe.wait_ge(rate_ready, i + 1)
                    pe.wait_ge(sq_ready, i + 1)
                    both(ps_x, mat(k, "head_ones"), sq).then_inc(norm_sum, 1)
                    pe.wait_ge(r_loaded, 16 * i + 16)
                    pe.wait_ge(k_raw, i + 1)
                    project(nc, ps_a, w_r, k.xT).then_inc(r_proj, 1)

                rounds(pe, body)
                finish(RT)

            @block.scalar
            def _(act):
                act.sem_inc(tok_ready, 1)
                flat = lambda ps: ps[:, :, :].rearrange("p a b -> p (a b)")
                act.wait_ge(pads, 3)
                act.wait_ge(inner_proj, 1)
                nc.scalar.copy(raw_k[:, 1:T + 1], flat(ps_a)).then_inc(inner_raw, 1)
                act.wait_ge(inner_proj, 2)
                nc.scalar.copy(raw_v[:, 1:T + 1], flat(ps_b)).then_inc(inner_raw, 1)
                act.wait_ge(inner_mixed, 2)
                nc.scalar.activation(wa[0:HD, :], kx[0:HD, :], ACT.Tanh).then_inc(inner_done, 1)
                nc.scalar.copy(wa[HD:P, :], kx[HD:P, :]).then_inc(inner_done, 1)
                nc.scalar.activation(k.gate_in[:, :], vx[:, :], ACT.Sigmoid).then_inc(inner_done, 1)

                def turn_out(i):
                    for n in range(3):
                        act.wait_ge(turned, 3 * i - 3 + n + 1)
                        act.wait_ge(tok_free, i)
                        nc.scalar.copy(tok[:, n, :, :], ps_t[:, :, :]).then_inc(tok_ready, 1)

                def body(i, first):
                    if first:
                        act.wait_ge(inner_mixed, 1)
                    else:
                        act.wait_ge(k_mixed, i)
                    act.wait_ge(k_proj, i + 1)
                    nc.scalar.copy(raw_k[:, 1:T + 1], flat(ps_a)).then_inc(k_raw, 1)
                    if not first:
                        turn_out(i)
                    if first:
                        act.wait_ge(inner_mixed, 2)
                    else:
                        act.wait_ge(v_mixed, i)
                    act.wait_ge(v_proj, i + 1)
                    nc.scalar.copy(raw_v[:, 1:T + 1], flat(ps_b)).then_inc(v_raw, 1)
                    act.wait_ge(lora_w, i + 1)
                    if not first:
                        act.wait_ge(ch_ready, i)
                    nc.scalar.activation(sg[:, :], flat(ps_x), ACT.Sigmoid, bias=col(k, "w0", i)).then_inc(sg_ready, 1)
                    act.wait_ge(lora_a, i + 1)
                    nc.scalar.activation(rate[:, :], flat(ps_x), ACT.Sigmoid, bias=col(k, "a0", i)).then_inc(rate_ready, 1)
                    act.wait_ge(kk_ready, i + 1)
                    if not first:
                        act.wait_ge(norm_sum, i)
                    nc.scalar.activation(sq[:, :], kk[:, :], ACT.Square).then_inc(sq_ready, 1)
                    act.wait_ge(norm_floored, i + 1)
                    nc.scalar.activation(norm[:, :], norm[:, :], ACT.Sqrt).then_inc(norm_ready, 1)
                    if not first:
                        act.wait_ge(r_mixed, i)
                    act.wait_ge(r_proj, i + 1)
                    nc.scalar.copy(raw_r[:, 1:T + 1], flat(ps_a)).then_inc(r_raw, 1)
                    act.wait_ge(cc_ready, i + 1)
                    nc.scalar.activation(e_pos[:, :], cc[:, :], ACT.Exp, scale=-KAPPA).then_inc(exps_ready, 1)
                    act.wait_ge(exps_ready, 4 * i + 1)
                    nc.scalar.activation(e_neg[:, :], cc[:, :], ACT.Exp, scale=KAPPA).then_inc(exps_ready, 1)
                    nc.scalar.activation(e_ex[:, :], cx[:, :], ACT.Exp, scale=-KAPPA).then_inc(exps_ready, 1)
                    nc.scalar.activation(k.decays[:, bass.ds(i, 1), :].rearrange("p a c -> p (a c)"), span[:, :],
                                         ACT.Exp, scale=-KAPPA).then_inc(exps_ready, 1)

                rounds(act, body)
                turn_out(RT)

            @block.vector
            def _(dve):
                then = Chain(dve, dve_last)
                for raw in (raw_k, raw_v, raw_r):
                    nc.vector.memset(raw[:, 0:1], 0.0).then_inc(pads, 1)
                then(nc.vector.tensor_scalar(ka1[:, :], k.cols[:, COLS["k_a"]:COLS["k_a"] + RT], -1.0, 1.0, ALU.mult,
                                             ALU.add))
                dve.wait_ge(pads, 3)

                def mix(out, raw, mu_tile, sem, link):
                    link(nc.vector.tensor_tensor(diff[:, :], raw[:, 0:T], raw[:, 1:T + 1], ALU.subtract))
                    return nc.vector.scalar_tensor_tensor(out[:, :], diff[:, :], col(k, "mu", mu_tile), raw[:, 1:T + 1],
                                                          ALU.mult, ALU.add).then_inc(sem, 1)

                dve.wait_ge(inner_raw, 1)
                mix(kx, raw_k, T_WA, inner_mixed, then)
                dve.wait_ge(inner_raw, 2)
                dve.wait_ge(inner_mixed, 1)
                mix(vx, raw_v, T_G, inner_mixed, then)
                dve.wait_ge(inner_done, 3)
                start = then.n
                chunks = lambda t: t[:, :].rearrange("p (c t) -> p c t", t=P)

                def body(i, first):
                    link = Chain(dve, dve_last, 14)
                    link.base = i * 14 + start
                    if not first:
                        finish(i)
                    dve.wait_ge(k_raw, i + 1)
                    mix(kx, raw_k, i + T_K, k_mixed, link)
                    dve.wait_ge(k_mixed, i + 1)
                    nc.vector.tensor_scalar(kk[:, :], kx[:, :], col(k, "k_k", i), None, ALU.mult).then_inc(kk_ready, 1)
                    dve.wait_ge(sg_ready, i + 1)
                    link(nc.vector.tensor_tensor_scan(cum[:, :], mat(k, "reset", T), sg[:, :], 0.0, ALU.mult, ALU.add))
                    link(nc.vector.tensor_tensor(chunks(cc), chunks(cum),
                                                 chunks(cum)[:, :, P // 2 - 1:P // 2].to_broadcast([P, NT, P]),
                                                 ALU.subtract))
                    link(nc.vector.tensor_tensor(cx[:, :], cc[:, :], sg[:, :], ALU.subtract))
                    link(nc.vector.tensor_copy(span[:, :], chunks(cc)[:, :, P - 1]))
                    nc.vector.tensor_tensor(span[:, 0:NT - 1], span[:, 0:NT - 1], chunks(cum)[:, 1:NT, P // 2 - 1],
                                            ALU.add).then_inc(cc_ready, 1)
                    dve.wait_ge(norm_sum, i + 1)
                    nc.vector.tensor_scalar(norm[:, :], ps_x[:, :, :].rearrange("p a b -> p (a b)"), 1e-24, None,
                                            ALU.max).then_inc(norm_floored, 1)
                    dve.wait_ge(norm_ready, i + 1)
                    link(nc.vector.reciprocal(norm[:, :], norm[:, :]))
                    dve.wait_ge(kk_ready, i + 1)
                    link(nc.vector.tensor_tensor(kk[:, :], kk[:, :], norm[:, :], ALU.mult))
                    dve.wait_ge(rate_ready, i + 1)
                    link(nc.vector.tensor_scalar(k2[:, :], rate[:, :], col(k, "k_a", i), ka1[:, bass.ds(i, 1)], ALU.mult,
                                                 ALU.add))
                    link(nc.vector.tensor_tensor(k2[:, :], k2[:, :], kx[:, :], ALU.mult))
                    link(nc.vector.tensor_tensor(b[:, :], kk[:, :], rate[:, :], ALU.mult))
                    dve.wait_ge(r_raw, i + 1)
                    mix(rx, raw_r, i + T_R, r_mixed, link)
                    dve.wait_ge(r_mixed, i + 1)
                    if not first:
                        dve.wait_ge(bonus_sum, i)
                    nc.vector.scalar_tensor_tensor(rkk[:, :], rx[:, :], col(k, "r_k", i), k2[:, :], ALU.mult,
                                                   ALU.mult).then_inc(rkk_ready, 1)
                    dve.wait_ge(exps_ready, 4 * i + 4)
                    if not first:
                        dve.wait_ge(ch_out, 16 * i)
                        dve.wait_ge(turned, 3 * i)
                    link(nc.vector.scalar_tensor_tensor(ch[:, :, 0, :], chunks(kk), -1.0, chunks(e_ex), ALU.mult, ALU.mult))
                    nc.vector.tensor_tensor(ch[:, :, 1, :], chunks(rx), chunks(e_pos), ALU.mult)
                    nc.vector.tensor_tensor(ch[:, :, 2, :], chunks(b), chunks(e_neg), ALU.mult)
                    link(nc.vector.tensor_tensor(ch[:, :, 3, :], chunks(k2), chunks(e_neg), ALU.mult))
                    dve.sem_inc(ch_ready, 1)
                    dve.wait_ge(v_raw, i + 1)
                    mix(vx, raw_v, i + T_V, v_mixed, link)
                    link.done()

                def finish(i):
                    dve.wait_ge(bonus_sum, i)
                    dve.wait_ge(v_mixed, i)
                    nc.vector.tensor_tensor(k.bonus[:, bass.ds(i - 1, 1), :].rearrange("p a t -> p (a t)"),
                                            ps_x[:, :, :].rearrange("p a b -> p (a b)"), vx[:, :],
                                            ALU.mult).then_inc(bonus_ready, 1)

                rounds(dve, body)
                finish(RT)
                dve.wait_ge(bonus_ready, RT)


LEVELS = 6


def rwkv_chunks(nc, k):
    G = 2
    HG = RH // G
    with Space(nc, "rc") as s:
        ar = [s.sb(f"ar{b}", [P, RT, 2, 2 * P]) for b in range(2)]
        bk = [s.sb(f"bk{b}", [P, RT, 2, P]) for b in range(2)]
        tok = [s.sb(f"tok{b}", [P, 3, RT * P]) for b in range(2)]
        ab = [s.sb(f"ab{b}", [P, RH, 2 * P]) for b in range(2)]
        ak = [s.sb(f"ak{b}", [P, RH, 2 * P]) for b in range(2)]
        low = [s.sb(f"low{g}", [P, HG, P]) for g in range(G)]
        z = [s.sb(f"z{g}", [P, HG, P]) for g in range(G)]
        x = [s.sb(f"x{g}", [P, HG, P]) for g in range(G)]
        xt = [[s.sb(f"xt{b}{g}", [P, HG, P]) for g in range(G)] for b in range(2)]
        tmp = s.sb("tmp", [P, HG, P])
        p1, u = s.sb("p1", [P, RH, HD]), s.sb("u", [P, RH, HD])
        state = s.sb("state", [P, RT, HD])
        eye = s.sb("eye", [P, HG, P], BF16)
        ps_z, ps_x, ps_xt = ([s.ps(f"{n}{g}", [P, HALF]) for g in range(G)] for n in ("z", "x", "xt"))
        ps_p, ps_y = s.ps("p", [P, HALF]), s.ps("y", [P, HALF])
        loaded = [s.sem(f"loaded{b}") for b in range(2)]
        (prod_b, prod_k, prod_l, z_done, x_done, xt_done, b_masked, k_masked, l_masked, z_masked, x0_ready, x_copied,
         xt_copied) = ([s.sem(f"{n}{g}") for g in range(G)] for n in (
             "prod_b", "prod_k", "prod_l", "z_done", "x_done", "xt_done", "b_masked", "k_masked", "l_masked", "z_masked",
             "x0_ready", "x_copied", "xt_copied"))
        p_done, u_done, y_done, s_done, p_copied, u_copied, y_copied, s_scaled, ready, pool_last = (s.sem(n) for n in (
            "p_done", "u_done", "y_done", "s_done", "p_copied", "u_copied", "y_copied", "s_scaled", "ready", "pool_last"))
        zeroed = s.sem("zeroed")
        x_one = [s.sem(f"x_one{g}") for g in range(G)]
        XL, ZL = LEVELS - 1, LEVELS

        def heads(g):
            return range(g * HG, (g + 1) * HG)

        def four(ps):
            return ps[:, :].rearrange("p (h t) -> p h t", h=HG)

        def steps(eng, step):
            step((0, 0, True), None)
            step((1, 1, True), (0, 0, True))
            with eng.Fori(1, NT // 2) as i:
                for b in range(2):
                    step((2 * i + b, b, False), (2 * i + b - 1, 1 - b, False))
            step(None, (NT - 1, 1, False))

        with s.block() as block:
            @block.sync
            def _(sp):
                sp.wait_ge(zeroed, 2)

                def step(front, back):
                    if front is None:
                        return
                    c, b, early = front
                    if not early:
                        sp.wait_ge(s_done, c - 1)
                        sp.wait_ge(y_done, c - 1)
                    src = k.chunk_ch[bass.ds(c, 1)].rearrange("o p r a t -> (o p) r (a t)")
                    for n in range(2):
                        q = slice(n * HD, n * HD + HD)
                        sp.dma_start(ar[b][q, :, n, :], src[q, :, 0:2 * P]).then_inc(loaded[b], 16)
                    sp.dma_start(bk[b][:, :, :, :].rearrange("p r a t -> p r (a t)"), src[:, :, 2 * P:]
                                 ).then_inc(loaded[b], 16)
                    for n in range(3):
                        sp.dma_start(tok[b][:, n, :], k.chunk_tok[n, bass.ds(c, 1)].rearrange("o p r t -> (o p) (r t)")
                                     ).then_inc(loaded[b], 16)

                steps(sp, step)

            @block.tensor
            def _(pe):
                mm = nc.tensor.matmul
                pe.wait_ge(ready, 2)

                def products(front):
                    c, b, early = front
                    pe.wait_ge(loaded[b], (c - b) * 48 + 96)
                    for g in range(G):
                        if not isinstance(c, int) or c > 0:
                            pe.wait_ge(xt_copied[g], ZL * c)
                            pe.wait_ge(x_copied[g], XL * c)
                            pe.wait_ge(z_masked[g], ZL * c)
                        for j, h in enumerate(heads(g)):
                            t, o = h // 2, h % 2
                            last = mm(four(ps_xt[g])[:, j, :], ar[b][:, t, o, 0:P], bk[b][:, t, 0, :], start=True, stop=True)
                        last.then_inc(prod_l[g], 1)
                        for n, sem in ((0, prod_b), (1, prod_k)):
                            if n == 1:
                                pe.wait_ge(b_masked[g], c + 1)
                            for j, h in enumerate(heads(g)):
                                t, o = h // 2, h % 2
                                out = (ps_z, ps_x)[j // 2][g][:, (j % 2) * 2 * P:(j % 2 + 1) * 2 * P]
                                last = mm(out, bk[b][:, t, n, :], ar[b][:, t, o, :], start=True, stop=True)
                            last.then_inc(sem[g], 1)

                def level(front, n):
                    c, b, early = front
                    for g in range(G):
                        if n == 1:
                            pe.wait_ge(x0_ready[g], c + 1)
                            pe.wait_ge(k_masked[g], c + 1)
                        else:
                            pe.wait_ge(x_copied[g], XL * c + n - 1)
                        mm(ps_z[g][:, :], eye[:, 0, :], eye[:, :, :].rearrange("p h t -> p (h t)"), start=True, stop=False,
                           skip_group_check=True)
                        for j, h in enumerate(heads(g)):
                            last = mm(four(ps_z[g])[:, j, :], ab[b][:, h, 0:P], x[g][:, j, :], start=False,
                                      stop=(j == HG - 1), skip_group_check=True)
                        last.then_inc(z_done[g], 1)
                    for g in range(G):
                        pe.wait_ge(z_masked[g], ZL * c + n)
                        if n > 1:
                            pe.wait_ge(xt_copied[g], ZL * c + n - 1)
                        if n < LEVELS:
                            for j in range(HG):
                                last = mm(four(ps_x[g])[:, j, :], xt[b][g][:, j, :], z[g][:, j, :], start=True, stop=True)
                            last.then_inc(x_done[g], 1)
                        if n == 1:
                            pe.wait_ge(l_masked[g], c + 1)
                        for j in range(HG):
                            last = mm(four(ps_xt[g])[:, j, :], z[g][:, j, :], xt[b][g][:, j, :], start=True, stop=True)
                        last.then_inc(xt_done[g], 1)

                def through(back, n):
                    c, b, first = back
                    for h in range(RH) if n < 5 else ():
                        t, o = h // 2, h % 2
                        q, cols = slice(o * HD, o * HD + HD), slice(h * HD, h * HD + HD)
                        g, j = h // HG, h % HG
                        v, bt, kt = (tok[b][:, a, cols] for a in range(3))
                        if n == 1:
                            if h == 0 and not first:
                                pe.wait_ge(s_scaled, c)
                            mm(ps_p[:, cols], ar[b][:, t, o, 0:P], state[:, t, :], start=True, stop=False)
                            last = mm(ps_p[:, cols], ak[b][:, h, 0:P], v, start=False, stop=True)
                        elif n == 2:
                            if h == 0:
                                pe.wait_ge(p_copied, c + 1)
                                if not first:
                                    pe.wait_ge(y_copied, c)
                            if j == 0:
                                pe.wait_ge(xt_copied[g], ZL * c + ZL)
                            last = mm(ps_y[:, cols], xt[b][g][:, j, :], p1[:, h, :], start=True, stop=True)
                        elif n == 3:
                            if h == 0:
                                pe.wait_ge(u_copied, c + 1)
                            out = ps_y[q, t * P:(t + 1) * P]
                            mm(out, state[:, t, :], ar[b][:, t, o, P:2 * P], start=True, stop=False)
                            mm(out, u[:, h, :], ab[b][:, h, P:2 * P], start=False, stop=False)
                            last = mm(out, v, ak[b][:, h, P:2 * P], start=False, stop=True)
                        elif n == 4:
                            out = ps_p[q, t * HD:(t + 1) * HD]
                            mm(out, mat(k, "ident")[:, q], state[:, t, :], start=True, stop=False)
                            mm(out, bt, u[:, h, :], start=False, stop=False)
                            last = mm(out, kt, v, start=False, stop=True)
                    if n < 5:
                        last.then_inc((p_done, u_done, y_done, s_done)[n - 1], 1)

                def step(front, back):
                    if front is not None:
                        products(front)
                    for n in range(1, LEVELS + 1):
                        if front is not None:
                            level(front, n)
                        if back is not None:
                            through(back, n)

                steps(pe, step)

            @block.vector
            def _(dve):
                tt = nc.vector.tensor_tensor
                nc.vector.tensor_copy(eye[:, :, :], mat(k, "ident").unsqueeze(1).to_broadcast([P, HG, P])
                                      ).then_inc(ready, 1)
                nc.vector.memset(state[:, :, :], 0.0).then_inc(ready, 1)
                masks = mat(k, "before", 2 * P).unsqueeze(1).to_broadcast([P, 2, 2 * P])

                def level_mask(n):
                    return mat(k, "levels", P, n * P).unsqueeze(1).to_broadcast([P, HG, P])

                def step(front, back):
                    if front is not None:
                        c, b, early = front
                        if not early:
                            dve.wait_ge(s_done, c - 1)
                            dve.wait_ge(y_done, c - 1)
                        for g in range(G):
                            dve.wait_ge(prod_l[g], c + 1)
                            if not isinstance(c, int) or c > 0:
                                dve.wait_ge(x0_ready[g], c)
                            tt(low[g][:, :, :], four(ps_xt[g]), mat(k, "after").unsqueeze(1).to_broadcast([P, HG, P]),
                               ALU.mult).then_inc(l_masked[g], 1)
                            for sem, done, out in ((prod_b, b_masked, ab), (prod_k, k_masked, ak)):
                                dve.wait_ge(sem[g], c + 1)
                                for n, ps in enumerate((ps_z, ps_x)):
                                    h = g * HG + 2 * n
                                    last = tt(out[b][:, h:h + 2, :], ps[g][:, :].rearrange("p (h t) -> p h t", h=2), masks,
                                              ALU.mult)
                                last.then_inc(done[g], 1)
                    for n in range(1, LEVELS + 1):
                        if front is not None:
                            for g in range(G):
                                dve.wait_ge(z_done[g], ZL * c + n)
                                if n == 1 and (not isinstance(c, int) or c > 0):
                                    dve.wait_ge(xt_done[g], ZL * c)
                                if n > 1:
                                    dve.wait_ge(xt_done[g], ZL * c + n - 1)
                                tt(z[g][:, :, :], four(ps_z[g]), level_mask(n), ALU.mult).then_inc(z_masked[g], 1)
                        if back is not None and n == 4:
                            bc = back[0]
                            dve.wait_ge(s_done, bc + 1)
                            dve.wait_ge(y_done, bc + 1)
                            tt(state[:, :, :], ps_p[:, 0:RT * HD].rearrange("p (t d) -> p t d", d=HD),
                               k.decays[:, :, bass.ds(bc, 1)].to_broadcast([P, RT, HD]), ALU.mult).then_inc(s_scaled, 1)

                steps(dve, step)

            @block.gpsimd
            def _(pool):
                tt = nc.gpsimd.tensor_tensor
                for b in range(2):
                    nc.gpsimd.memset(ar[b][:, :, :, :], 0.0).then_inc(zeroed, 1)
                eye4 = mat(k, "ident").unsqueeze(1).to_broadcast([P, HG, P])

                def step(front, back):
                    if front is None:
                        return
                    c, b, early = front
                    if not early:
                        pool.wait_ge(u_done, c - 1)
                    link = Chain(pool, pool_last, 2 * G)
                    link.base = c * 2 * G
                    for g in range(G):
                        pool.wait_ge(l_masked[g], c + 1)
                        pool.wait_ge(b_masked[g], c + 1)
                        if not isinstance(c, int) or c > 0:
                            pool.wait_ge(z_done[g], ZL * c)
                            pool.wait_ge(x_copied[g], XL * c)
                        for src, name, out in ((low[g][:, :, :], "levels", x[g]),
                                               (ab[b][:, g * HG:(g + 1) * HG, 0:P], "level0_t", xt[b][g])):
                            link(tt(tmp[:, :, :], src, mat(k, name).unsqueeze(1).to_broadcast([P, HG, P]), ALU.mult))
                            last = tt(out[:, :, :], tmp[:, :, :], eye4, ALU.add)
                            if name == "levels":
                                last.then_inc(x_one[g], 1)
                                pool.wait_ge(x_one[g], c + 1)
                        last.then_inc(x0_ready[g], 1)
                        pool.wait_ge(x0_ready[g], c + 1)

                steps(pool, step)

            @block.scalar
            def _(act):
                def step(front, back):
                    for n in range(1, LEVELS + 1):
                        if front is not None:
                            c, b, early = front
                            for g in range(G):
                                if n < LEVELS:
                                    act.wait_ge(x_done[g], XL * c + n)
                                    nc.scalar.copy(x[g][:, :, :], four(ps_x[g])).then_inc(x_copied[g], 1)
                                act.wait_ge(xt_done[g], ZL * c + n)
                                nc.scalar.copy(xt[b][g][:, :, :], four(ps_xt[g])).then_inc(xt_copied[g], 1)
                        if back is not None:
                            bc = back[0]
                            if n == 1:
                                act.wait_ge(p_done, bc + 1)
                                nc.scalar.copy(p1[:, :, :].rearrange("p h d -> p (h d)"), ps_p[:, :]).then_inc(p_copied, 1)
                            elif n == 2:
                                act.wait_ge(u_done, bc + 1)
                                nc.scalar.copy(u[:, :, :].rearrange("p h d -> p (h d)"), ps_y[:, :]).then_inc(u_copied, 1)
                            elif n == 3:
                                act.wait_ge(y_done, bc + 1)
                                nc.scalar.copy(k.rwkv_oT[:, :, bass.ts(bc, P)],
                                               ps_y[:, :].rearrange("p (r t) -> p r t", r=RT)).then_inc(y_copied, 1)

                steps(act, step)


def rwkv_outputs(nc, k):
    with Space(nc, "ro") as s:
        g_up = s.sb("g_up", [P, P])
        yc, sq, sd, yn = (s.sb(n, [P, T]) for n in ("yc", "sq", "sd", "yn"))
        eps = s.sb("eps", [P, 1])
        ps_m, ps_v, ps_g = (s.ps(n, [P, 2, HALF]) for n in "mvg")
        up_loaded, summed, sq_ready, squares_summed, gate_done, eps_set, sd_ready, last = (s.sem(n) for n in (
            "up_loaded", "summed", "sq_ready", "squares_summed", "gate_done", "eps_set", "sd_ready", "last"))
        centered, gated = s.sem("centered"), s.sem("gated")

        def flat(ps):
            return ps[:, :, :].rearrange("p a b -> p (a b)")

        def tile_of(t, i):
            return t[:, bass.ds(i, 1), :].rearrange("p a t -> p (a t)")

        with s.block() as block:
            @block.sync
            def _(sp):
                with sp.Fori(0, RT) as i:
                    sp.wait_ge(gated, i + 1)
                    sp.dma_start(g_up[:, :], k.rwkv_g_up[:, bass.ts(i, P)]).then_inc(up_loaded, 16)

            @block.tensor
            def _(pe):
                with pe.Fori(0, RT) as i:
                    pe.wait_ge(gated, i + 1)
                    for h in range(2):
                        m = nc.tensor.matmul(ps_m[:, h, :], mat(k, "head_ones"),
                                             tile_of(k.rwkv_oT, i)[:, h * HALF:(h + 1) * HALF], start=True, stop=True)
                    m.then_inc(summed, 1)
                    pe.wait_ge(up_loaded, 16 * i + 16)
                    for h in range(2):
                        m = nc.tensor.matmul(ps_g[:, h, :], g_up[:, :], k.gate_in[:, h * HALF:(h + 1) * HALF],
                                             start=True, stop=True)
                    m.then_inc(gate_done, 1)
                    pe.wait_ge(sq_ready, i + 1)
                    for h in range(2):
                        m = nc.tensor.matmul(ps_v[:, h, :], mat(k, "head_ones"), sq[:, h * HALF:(h + 1) * HALF],
                                             start=True, stop=True)
                    m.then_inc(squares_summed, 1)

            @block.scalar
            def _(act):
                act.wait_ge(eps_set, 1)
                with act.Fori(0, RT) as i:
                    act.wait_ge(centered, i + 2)
                    nc.scalar.activation(sq[:, :], yc[:, :], ACT.Square).then_inc(sq_ready, 1)
                    act.wait_ge(squares_summed, i + 1)
                    nc.scalar.activation(sd[:, :], flat(ps_v), ACT.Sqrt, bias=eps[:, :], scale=1.0 / HD
                                         ).then_inc(sd_ready, 1)

            @block.vector
            def _(dve):
                nc.vector.memset(eps[:, :], RWKV_EPS).then_inc(eps_set, 1)
                dve.sem_inc(centered, 1)
                dve.sem_inc(gated, 1)
                with dve.Fori(0, RT) as i:
                    link = Chain(dve, last, 4)
                    link.base = i * 4
                    dve.wait_ge(summed, i + 1)
                    nc.vector.scalar_tensor_tensor(yc[:, :], flat(ps_m), -1.0 / HD, tile_of(k.rwkv_oT, i), ALU.mult,
                                                   ALU.add).then_inc(centered, 1)
                    dve.wait_ge(sd_ready, i + 1)
                    link(nc.vector.reciprocal(sd[:, :], sd[:, :]))
                    link(nc.vector.tensor_tensor(yn[:, :], yc[:, :], sd[:, :], ALU.mult))
                    link(nc.vector.tensor_scalar(yn[:, :], yn[:, :], col(k, "gn_g", i), col(k, "gn_b", i), ALU.mult,
                                                 ALU.add))
                    link(nc.vector.tensor_tensor(yn[:, :], yn[:, :], tile_of(k.bonus, i), ALU.add))
                    dve.wait_ge(gate_done, i + 1)
                    nc.vector.tensor_tensor(tile_of(k.rwkv_oT, i), yn[:, :], flat(ps_g), ALU.mult).then_inc(gated, 1)
                    dve.wait_ge(gated, i + 2)
                    link.done()


SMALL = 48


def fox_project(nc, k):
    with Space(nc, "fp") as s:
        w = [s.sb(f"w{b}", [P, KD, P]) for b in range(2)]
        w_v, w_small = s.sb("w_v", [P, KD, HALF]), s.sb("w_small", [P, KD, SMALL])
        qk = [s.sb(f"qk{b}", [P, T]) for b in range(2)]
        raw, ab, ln, one, c = (s.sb(n, [FH, T]) for n in ("raw", "ab", "ln", "one", "c"))
        neg_c = s.sb("neg_c", [FH, T])
        bias = s.sb("bias", [FH, 1])
        ps = [s.ps(f"t{b}", [P, 2, HALF]) for b in range(2)]
        ps_v = [s.ps(f"v{b}", [P, HALF]) for b in range(2)]
        ps_s = s.ps("s", [SMALL, 2, HALF])
        w_loaded = [s.sem(f"w_loaded{b}") for b in range(2)]
        stored = [s.sem(f"stored{b}") for b in range(2)]
        qk_free = [s.sem(f"qk_free{b}") for b in range(2)]
        (v_loaded, small_loaded, bias_in, projected, small_done, v_done, copied, v_copied, dt_copied, raw_done, abs_done,
         log_done, last, c_ready, c_stored) = (s.sem(n) for n in (
             "v_loaded", "small_loaded", "bias_in", "projected", "small_done", "v_done", "copied", "v_copied", "dt_copied",
             "raw_done", "abs_done", "log_done", "last", "c_ready", "c_stored"))
        pairs = FH * HD * 2 // P // 2

        with s.block() as block:
            @block.sync
            def _(sp):
                sp.dma_start(w_small[:, :, :], k.w_small).then_inc(small_loaded, 16)
                sp.dma_start(bias[:, :], k.f_bias).then_inc(bias_in, 16)
                with sp.Fori(0, pairs) as i:
                    for b in range(2):
                        sp.wait_ge(projected, 2 * i + b + 1)
                        sp.dma_start(w[b][:, :, :], k.w_tiles[bass.ds(2 * i + b + T_FQ, 1)].rearrange(
                            "a p k c -> (a p) k c")).then_inc(w_loaded[b], 16)
                sp.dma_start(w_v[:, :, :], k.w_fox_v).then_inc(v_loaded, 16)
                sp.wait_ge(c_ready, 2)
                sp.dma_start(k.fox_c[0], c[:, :]).then_inc(c_stored, 16)
                sp.dma_start(k.fox_c[1], neg_c[:, :]).then_inc(c_stored, 16)
                sp.wait_ge(c_stored, 32)

            @block.tensor
            def _(pe):
                pe.sem_inc(projected, 2)
                pe.wait_ge(small_loaded, 16)
                for half in range(2):
                    for d in range(KD):
                        m = nc.tensor.matmul(ps_s[:, half, :], w_small[:, d, :], k.xT[:, d, half * HALF:(half + 1) * HALF],
                                             start=(d == 0), stop=(d == KD - 1))
                m.then_inc(small_done, 1)
                with pe.Fori(0, pairs) as i:
                    for b in range(2):
                        pe.wait_ge(w_loaded[b], 16 * i + 16)
                        pe.wait_ge(copied, 2 * i + b + 1)
                        project(nc, ps[b], w[b], k.xT).then_inc(projected, 1)
                pe.wait_ge(v_loaded, 16)
                for n in range(NT):
                    if n >= 2:
                        pe.wait_ge(v_copied, n - 1)
                    for d in range(KD):
                        m = nc.tensor.matmul(ps_v[n % 2][:, :], k.xT[:, d, n * P:(n + 1) * P], w_v[:, d, :],
                                             start=(d == 0), stop=(d == KD - 1))
                    m.then_inc(v_done, 1)

            @block.scalar
            def _(act):
                act.sem_inc(copied, 2)
                act.wait_ge(raw_done, 1)
                nc.scalar.activation(ln[:, :], ab[:, :], ACT.Exp).then_inc(log_done, 1)
                act.wait_ge(log_done, 1)
                nc.scalar.activation(ln[:, :], ln[:, :], ACT.Ln, bias=1.0).then_inc(log_done, 1)
                for part, scale in ((0, HD ** -0.5), (1, 1.0)):
                    with act.Fori(part * pairs // 2, (part + 1) * pairs // 2) as i:
                        for b in range(2):
                            act.wait_ge(projected, 2 * i + b + 3)
                            act.wait_ge(qk_free[b], i + 1)
                            nc.scalar.activation(qk[b][:, :], ps[b][:, :, :].rearrange("p a b -> p (a b)"), ACT.Copy,
                                                 scale=scale).then_inc(copied, 1)
                for n in range(NT):
                    act.wait_ge(v_done, n + 1)
                    nc.scalar.copy(k.fox_v[:, n, :], ps_v[n % 2][:, :]).then_inc(v_copied, 1)

            @block.gpsimd
            def _(pool):
                dst = k.fox_qk.rearrange("(t two) d s -> t (two d) s", two=2)
                for b in range(2):
                    pool.sem_inc(qk_free[b], 1)
                with pool.Fori(0, pairs) as i:
                    for b in range(2):
                        pool.wait_ge(copied, 2 * i + b + 3)
                        pool.dma_start(dst[bass.ds(2 * i + b, 1)].rearrange("a p s -> (a p) s"), qk[b][:, :]
                                       ).then_inc(stored[b], 16)
                    for b in range(2):
                        pool.wait_ge(stored[b], 16 * i + 16)
                        pool.sem_inc(qk_free[b], 1)

            @block.vector
            def _(dve):
                link = Chain(dve, last)
                link(nc.vector.memset(one[:, :], 1.0))
                dve.wait_ge(bias_in, 16)
                dve.wait_ge(small_done, 1)
                nc.vector.tensor_copy(k.dt_raw[:, :], ps_s[32:32 + SH, :, :].rearrange("p a b -> p (a b)")
                                      ).then_inc(dt_copied, 1)
                link(nc.vector.tensor_scalar(raw[:, :], ps_s[0:FH, :, :].rearrange("p a b -> p (a b)"), bias[:, :], None,
                                             ALU.add))
                link(nc.vector.tensor_scalar(ab[:, :], raw[:, :], -1.0, None, ALU.mult))
                nc.vector.tensor_tensor(ab[:, :], ab[:, :], raw[:, :], ALU.min).then_inc(raw_done, 1)
                dve.wait_ge(log_done, 2)
                link(nc.vector.tensor_scalar(raw[:, :], raw[:, :], 0.0, None, ALU.min))
                link(nc.vector.tensor_tensor(raw[:, :], raw[:, :], ln[:, :], ALU.subtract))
                nc.vector.tensor_tensor_scan(c[:, :], one[:, :], raw[:, :], 0.0, ALU.mult, ALU.add).then_inc(c_ready, 1)
                dve.wait_ge(c_ready, 1)
                nc.vector.tensor_scalar(neg_c[:, :], c[:, :], -1.0, None, ALU.mult).then_inc(c_ready, 1)
                dve.wait_ge(dt_copied, 1)


def fox_attend(nc, k):
    with Space(nc, "fa") as s:
        qh = [s.sb(f"q{b}", [HD + 2, T]) for b in range(2)]
        kh = [s.sb(f"k{b}", [HD + 2, T]) for b in range(2)]
        eye, far = s.sb("eye", [P, P], BF16), s.sb("far", [P, P], BF16)
        p = [s.sb(f"p{b}", [P, T]) for b in range(2)]
        pt = [s.sb(f"pt{b}", [P, NT, P]) for b in range(2)]
        neg_max, total, inv = ([s.sb(f"{n}{b}", [P, 1]) for b in range(2)] for n in ("neg_max", "total", "inv"))
        o = s.sb("o", [P, NT, FH * HD])
        ps_s = [s.ps(f"s{b}", [P, T]) for b in range(2)]
        ps_t = s.ps("t", [P, NT, P])
        ps_o = [s.ps(f"o{b}", [P, HALF]) for b in range(2)]
        loaded = [s.sem(f"loaded{b}") for b in range(2)]
        (consts, scored, max_ready, exp_ready, turned_a, turned_b, a_copied, b_copied, pv_done, inv_ready, o_ready,
         o_turned, o_copied) = (s.sem(n) for n in (
             "consts", "scored", "max_ready", "exp_ready", "turned_a", "turned_b", "a_copied", "b_copied", "pv_done",
             "inv_ready", "o_ready", "o_turned", "o_copied"))

        def units(eng, head):
            with eng.Fori(0, FH // 2) as r:
                for b in range(2):
                    head(2 * r + b, b)

        with s.block() as block:
            @block.sync
            def _(sp):
                sp.wait_ge(consts, 6)
                def load(h, b):
                    sp.dma_start(qh[b][0:HD, :], k.fox_qk[bass.ds(h, 1)].rearrange("o d s -> (o d) s")).then_inc(loaded[b], 16)
                    sp.dma_start(kh[b][0:HD, :], k.fox_qk[bass.ds(h + FH, 1)].rearrange("o d s -> (o d) s")
                                 ).then_inc(loaded[b], 16)
                    sp.dma_start(qh[b][HD:HD + 1, :], k.fox_c[0, bass.ds(h, 1)]).then_inc(loaded[b], 16)
                    sp.dma_start(kh[b][HD + 1:HD + 2, :], k.fox_c[1, bass.ds(h, 1)]).then_inc(loaded[b], 16)

                load(0, 0)
                load(1, 1)
                with sp.Fori(1, FH // 2) as r:
                    for b in range(2):
                        sp.wait_ge(scored, NT * (2 * r + b - 1))
                        load(2 * r + b, b)

            @block.tensor
            def _(pe):
                mm = nc.tensor.matmul
                pe.wait_ge(consts, 6)

                def score(h, b, i):
                    u, q = NT * h + i, i * P
                    if i == 0:
                        pe.wait_ge(loaded[b], (h - b) * 32 + 64)
                    pe.wait_ge(exp_ready, u + 1)
                    n = (i + 1) * P
                    for lo in range(0, n, HALF):
                        hi = min(lo + HALF, n)
                        mm(ps_s[i % 2][:, lo:hi], qh[b][:, q:q + P], kh[b][:, lo:hi], start=True, stop=(hi < n),
                           skip_group_check=True)
                    mm(ps_s[i % 2][:, q:q + P], eye[:, :], far[:, :], start=False, stop=True,
                       skip_group_check=True).then_inc(scored, 1)

                def turn(h, b, i):
                    u = NT * h + i
                    pe.wait_ge(exp_ready, u + 3)
                    pe.wait_ge(a_copied, u + 1)
                    for j in range(min(i + 1, 4)):
                        m = nc.tensor.transpose(ps_t[:, j, :], p[i % 2][:, j * P:(j + 1) * P], mat(k, "ident"))
                    m.then_inc(turned_a, 1)
                    if i >= 4:
                        pe.wait_ge(b_copied, 4 * h + i - 4 + 1)
                        for j in range(4, i + 1):
                            m = nc.tensor.transpose(ps_t[:, j, :], p[i % 2][:, j * P:(j + 1) * P], mat(k, "ident"))
                        m.then_inc(turned_b, 1)

                def times_v(h, b, i):
                    u = NT * h + i
                    pe.wait_ge(o_ready, u + 1)
                    pe.wait_ge(a_copied, u + 2)
                    if i >= 4:
                        pe.wait_ge(b_copied, 4 * h + i - 4 + 2)
                    for j in range(i + 1):
                        m = mm(ps_o[i % 2][:, 0:HD], pt[i % 2][:, j, :], k.fox_v[:, j, bass.ts(h, HD)],
                               start=(j == 0), stop=(j == i))
                    m.then_inc(pv_done, 1)

                def head(h, b):
                    score(h, b, 0)
                    for i in range(NT):
                        if i + 1 < NT:
                            score(h, b, i + 1)
                        if i >= 1:
                            times_v(h, b, i - 1)
                        turn(h, b, i)
                    times_v(h, b, NT - 1)

                units(pe, head)
                for i in range(NT):
                    if i == 0:
                        pe.wait_ge(o_ready, NT * FH + 2)
                        pe.wait_ge(a_copied, NT * FH + 1)
                        pe.wait_ge(b_copied, 4 * FH + 1)
                    if i >= 2:
                        pe.wait_ge(o_copied, i - 1)
                    for t in range(4):
                        m = nc.tensor.transpose(ps_t[:, (i % 2) * 4 + t, :], o[:, i, t * P:(t + 1) * P], mat(k, "ident"))
                    m.then_inc(o_turned, 1)

            @block.scalar
            def _(act):
                act.sem_inc(exp_ready, 2)
                act.sem_inc(b_copied, 1)

                def head(h, b):
                    for i in range(NT + 1):
                        if i < NT:
                            u, n = NT * h + i, (i + 1) * P
                            act.wait_ge(max_ready, u + 1)
                            if i >= 2:
                                act.wait_ge(turned_a, u - 1)
                                act.wait_ge(inv_ready, u - 1)
                            if i >= 6:
                                act.wait_ge(turned_b, 4 * h + i - 5)
                            nc.scalar.activation(p[i % 2][:, 0:n], ps_s[i % 2][:, 0:n], ACT.Exp, bias=neg_max[i % 2][:, :],
                                                 accum_out=total[i % 2][:, :]).then_inc(exp_ready, 1)
                        j = i - 1
                        if j >= 4:
                            act.wait_ge(turned_b, 4 * h + j - 4 + 1)
                            nc.scalar.copy(pt[j % 2][:, 4:j + 1, :], ps_t[:, 4:j + 1, :]).then_inc(b_copied, 1)

                units(act, head)

            @block.vector
            def _(dve):
                for b in range(2):
                    nc.vector.memset(qh[b][HD:HD + 2, :], 1.0).then_inc(consts, 1)
                    nc.vector.memset(kh[b][HD:HD + 2, :], 1.0).then_inc(consts, 1)
                nc.vector.tensor_copy(eye[:, :], mat(k, "ident")).then_inc(consts, 1)
                nc.vector.tensor_scalar(far[:, :], mat(k, "before"), NEG, None, ALU.mult).then_inc(consts, 1)
                dve.sem_inc(a_copied, 1)
                dve.sem_inc(o_ready, 2)

                def head(h, b):
                    for i in range(NT + 2):
                        if i < NT:
                            u, n = NT * h + i, (i + 1) * P
                            dve.wait_ge(scored, u + 1)
                            if i >= 2:
                                dve.wait_ge(exp_ready, u + 1)
                            nc.vector.tensor_reduce(neg_max[i % 2][:, :], ps_s[i % 2][:, 0:n], AX.X, ALU.max,
                                                    negate=True).then_inc(max_ready, 1)
                        j = i - 2
                        if 0 <= j < NT:
                            v = NT * h + j
                            dve.wait_ge(exp_ready, v + 3)
                            nc.vector.reciprocal(inv[j % 2][:, :], total[j % 2][:, :]).then_inc(inv_ready, 1)
                        j = i - 1
                        if 0 <= j < NT:
                            v = NT * h + j
                            dve.wait_ge(turned_a, v + 1)
                            if j >= 2:
                                dve.wait_ge(pv_done, v - 1)
                            m = min(j + 1, 4)
                            nc.vector.tensor_copy(pt[j % 2][:, 0:m, :], ps_t[:, 0:m, :]).then_inc(a_copied, 1)
                        j = i - 2
                        if 0 <= j < NT:
                            v = NT * h + j
                            dve.wait_ge(inv_ready, v + 1)
                            dve.wait_ge(pv_done, v + 1)
                            nc.vector.tensor_scalar(o[:, j, bass.ts(h, HD)], ps_o[j % 2][:, 0:HD], inv[j % 2][:, :], None,
                                                    ALU.mult).then_inc(o_ready, 1)

                units(dve, head)
                for i in range(NT):
                    dve.wait_ge(o_turned, i + 1)
                    nc.vector.tensor_copy(k.fox_oT[:, :, i * P:(i + 1) * P], ps_t[:, (i % 2) * 4:(i % 2) * 4 + 4, :]
                                          ).then_inc(o_copied, 1)
                dve.wait_ge(o_copied, NT)


def ssm_inputs(nc, k):
    with Space(nc, "si") as s:
        w = [s.sb(f"w{b}", [P, KD, P]) for b in range(2)]
        raw = [s.sb(f"raw{b}", [P, T + 8]) for b in range(2)]
        acc = [s.sb(f"acc{b}", [P, T]) for b in range(2)]
        out = [s.sb(f"out{b}", [P, T]) for b in range(2)]
        ps = [s.ps(f"t{b}", [P, 2, HALF]) for b in range(2)]
        ps_t = s.ps("turn", [P, NT, P])
        w_loaded = [s.sem(f"w_loaded{b}") for b in range(2)]
        projected, copied, convolved, silu_done, kept, turned, turn_copied = (s.sem(n) for n in (
            "projected", "copied", "convolved", "silu_done", "kept", "turned", "turn_copied"))
        pads, last = s.sem("pads"), s.sem("last")
        n_turned = NCONV - SG

        def tiles(eng, body):
            with eng.Fori(0, n_turned // 2) as i:
                for b in range(2):
                    body(2 * i + b, b, True)
            for t in range(n_turned, NCONV):
                body(t, t % 2, False)

        with s.block() as block:
            @block.sync
            def _(sp):
                def body(t, b, turn):
                    sp.wait_ge(projected, t + 1)
                    sp.dma_start(w[b][:, :, :], k.w_tiles[bass.ds(t + T_XBC, 1)].rearrange("a p k c -> (a p) k c")
                                 ).then_inc(w_loaded[b], 16)

                tiles(sp, body)

            @block.tensor
            def _(pe):
                pe.sem_inc(projected, 2)

                def turn_tile(t, b):
                    pe.wait_ge(silu_done, t + 3)
                    pe.wait_ge(turn_copied, t + 1)
                    for c in range(NT):
                        m = nc.tensor.transpose(ps_t[:, c, :], out[b][:, c * P:(c + 1) * P], mat(k, "ident"))
                    m.then_inc(turned, 1)

                def body(t, b, turn, first=False):
                    pe.wait_ge(w_loaded[b], (t - b) * 8 + 16)
                    pe.wait_ge(copied, t + 1)
                    project(nc, ps[b], w[b], k.xT).then_inc(projected, 1)
                    if not first:
                        turn_tile(t - 1, 1 - b)

                body(0, 0, True, True)
                body(1, 1, True)
                with pe.Fori(1, n_turned // 2) as i:
                    for b in range(2):
                        body(2 * i + b, b, True)
                body(n_turned, 0, True)
                pe.wait_ge(w_loaded[1], (NCONV // 2) * 16)
                pe.wait_ge(copied, NCONV)
                project(nc, ps[1], w[1], k.xT).then_inc(projected, 1)

            @block.scalar
            def _(act):
                act.sem_inc(copied, 2)
                act.sem_inc(silu_done, 2)
                act.sem_inc(turn_copied, 1)
                act.wait_ge(pads, 2)

                def copy_in(t, b):
                    act.wait_ge(projected, t + 3)
                    act.wait_ge(convolved, t + 1)
                    nc.scalar.copy(raw[b][:, 8:8 + T], ps[b][:, :, :].rearrange("p a b -> p (a b)")).then_inc(copied, 1)

                def body(t, b, turn):
                    copy_in(t, b)
                    act.wait_ge(convolved, t + 3)
                    act.wait_ge(kept, t + 1)
                    if turn:
                        act.wait_ge(turned, t + 1)
                    nc.scalar.activation(out[b][:, :], acc[b][:, :], ACT.Silu).then_inc(silu_done, 1)
                    if turn:
                        act.wait_ge(turned, t + 3)
                        nc.scalar.copy(k.ssm_tok[:, :, bass.ts(t, P)], ps_t[:, :, :]).then_inc(turn_copied, 1)

                act.sem_inc(turned, 2)
                tiles(act, body)

            @block.gpsimd
            def _(pool):
                pool.sem_inc(kept, 2)

                def body(t, b, turn):
                    pool.wait_ge(silu_done, t + 3)
                    nc.gpsimd.tensor_copy(k.ssm[:, bass.ds(t, 1), :].rearrange("p a t -> p (a t)"), out[b][:, :]
                                          ).then_inc(kept, 1)

                tiles(pool, body)
                pool.wait_ge(kept, NCONV + 2)

            @block.vector
            def _(dve):
                dve.sem_inc(convolved, 2)
                for b in range(2):
                    nc.vector.memset(raw[b][:, 0:8], 0.0).then_inc(pads, 1)
                dve.wait_ge(pads, 2)

                def tap(t, n):
                    return k.cols[:, bass.ds(t + (COLS["conv_w"] + n * NCONV), 1)]

                def body(t, b, turn):
                    link = Chain(dve, last)
                    link.base = t * 3
                    dve.wait_ge(copied, t + 3)
                    dve.wait_ge(silu_done, t + 1)
                    a = acc[b][:, :]
                    link(nc.vector.tensor_scalar(a, raw[b][:, 8:8 + T], tap(t, 3), col(k, "conv_b", t), ALU.mult, ALU.add))
                    for n in (2, 1):
                        link(nc.vector.scalar_tensor_tensor(a, raw[b][:, 5 + n:5 + n + T], tap(t, n), a, ALU.mult, ALU.add))
                    nc.vector.scalar_tensor_tensor(a, raw[b][:, 5:5 + T], tap(t, 0), a, ALU.mult, ALU.add
                                                   ).then_inc(convolved, 1)

                tiles(dve, body)


def ssm_scan(nc, k):
    with Space(nc, "sc") as s:
        row = [s.sb(f"row{b}", [SH, P]) for b in range(2)]
        soft, cums = s.sb("soft", [SH, T]), s.sb("cums", [SH, T])
        x0, dt = k.dt_raw, soft
        bias, a_exp = s.sb("bias", [SH, 1]), s.sb("a_exp", [SH, 1])
        dt_tok, cums_tok = s.sb("dt_tok", [P, NT, SH]), s.sb("cums_tok", [P, NT, SH])
        cb = k.ssm[:, ST:ST + SG, :].rearrange("p g (c t) -> p g c t", t=P)
        lm = [s.sb(f"lm{b}", [P, NT, P]) for b in range(2)]
        ec = [s.sb(f"ec{b}", [P, NT, P]) for b in range(2)]
        end = [s.sb(f"end{b}", [P, NT]) for b in range(2)]
        xs = [s.sb(f"xs{b}", [P, NT, HD]) for b in range(2)]
        xd = [s.sb(f"xd{b}", [P, NT, HD]) for b in range(2)]
        st = [s.sb(f"st{b}", [P, NT, HD]) for b in range(2)]
        ps_s = [s.ps(f"s{b}", [P, 2, HALF]) for b in range(2)]
        ps_y = s.ps("y", [P, NT, P])
        ps_d = [s.ps(f"d{b}", [P, NT, HD]) for b in range(2)]
        row_in = [s.sem(f"row_in{b}") for b in range(2)]
        (consts_in, floored, exps_done, log_done, dt_ready, tok_done, tok_copied, cb_done, cb_masked, zeroed, spread,
         arg_ready, e_ready, l_ready, x_ready, m_ready, c_ready, d_done, st_ready, y_done, y_kept, link_a, link_c,
         link_s) = (s.sem(n) for n in (
             "consts_in", "floored", "exps_done", "log_done", "dt_ready", "tok_done", "tok_copied", "cb_done", "cb_masked",
             "zeroed", "spread", "arg_ready", "e_ready", "l_ready", "x_ready", "m_ready", "c_ready", "d_done", "st_ready",
             "y_done", "y_kept", "link_a", "link_c", "link_s"))
        pairs = SH // 2

        def heads(eng, head):
            head(0, 0, 0)
            head(0, 1, 0)
            for lo, hi, g in ((1, pairs // 2, 0), (pairs // 2, pairs, 1)):
                with eng.Fori(lo, hi) as i:
                    for b in range(2):
                        head(i, b, g)

        def chunks(t):
            return t.rearrange("p a (c t) -> p (a c) t", t=P)

        with s.block() as block:
            @block.sync
            def _(sp):
                sp.dma_start(bias[:, :], k.dt_bias).then_inc(consts_in, 16)
                sp.dma_start(a_exp[:, :], k.a_log).then_inc(consts_in, 16)

                def head(i, b, g):
                    sp.wait_ge(spread, 2 * i + b + 1)
                    sp.dma_start(row[b][:, :], k.head_rows_d[:, bass.ds(2 * i + b, 1), :].rearrange("h a p -> h (a p)")
                                 ).then_inc(row_in[b], 16)

                heads(sp, head)

            @block.tensor
            def _(pe):
                mm = nc.tensor.matmul
                for sem in (spread, d_done, y_done):
                    pe.sem_inc(sem, 2)
                for g in range(SG):
                    for c in range(NT):
                        q = slice(c * P, (c + 1) * P)
                        m = mm(chunks(ps_s[g][:, :, :])[:, c, :], k.ssm[:, ST + g, q], k.ssm[:, ST + SG + g, q],
                               start=True, stop=True)
                    m.then_inc(cb_done, 1)
                pe.wait_ge(dt_ready, 2)
                for n, t in ((0, dt), (1, cums)):
                    for c in range(NT):
                        m = nc.tensor.transpose(ps_y[:, c, n * SH:(n + 1) * SH], t[:, c * P:(c + 1) * P],
                                                mat(k, "ident")[0:SH, 0:SH])
                m.then_inc(tok_done, 1)
                pe.wait_ge(cb_masked, SG)
                pe.wait_ge(tok_copied, 2)

                def outputs(i, b):
                    h = 2 * i + b
                    pe.wait_ge(m_ready, h + 1)
                    pe.wait_ge(c_ready, h + 1)
                    pe.wait_ge(st_ready, h + 3)
                    if b == 0:
                        pe.wait_ge(y_kept, i + 1)
                    for c in range(NT):
                        y = ps_y[b * HD:(b + 1) * HD, c, :]
                        mm(y, xs[b][:, c, :], lm[b][:, c, :], start=True, stop=False)
                        m = mm(y, st[b][:, c, :], ec[b][:, c, :], start=False, stop=True)
                    m.then_inc(y_done, 1)

                def head(i, b, g):
                    h = 2 * i + b
                    pe.wait_ge(row_in[b], 16 * i + 16)
                    pe.wait_ge(e_ready, h + 1)
                    pe.wait_ge(arg_ready, h + 1)
                    for half in range(2):
                        m = mm(ps_s[b][:, half, :], row[b][:, :], cums[:, half * HALF:(half + 1) * HALF], start=True,
                               stop=True)
                    m.then_inc(spread, 1)
                    if b == 1:
                        outputs(i, 0)
                    elif not isinstance(i, int):
                        outputs(i - 1, 1)
                    pe.wait_ge(x_ready, h + 1)
                    pe.wait_ge(st_ready, h + 1)
                    for c in range(NT):
                        m = mm(ps_d[b][:, c, :], k.ssm_tok[:, c, SH * HD + g * SN:SH * HD + (g + 1) * SN], xd[b][:, c, :],
                               start=True, stop=True)
                    m.then_inc(d_done, 1)

                heads(pe, head)
                outputs(pairs - 1, 1)

            @block.scalar
            def _(act):
                act.sem_inc(e_ready, 2)
                act.wait_ge(consts_in, 32)
                nc.scalar.activation(a_exp[:, :], a_exp[:, :], ACT.Exp).then_inc(exps_done, 1)
                act.wait_ge(floored, 1)
                nc.scalar.activation(soft[:, :], soft[:, :], ACT.Exp).then_inc(exps_done, 1)
                act.wait_ge(exps_done, 2)
                nc.scalar.activation(soft[:, :], soft[:, :], ACT.Ln, bias=1.0).then_inc(log_done, 1)

                def head(i, b, g):
                    h = 2 * i + b
                    act.wait_ge(spread, h + 3)
                    act.wait_ge(y_done, h + 1)
                    nc.scalar.activation(ec[b][:, :, :], chunks(ps_s[b][:, :, :]), ACT.Exp).then_inc(e_ready, 1)
                    act.wait_ge(arg_ready, h + 3)
                    nc.scalar.activation(lm[b][:, :, :], lm[b][:, :, :], ACT.Exp).then_inc(l_ready, 1)

                heads(act, head)

            @block.gpsimd
            def _(pool):
                tt = nc.gpsimd.tensor_tensor

                def head(i, b, g):
                    pool.wait_ge(x_ready, 2 * i + b + 1)
                    tt(lm[b][:, :, :], lm[b][:, :, :], cb[:, g], ALU.mult).then_inc(m_ready, 1)
                    tt(ec[b][:, :, :], ec[b][:, :, :], k.ssm[:, ST + SG + g, :].rearrange("p (c t) -> p c t", t=P),
                       ALU.mult).then_inc(c_ready, 1)

                heads(pool, head)

            @block.vector
            def _(dve):
                v = nc.vector
                dve.sem_inc(arg_ready, 2)
                dve.sem_inc(st_ready, 2)
                dve.sem_inc(y_kept, 1)
                link = Chain(dve, link_s)
                for b in range(2):
                    v.memset(st[b][:, 0, :], 0.0).then_inc(zeroed, 1)
                dve.wait_ge(consts_in, 32)
                link(v.tensor_scalar(x0[:, :], k.dt_raw[:, :], bias[:, :], None, ALU.add))
                link(v.tensor_scalar(soft[:, :], x0[:, :], -1.0, None, ALU.mult))
                v.tensor_tensor(soft[:, :], soft[:, :], x0[:, :], ALU.min).then_inc(floored, 1)
                for g in range(SG):
                    dve.wait_ge(cb_done, g + 1)
                    v.tensor_tensor(cb[:, g], chunks(ps_s[g][:, :, :]),
                                    mat(k, "before_or_at").unsqueeze(1).to_broadcast([P, NT, P]), ALU.mult
                                    ).then_inc(cb_masked, 1)
                dve.wait_ge(log_done, 1)
                v.scalar_tensor_tensor(dt[:, :], x0[:, :], 0.0, soft[:, :], ALU.max, ALU.add).then_inc(dt_ready, 1)
                dve.wait_ge(dt_ready, 1)
                dve.wait_ge(exps_done, 1)
                link(v.tensor_scalar(x0[:, :], dt[:, :], a_exp[:, :], -1.0, ALU.mult, ALU.mult))
                v.tensor_tensor_scan(cums[:, :], mat(k, "reset", T)[0:SH, :], x0[:, :], 0.0, ALU.mult, ALU.add
                                     ).then_inc(dt_ready, 1)
                dve.wait_ge(tok_done, 1)
                for n, t in ((0, dt_tok), (1, cums_tok)):
                    v.tensor_copy(t[:, :, :], ps_y[:, :, n * SH:(n + 1) * SH]).then_inc(tok_copied, 1)
                dve.wait_ge(tok_copied, 2)
                dve.wait_ge(zeroed, 2)

                def states(i, b):
                    h = 2 * i + b
                    link = Chain(dve, link_c)
                    link.base = h * (NT - 2)
                    dve.wait_ge(d_done, h + 3)
                    for c in range(NT - 1):
                        m = v.scalar_tensor_tensor(st[b][:, c + 1, :], st[b][:, c, :], end[b][:, c:c + 1], ps_d[b][:, c, :],
                                                   ALU.mult, ALU.add)
                        if c < NT - 2:
                            link(m)
                    m.then_inc(st_ready, 1)

                def keep(i):
                    dve.wait_ge(y_done, 2 * i + 4)
                    x = k.ssm[:, bass.ds(i, 1), :].rearrange("p a t -> p (a t)")
                    v.scalar_tensor_tensor(x, x, col(k, "ssm_d", i), ps_y[:, :, :].rearrange("p a t -> p (a t)"), ALU.mult,
                                           ALU.add).then_inc(y_kept, 1)

                def head(i, b, g):
                    h = 2 * i + b
                    link = Chain(dve, link_a)
                    link.base = h * 3
                    if b == 1 and not isinstance(i, int):
                        keep(i - 1)
                    dve.wait_ge(spread, h + 3)
                    dve.wait_ge(y_done, h + 1)
                    dve.wait_ge(e_ready, h + 3)
                    of_head = lambda t: t[:, :, bass.ds(h, 1)].to_broadcast([P, NT, P])
                    link(v.tensor_tensor(lm[b][:, :, :], chunks(ps_s[b][:, :, :]), of_head(cums_tok), ALU.subtract))
                    v.tensor_scalar(lm[b][:, :, :], lm[b][:, :, :], 0.0, None, ALU.min).then_inc(arg_ready, 1)
                    link(v.tensor_tensor(xs[b][:, :, :], k.ssm_tok[:, :, bass.ts(h, HD)],
                                         dt_tok[:, :, bass.ds(h, 1)].to_broadcast([P, NT, HD]), ALU.mult))
                    if b == 1:
                        states(i, 0)
                    elif not isinstance(i, int):
                        states(i - 1, 1)
                    link(v.tensor_copy(end[b][:, :], ec[b][:, :, P - 1]))
                    dve.wait_ge(l_ready, h + 1)
                    dve.wait_ge(d_done, h + 1)
                    v.tensor_tensor(xd[b][:, :, :], xs[b][:, :, :], lm[b][:, :, P - 1:P].to_broadcast([P, NT, HD]),
                                    ALU.mult).then_inc(x_ready, 1)

                heads(dve, head)
                states(pairs - 1, 1)
                keep(pairs - 1)
                dve.wait_ge(y_kept, pairs + 1)


def ssm_outputs(nc, k):
    with Space(nc, "so") as s:
        w = [s.sb(f"w{b}", [P, KD, P]) for b in range(2)]
        zs = [s.sb(f"z{b}", [P, T]) for b in range(2)]
        sq = [s.sb(f"sq{b}", [P, T]) for b in range(2)]
        inv = s.sb("inv", [P, T])
        eps = s.sb("eps", [P, 1])
        ps = [s.ps(f"t{b}", [P, 2, HALF]) for b in range(2)]
        ps_q = s.ps("q", [P, 2, HALF])
        w_loaded = [s.sem(f"w_loaded{b}") for b in range(2)]
        projected, silu_done, gated, squared, summed, root_done, inv_done, normed, eps_set = (s.sem(n) for n in (
            "projected", "silu_done", "gated", "squared", "summed", "root_done", "inv_done", "normed", "eps_set"))
        per = ST // SG

        def flat(p):
            return p[:, :, :].rearrange("p a b -> p (a b)")

        def y(t):
            return k.ssm[:, bass.ds(t, 1), :].rearrange("p a t -> p (a t)")

        with s.block() as block:
            @block.sync
            def _(sp):
                with sp.Fori(0, ST // 2) as i:
                    for b in range(2):
                        sp.wait_ge(projected, 2 * i + b + 1)
                        sp.dma_start(w[b][:, :, :], k.w_tiles[bass.ds(2 * i + b + T_Z, 1)].rearrange(
                            "a p k c -> (a p) k c")).then_inc(w_loaded[b], 16)

            @block.tensor
            def _(pe):
                pe.sem_inc(projected, 2)
                pe.sem_inc(summed, 2)

                def sums(t, b, j):
                    pe.wait_ge(squared, t + 1)
                    for half in range(2):
                        m = nc.tensor.matmul(ps_q[:, half, :], mat(k, "ones"), sq[b][:, half * HALF:(half + 1) * HALF],
                                             start=(j == 0), stop=(j == per - 1), skip_group_check=True)
                    m.then_inc(summed, 1)

                with pe.Fori(0, SG) as g:
                    for j in range(per):
                        t, b = per * g + j, j % 2
                        pe.wait_ge(w_loaded[b], 32 * g + 16 * (j // 2) + 16)
                        pe.wait_ge(silu_done, t + 1)
                        project(nc, ps[b], w[b], k.xT).then_inc(projected, 1)
                        if j > 0:
                            if j == 1:
                                pe.wait_ge(root_done, g + 1)
                            sums(t - 1, 1 - b, j - 1)
                    sums(per * g + per - 1, 1, per - 1)

            @block.scalar
            def _(act):
                act.sem_inc(silu_done, 2)
                act.sem_inc(root_done, 1)
                act.wait_ge(eps_set, 1)

                def square(t, b):
                    act.wait_ge(gated, t + 3)
                    act.wait_ge(summed, t + 1)
                    nc.scalar.activation(sq[b][:, :], y(t), ACT.Square).then_inc(squared, 1)

                with act.Fori(0, SG) as g:
                    for j in range(per):
                        t, b = per * g + j, j % 2
                        act.wait_ge(projected, t + 3)
                        act.wait_ge(gated, t + 1)
                        nc.scalar.activation(zs[b][:, :], flat(ps[b]), ACT.Silu).then_inc(silu_done, 1)
                        square(t, b)
                    act.wait_ge(summed, per * g + per + 2)
                    act.wait_ge(normed, per * g + 1)
                    nc.scalar.activation(inv[:, :], flat(ps_q), ACT.Sqrt, bias=eps[:, :], scale=1.0 / (per * P)
                                         ).then_inc(root_done, 1)

            @block.vector
            def _(dve):
                dve.sem_inc(gated, 2)
                dve.sem_inc(normed, 1)
                nc.vector.memset(eps[:, :], NORM_EPS).then_inc(eps_set, 1)
                with dve.Fori(0, SG) as g:
                    for j in range(per):
                        t, b = per * g + j, j % 2
                        dve.wait_ge(silu_done, t + 3)
                        nc.vector.tensor_tensor(y(t), y(t), zs[b][:, :], ALU.mult).then_inc(gated, 1)
                    dve.wait_ge(root_done, g + 2)
                    nc.vector.reciprocal(inv[:, :], inv[:, :]).then_inc(inv_done, 1)
                    dve.wait_ge(inv_done, g + 1)
                    dve.wait_ge(squared, per * g + per)
                    for j in range(per):
                        t = per * g + j
                        nc.vector.scalar_tensor_tensor(y(t), y(t), col(k, "norm_g", t), inv[:, :], ALU.mult, ALU.mult
                                                       ).then_inc(normed, 1)
                dve.wait_ge(normed, ST + 1)


def merge(nc, k):
    with Space(nc, "mg") as s:
        w_g = [s.sb(f"w_g{n}", [P, KD, P]) for n in range(3)]
        sizes = (RT, RT, ST)
        w_b = [s.sb(f"w_b{n}", [P, sizes[n], P]) for n in range(3)]
        sources = (k.rwkv_oT, k.fox_oT, k.ssm)
        gate = [s.sb(f"gate{n}", [P, T]) for n in range(3)]
        term = [k.spare[:, 0, :], k.spare[:, 1, :], s.sb("term2", [P, T])]
        ps_g = [s.ps(f"g{b}", [P, 2, HALF]) for b in range(2)]
        ps_b = [s.ps(f"b{b}", [P, 2, HALF]) for b in range(2)]
        g_in, b_in = [s.sem(f"g_in{n}") for n in range(3)], [s.sem(f"b_in{n}") for n in range(3)]
        g_done, b_done, g_ready, term_ready, summed = (s.sem(n) for n in ("g_done", "b_done", "g_ready", "term_ready",
                                                                         "summed"))

        gate_free, two_summed = s.sem("gate_free"), s.sem("two_summed")

        def flat(p):
            return p[:, :, :].rearrange("p a b -> p (a b)")

        with s.block() as block:
            @block.sync
            def _(sp):
                with sp.Fori(0, KD) as i:
                    for n in range(3):
                        sp.wait_ge(g_done, 3 * i + n + 1)
                        sp.dma_start(w_g[n][:, :, :], k.w_tiles[bass.ds(i + (T_GATE + n * KD), 1)].rearrange(
                            "a p k c -> (a p) k c")).then_inc(g_in[n], 16)
                        at = sum(sizes[:n])
                        sp.wait_ge(b_done, 3 * i + n + 1)
                        sp.dma_start(w_b[n][:, :, :], k.w_br[bass.ds(i, 1), :, at:at + sizes[n], :].rearrange(
                            "a p k c -> (a p) k c")).then_inc(b_in[n], 16)

            @block.tensor
            def _(pe):
                pe.sem_inc(g_done, 3)
                pe.sem_inc(b_done, 3)
                with pe.Fori(0, KD // 2) as r:
                    for j in range(2):
                        for n in range(3):
                            i, b = 2 * r + j, (3 * j + n) % 2
                            m = 3 * i + n
                            pe.wait_ge(g_in[n], 16 * i + 16)
                            pe.wait_ge(g_ready, m + 1)
                            project(nc, ps_g[b], w_g[n], k.xT).then_inc(g_done, 1)
                            pe.wait_ge(b_in[n], 16 * i + 16)
                            pe.wait_ge(term_ready, m + 1)
                            for half in range(2):
                                for c in range(sizes[n]):
                                    last = nc.tensor.matmul(ps_b[b][:, half, :], w_b[n][:, c, :],
                                                            sources[n][:, c, half * HALF:(half + 1) * HALF],
                                                            start=(c == 0), stop=(c == sizes[n] - 1))
                            last.then_inc(b_done, 1)

            @block.scalar
            def _(act):
                act.sem_inc(g_ready, 2)
                with act.Fori(0, KD // 2) as r:
                    for j in range(2):
                        for n in range(3):
                            i, b = 2 * r + j, (3 * j + n) % 2
                            m = 3 * i + n
                            act.wait_ge(g_done, m + 4)
                            act.wait_ge(gate_free, m + 1)
                            nc.scalar.activation(gate[n][:, :], flat(ps_g[b]), ACT.Sigmoid,
                                                 bias=col(k, "gate_bias", i + n * KD)).then_inc(g_ready, 1)

            @block.vector
            def _(dve):
                dve.sem_inc(term_ready, 2)
                dve.sem_inc(gate_free, 3)
                with dve.Fori(0, KD // 2) as r:
                    for j in range(2):
                        for n in range(3):
                            i, b = 2 * r + j, (3 * j + n) % 2
                            m = 3 * i + n
                            dve.wait_ge(g_ready, m + 3)
                            dve.wait_ge(b_done, m + 4)
                            if n == 0:
                                dve.wait_ge(summed, i + 1)
                            nc.vector.tensor_tensor(term[n][:, :], gate[n][:, :], flat(ps_b[b]), ALU.mult
                                                    ).then_inc(term_ready, 1)
                            dve.wait_ge(term_ready, m + 3)
                            dve.sem_inc(gate_free, 1)

            @block.gpsimd
            def _(pool):
                pool.sem_inc(summed, 1)
                with pool.Fori(0, KD) as i:
                    pool.wait_ge(term_ready, 3 * i + 4)
                    nc.gpsimd.tensor_tensor(term[0][:, :], term[0][:, :], term[1][:, :], ALU.add).then_inc(two_summed, 1)
                    pool.wait_ge(two_summed, i + 1)
                    pool.wait_ge(term_ready, 3 * i + 5)
                    nc.gpsimd.tensor_tensor(k.merged[:, bass.ds(i, 1), :].rearrange("p a t -> p (a t)"), term[0][:, :],
                                            term[2][:, :], ALU.add).then_inc(summed, 1)
                pool.wait_ge(summed, KD + 1)


def layer_norm(nc, dve, link, r, out, ln, mv, stats, sd, halves, stood, aggregated, wait_root):
    v = nc.vector
    link(v.bn_stats(stats[:, 0, :], r[:, 0:HALF]))
    v.bn_stats(stats[:, 1, :], r[:, HALF:D]).then_inc(halves, 1)
    wait_apart(dve, halves, aggregated[2], stood)
    v.bn_aggr(mv[:, :], stats[:, :, :]).then_inc(*aggregated[:2])
    dve.wait_ge(aggregated[0], aggregated[2])
    link(v.scalar_tensor_tensor(r[:, :], r[:, :], mv[:, 0:1], ln[:, 0, :], ALU.subtract, ALU.mult))
    wait_root()
    link(v.reciprocal(sd[:, :], sd[:, :]))
    return v.scalar_tensor_tensor(out, r[:, :], sd[:, :], ln[:, 1, :], ALU.mult, ALU.add)


def out_project(nc, k):
    with Space(nc, "op") as s:
        w = s.sb("w", [P, KD, D])
        lhs = [s.sb(f"lhs{b}", [P, KD, P]) for b in range(2)]
        r = [s.sb(f"r{b}", [P, D]) for b in range(2)]
        x1 = [s.sb(f"x1{b}", [P, D]) for b in range(2)]
        ln = s.sb("ln", [P, 2, D])
        w_r, b_r = s.sb("w_r", [P, KD, E]), s.sb("b_r", [P, E])
        xt = [s.sb(f"xt{b}", [P, KD, P]) for b in range(2)]
        zeros = s.sb("zeros", [P, D])
        stats, mv, sd, eps = s.sb("stats", [P, 2, 6]), s.sb("mv", [P, 2]), s.sb("sd", [P, 1]), s.sb("eps", [P, 1])
        ps = [s.ps(f"t{b}", [P, 2, HALF]) for b in range(2)]
        ps_t = s.ps("turn", [P, KD, P])
        ps_l = [s.ps(f"l{b}", [P, HALF]) for b in range(2)]
        x_in = [s.sem(f"x_in{b}") for b in range(2)]
        stored = [s.sem(f"stored{b}") for b in range(2)]
        zeroed, slots_zeroed = s.sem("zeroed"), s.sem("slots_zeroed")
        (w_in, ln_in, router_in, lhs_ready, projected, mixed, aggregated, root_done, x1_ready, turned, turn_copied,
         logits_done, logits_copied, aff_ready, sel_ready, eps_set, last, halves, stood) = (s.sem(n) for n in (
             "w_in", "ln_in", "router_in", "lhs_ready", "projected", "mixed", "aggregated", "root_done", "x1_ready", "turned",
             "turn_copied", "logits_done", "logits_copied", "aff_ready", "sel_ready", "eps_set", "last",
             "halves", "stood"))
        x_rows = k.x.rearrange("a (n p) d -> (a n) p d", p=P)
        x1_rows = k.x1_d.rearrange("(n p) d -> n p d", p=P)

        def tiles(eng, body):
            with eng.Fori(0, NT // 2) as i:
                for b in range(2):
                    body(2 * i + b, b)

        with s.block() as block:
            @block.sync
            def _(sp):
                for b in range(2):
                    sp.sem_inc(stored[b], 16)
                for h in range(2):
                    sp.dma_start(w[:, h * 4:h * 4 + 4, :], k.w_out[:, h * 4:h * 4 + 4, :]).then_inc(w_in, 16)
                for n in range(2):
                    sp.dma_start(ln[:, n, :], k.ln1[n:n + 1, :].partition_broadcast(P)).then_inc(ln_in, 16)
                sp.dma_start(w_r[:, :, :], k.router_w).then_inc(router_in, 16)
                sp.dma_start(b_r[:, :], k.router_b.partition_broadcast(P)).then_inc(router_in, 16)

                def load(t, b):
                    sp.dma_start(r[b][:, :], x_rows[bass.ds(t, 1)].rearrange("a p d -> (a p) d")).then_inc(x_in[b], 16)

                def store(t, b):
                    sp.wait_ge(x1_ready, t + 3)
                    sp.dma_start(x1_rows[bass.ds(t, 1)].rearrange("a p d -> (a p) d"), x1[b][:, :]).then_inc(stored[b], 16)

                load(0, 0)
                load(1, 1)
                with sp.Fori(0, NT // 2 - 1) as i:
                    for b in range(2):
                        store(2 * i + b, b)
                        load(2 * i + b + 2, b)
                for b in range(2):
                    store(NT - 2 + b, b)
                for b in range(2):
                    sp.wait_ge(stored[b], 16 + 8 * NT)

            @block.gpsimd
            def _(pool):
                nc.gpsimd.memset(zeros[:, :], 0.0).then_inc(zeroed, 1)
                pool.wait_ge(zeroed, 1)
                pool.dma_start(k.buf_tok.rearrange("(b p) o -> b (p o)", p=P), zeros[0:N_BLOCKS, 0:P]).then_inc(slots_zeroed, 16)
                with pool.Fori(E, N_BLOCKS) as n:
                    pool.dma_start(k.y_slots.rearrange("(b p) d -> b p d", p=P)[bass.ds(n, 1)].rearrange("a p d -> (a p) d"),
                                   zeros[:, :]).then_inc(slots_zeroed, 16)

                def copy(t, b):
                    pool.wait_ge(projected, t + 1)
                    nc.gpsimd.tensor_copy(lhs[b][:, :, :], k.merged[:, :, bass.ts(t, P)]).then_inc(lhs_ready, 1)

                tiles(pool, copy)
                pool.wait_ge(slots_zeroed, 16 * (1 + OVER))

            @block.tensor
            def _(pe):
                mm = nc.tensor.matmul
                pe.sem_inc(projected, 2)

                def mix(t, b):
                    pe.wait_ge(lhs_ready, t + 1)
                    pe.wait_ge(mixed, t + 1)
                    for h in range(2):
                        for d in range(KD):
                            m = mm(ps[b][:, h, :], lhs[b][:, d, :], w[:, d, h * HALF:(h + 1) * HALF], start=(d == 0),
                                   stop=(d == KD - 1))
                    m.then_inc(projected, 1)

                def turn(t, b):
                    pe.wait_ge(x1_ready, t + 3)
                    pe.wait_ge(turn_copied, t + 2)
                    for c in range(KD):
                        m = nc.tensor.transpose(ps_t[:, c, :], x1[b][:, c * P:(c + 1) * P], mat(k, "ident"))
                    m.then_inc(turned, 1)

                def logits(t, b):
                    pe.wait_ge(turn_copied, t + 3)
                    pe.wait_ge(logits_copied, t + 1)
                    for c in range(KD):
                        m = mm(ps_l[b][:, 0:E], xt[b][:, c, :], w_r[:, c, :], start=(c == 0), stop=(c == KD - 1))
                    m.then_inc(logits_done, 1)

                pe.wait_ge(w_in, 32)
                mix(0, 0)
                mix(1, 1)
                turn(0, 0)
                pe.wait_ge(router_in, 32)
                with pe.Fori(1, NT // 2) as i:
                    for b in range(2):
                        mix(2 * i + b, b)
                        turn(2 * i + b - 1, 1 - b)
                        logits(2 * i + b - 2, b)
                turn(NT - 1, 1)
                logits(NT - 2, 0)
                logits(NT - 1, 1)

            @block.scalar
            def _(act):
                act.sem_inc(turn_copied, 2)
                act.sem_inc(logits_copied, 2)
                act.sem_inc(logits_done, 2)
                act.wait_ge(eps_set, 1)

                def root(t):
                    act.wait_ge(aggregated, t + 1)
                    nc.scalar.activation(sd[:, :], mv[:, 1:2], ACT.Sqrt, bias=eps[:, :]).then_inc(root_done, 1)

                def out_of_psum(t, b):
                    act.wait_ge(turned, t + 3)
                    act.wait_ge(logits_done, t + 1)
                    nc.scalar.copy(xt[b][:, :, :], ps_t[:, :, :]).then_inc(turn_copied, 1)

                def keep_logits(t, b):
                    act.wait_ge(logits_done, t + 3)
                    nc.scalar.copy(k.aff[:, bass.ds(t, 1), :].rearrange("p a e -> p (a e)"), ps_l[b][:, 0:E]
                                   ).then_inc(logits_copied, 1)

                root(0)
                root(1)
                out_of_psum(0, 0)
                with act.Fori(1, NT // 2) as i:
                    for b in range(2):
                        root(2 * i + b)
                        out_of_psum(2 * i + b - 1, 1 - b)
                        keep_logits(2 * i + b - 2, b)
                out_of_psum(NT - 1, 1)
                keep_logits(NT - 2, 0)
                keep_logits(NT - 1, 1)
                act.wait_ge(logits_copied, NT + 2)
                nc.scalar.activation(k.aff[:, :, :], k.aff[:, :, :], ACT.Sigmoid).then_inc(aff_ready, 1)
                act.wait_ge(aff_ready, 1)

            @block.vector
            def _(dve):
                v = nc.vector
                v.memset(eps[:, :], LN_EPS).then_inc(eps_set, 1)
                dve.sem_inc(mixed, 2)
                dve.sem_inc(x1_ready, 2)
                dve.sem_inc(turned, 2)
                dve.wait_ge(ln_in, 32)

                def norm(t, b):
                    link = Chain(dve, last)
                    link.base = t * 3
                    dve.wait_ge(x_in[b], (t - b) * 8 + 16)
                    dve.wait_ge(projected, t + 3)
                    v.scalar_tensor_tensor(r[b][:, :], r[b][:, :], ALPHA, ps[b][:, :, :].rearrange("p a b -> p (a b)"),
                                           ALU.mult, ALU.add).then_inc(mixed, 1)
                    dve.wait_ge(mixed, t + 3)
                    dve.wait_ge(stored[b], (t - b) * 8 + 16)
                    dve.wait_ge(turned, t + 1)
                    layer_norm(nc, dve, link, r[b], x1[b][:, :], ln, mv, stats, sd, halves, stood, (aggregated, 1, t + 1),
                               lambda: dve.wait_ge(root_done, t + 1)).then_inc(x1_ready, 1)

                tiles(dve, norm)
                dve.wait_ge(router_in, 32)
                dve.wait_ge(aff_ready, 1)
                v.tensor_tensor(k.sel[:, :, :], k.aff[:, :, :], b_r[:, :].unsqueeze(1).to_broadcast([P, NT, E]), ALU.add
                                ).then_inc(sel_ready, 1)
                dve.wait_ge(sel_ready, 1)


def route(nc, k):
    with Space(nc, "rt") as s:
        def grid(name):
            return s.sb(name, [P, NT, E])

        eq, idx_of, cand, oh1, oh2, both, pos = (grid(n) for n in ("eq", "idx_of", "cand", "oh1", "oh2", "both", "pos"))
        best, first, score = (s.sb(n, [P, NT * EG]) for n in ("best", "first", "score"))
        g1, g2 = s.sb("g1", [P, NT]), s.sb("g2", [P, NT])
        before = s.sb("before", [P, NT + 1, E])
        over = s.sb("over", [P, E])
        over_end, over_slot, one_e = s.sb("over_end", [P, E]), s.sb("over_slot", [P, E]), s.sb("one_e", [P, E])
        ended = s.sb("ended", [P, 16, E])
        block_expert, rows = s.sb("block_expert", [P, 16]), s.sb("rows", [P, 16])
        token = s.sb("token", [P, NT])
        dest = s.sb("dest", [P, NT, 2])
        slots = s.sb("slots", [N_BLOCKS, P])
        ps_rank, ps_count, ps_slots = s.ps("rank", [P, NT, E]), s.ps("count", [P, HALF]), s.ps("slots", [P, HALF])
        (last, picked, ranked, dest_ready, scattered, slots_in, slots_turned, done) = (s.sem(n) for n in (
            "last", "picked", "ranked", "dest_ready", "scattered", "slots_in", "slots_turned", "done"))

        with s.block() as block:
            @block.vector
            def _(dve):
                v, link = nc.vector, Chain(dve, last)
                tt, ts = v.tensor_tensor, v.tensor_scalar

                def spread(t, shape):
                    return t.unsqueeze(2).to_broadcast(shape)

                def first_of_max(values, index, n, width, one_hot, value, take_out=None):
                    shape = [P, n, width]
                    link(v.tensor_reduce(value, values, AX.X, ALU.max))
                    link(tt(one_hot, values, spread(value, shape), ALU.is_lt))
                    link(v.scalar_tensor_tensor(one_hot, one_hot, float(P), index, ALU.mult, ALU.add))
                    link(v.tensor_reduce(first[:, 0:n], one_hot, AX.X, ALU.min))
                    link(tt(one_hot, index, spread(first[:, 0:n], shape), ALU.is_equal))
                    if take_out is not None:
                        link(v.scalar_tensor_tensor(take_out, one_hot, NEG, values, ALU.mult, ALU.add))

                def by_group(t):
                    return t[:, :, :].rearrange("p n (g e) -> p (n g) e", e=EPG)

                experts = mat(k, "experts", E).unsqueeze(1).to_broadcast([P, NT, E])
                link(v.tensor_copy(idx_of[:, :, :], experts))
                first_of_max(by_group(k.sel), by_group(idx_of), NT * EG, EPG, by_group(oh1), best[:, :], by_group(cand))
                link(v.tensor_reduce(score[:, :], by_group(cand), AX.X, ALU.max))
                link(tt(score[:, :], score[:, :], best[:, :], ALU.add))
                scores = score[:, :].rearrange("p (n g) -> p n g", g=EG)
                eq_g = eq[:, :, 0:EG]
                first_of_max(scores, idx_of[:, :, 0:EG], NT, EG, eq_g, g1[:, :])
                link(v.tensor_copy(score[:, :].rearrange("p (n g) -> p n g", g=EG), eq_g))
                in_group = score[:, :].unsqueeze(2).to_broadcast([P, NT * EG, EPG])
                link(v.tensor_copy(by_group(eq), in_group))
                link(tt(cand[:, :, :], k.sel[:, :, :], eq[:, :, :], ALU.mult))
                link(ts(eq[:, :, :], eq[:, :, :], 1.0, -NEG, ALU.subtract, ALU.mult))
                link(tt(cand[:, :, :], cand[:, :, :], eq[:, :, :], ALU.add))
                first_of_max(cand[:, :, :], idx_of[:, :, :], NT, E, oh1[:, :, :], g1[:, :], cand[:, :, :])
                first_of_max(cand[:, :, :], idx_of[:, :, :], NT, E, oh2[:, :, :], g2[:, :])
                tt(both[:, :, :], oh1[:, :, :], oh2[:, :, :], ALU.add).then_inc(picked, 1)
                dve.wait_ge(picked, 1)
                link(v.memset(before[:, 0, :], 0.0))
                for n in range(NT):
                    m = tt(before[:, n + 1, :], before[:, n, :], both[:, n, :], ALU.add)
                    if n < NT - 1:
                        link(m)
                m.then_inc(picked, 1)
                for g, oh in ((g1, oh1), (g2, oh2)):
                    link(tt(eq[:, :, :], k.aff[:, :, :], oh[:, :, :], ALU.mult))
                    link(v.tensor_reduce(g[:, :], eq[:, :, :], AX.X, ALU.add))
                link(tt(k.gates[:, :, 0], g1[:, :], g2[:, :], ALU.add))
                link(v.reciprocal(k.gates[:, :, 1], k.gates[:, :, 0]))
                link(tt(k.gates[:, :, 0], g1[:, :], k.gates[:, :, 1], ALU.mult))
                link(tt(k.gates[:, :, 1], g2[:, :], k.gates[:, :, 1], ALU.mult))
                dve.wait_ge(ranked, 2)
                link(ts(over[:, :], ps_count[:, 0:E], float(P), None, ALU.is_gt))
                for j in range(2, T // P):
                    link(v.scalar_tensor_tensor(over[:, :], ps_count[:, 0:E], float(j * P), over[:, :], ALU.is_gt, ALU.add))
                link(v.memset(one_e[:, :], 1.0))
                link(v.tensor_tensor_scan(over_end[:, :], one_e[:, :], over[:, :], 0.0, ALU.mult, ALU.add))
                link(tt(ended[:, :, :], over_end[:, :].unsqueeze(1).to_broadcast([P, 16, E]),
                        mat(k, "over_ids", 16).unsqueeze(2).to_broadcast([P, 16, E]), ALU.is_le))
                link(v.tensor_reduce(block_expert[:, :], ended[:, :, :], AX.X, ALU.add))
                link(ts(k.unused[:, :], block_expert[:, :], float(E), None, ALU.is_ge))
                link(ts(rows[:, :], block_expert[:, :], float(E - 1), float(P), ALU.min, ALU.mult))
                link(tt(k.over_rows[:, :], rows[:, :], mat(k, "row0", 16), ALU.add))
                link(tt(over_slot[:, :], over_end[:, :], over[:, :], ALU.subtract))
                link(ts(over_slot[:, :], over_slot[:, :], float(P), float((E - 1) * P), ALU.mult, ALU.add))
                link(tt(over_slot[:, :], over_slot[:, :], mat(k, "slot0", E), ALU.subtract))
                link(ts(pos[:, :, :], ps_rank[:, :, :], float(P), None, ALU.is_ge))
                link(tt(pos[:, :, :], pos[:, :, :], over_slot[:, :].unsqueeze(1).to_broadcast([P, NT, E]), ALU.mult))
                link(tt(pos[:, :, :], pos[:, :, :], ps_rank[:, :, :], ALU.add))
                link(tt(pos[:, :, :], pos[:, :, :], mat(k, "slot0", E).unsqueeze(1).to_broadcast([P, NT, E]), ALU.add))
                for n, oh in ((0, oh1), (1, oh2)):
                    link(tt(eq[:, :, :], pos[:, :, :], oh[:, :, :], ALU.mult))
                    link(v.tensor_reduce(dest[:, :, n], eq[:, :, :], AX.X, ALU.add))
                link(ts(token[:, :], mat(k, "slot0", NT), mat(k, "row0", 1), None, ALU.add))
                v.tensor_copy(k.dest[:, :, :], dest[:, :, :]).then_inc(dest_ready, 1)
                dve.wait_ge(dest_ready, 1)
                dve.wait_ge(slots_turned, 1)
                v.tensor_copy(k.slot_token[:, :], ps_slots[:, 0:N_BLOCKS]).then_inc(done, 1)
                dve.wait_ge(done, 1)

            @block.tensor
            def _(pe):
                mm = nc.tensor.matmul
                pe.wait_ge(picked, 2)
                mm(ps_rank[:, :, :], mat(k, "before"), both[:, :, :], start=True, stop=False)
                mm(ps_rank[:, :, :], mat(k, "ones"), before[:, 0:NT, :], start=False, stop=True).then_inc(ranked, 1)
                mm(ps_count[:, 0:E], mat(k, "ones"), before[:, NT, :], start=True, stop=True).then_inc(ranked, 1)
                pe.wait_ge(slots_in, 16)
                nc.tensor.transpose(ps_slots[:, 0:N_BLOCKS], slots[:, :], mat(k, "ident")[0:N_BLOCKS, 0:N_BLOCKS]
                                    ).then_inc(slots_turned, 1)

            @block.gpsimd
            def _(pool):
                pool.wait_ge(dest_ready, 1)
                for n in range(NT):
                    for j in range(2):
                        pool.indirect_dma_start(k.buf_tok, bass.IndirectOffsetOnAxis(ap=k.dest[:, n, j:j + 1], axis=0),
                                                token[:, n:n + 1], None).then_inc(scattered, 16)

            @block.sync
            def _(sp):
                sp.wait_ge(scattered, 16 * 2 * NT)
                sp.dma_start(slots[:, :], k.buf_tok.rearrange("(b p) o -> b (p o)", p=P)).then_inc(slots_in, 16)
                sp.wait_ge(slots_in, 16)


def experts(nc, k):
    with Space(nc, "ex") as s:
        w_g, w_u = ([s.sb(f"{n}{b}", [P, KD, DE]) for b in range(2)] for n in ("w_g", "w_u"))
        w_d = [s.sb(f"w_d{b}", [P, FF, D]) for b in range(2)]
        xb = [s.sb(f"xb{b}", [P, D]) for b in range(2)]
        idx = [s.sb(f"idx{b}", [P, 1], U32) for b in range(2)]
        xt, gate, h, ht = s.sb("xt", [P, KD, P]), s.sb("gate", [P, DE]), s.sb("h", [P, DE]), s.sb("ht", [P, FF, P])
        y = [s.sb(f"y{b}", [P, D]) for b in range(2)]
        ps_x, ps_y = s.ps("x", [P, KD, P]), s.ps("y", [P, 2, HALF])
        ps_g, ps_u, ps_h = s.ps("g", [P, DE]), s.ps("u", [P, DE]), s.ps("h", [P, FF, P])
        g_in, u_in, d_in, x_in = ([s.sem(f"{n}{b}") for b in range(2)] for n in ("g_in", "u_in", "d_in", "x_in"))
        y_out = [s.sem(f"y_out{b}") for b in range(2)]
        (idx_ready, g_done, u_done, d_done, x_turned, x_copied, silu_done, h_ready, h_turned, h_copied, y_kept, idx_stood) = (
            s.sem(n) for n in ("idx_ready", "g_done", "u_done", "d_done", "x_turned", "x_copied", "silu_done", "h_ready",
                               "h_turned", "h_copied", "y_kept", "idx_stood"))
        parts = [w.rearrange("e (p k) f -> e p k f", p=P) for w in (k.exp_gate, k.exp_up, k.exp_down)]
        y_blocks = k.y_slots.rearrange("(b p) d -> b p d", p=P)

        def pairs(eng, body, lo=0, hi=E // 2, first=0):
            with eng.Fori(lo, hi) as i:
                for n in range(2):
                    body(2 * i + n + first, (n + first) % 2)

        with s.block() as block:
            @block.sync
            def _(sp):
                def load(e, b):
                    for w, part, used, sem in ((w_g, 0, g_done, g_in), (w_u, 1, u_done, u_in), (w_d, 2, d_done, d_in)):
                        sp.wait_ge(used, e + 1)
                        sp.dma_start(w[b][:, :, :], parts[part][bass.ds(e, 1)].rearrange("a p k f -> (a p) k f")
                                     ).then_inc(sem[b], 16)

                pairs(sp, load)

            @block.gpsimd
            def _(pool):
                def gather(e, b):
                    pool.wait_ge(x_turned, e + 1)
                    nc.gpsimd.tensor_copy(idx[b][:, :], k.slot_token[:, bass.ds(e, 1)]).then_inc(idx_ready, 1)
                    wait_apart(pool, idx_ready, e + 1, idx_stood)
                    pool.indirect_dma_start(xb[b][:, :], None, k.x1_d, bass.IndirectOffsetOnAxis(ap=idx[b][:, :], axis=0)
                                            ).then_inc(x_in[b], 16)

                pairs(pool, gather)

            @block.tensor
            def _(pe):
                mm = nc.tensor.matmul
                for sem in (g_done, u_done, d_done, x_turned):
                    pe.sem_inc(sem, 2)

                def turn_x(e, b):
                    pe.wait_ge(x_in[b], (e - b) * 8 + 16)
                    pe.wait_ge(x_copied, e + 1)
                    for c in range(KD):
                        m = nc.tensor.transpose(ps_x[:, c, :], xb[b][:, c::KD], mat(k, "ident"))
                    m.then_inc(x_turned, 1)

                def gate_up(e, b):
                    pe.wait_ge(x_copied, e + 2)
                    for w, ps, loaded, read, done in ((w_g, ps_g, g_in, silu_done, g_done), (w_u, ps_u, u_in, h_ready, u_done)):
                        pe.wait_ge(loaded[b], (e - b) * 8 + 16)
                        pe.wait_ge(read, e + 1)
                        for c in range(KD):
                            m = mm(ps[:, :], xt[:, c, :], w[b][:, c, :], start=(c == 0), stop=(c == KD - 1))
                        m.then_inc(done, 1)

                def turn_h(e, b):
                    pe.wait_ge(h_ready, e + 2)
                    pe.wait_ge(h_copied, e + 1)
                    for c in range(FF):
                        m = nc.tensor.transpose(ps_h[:, c, :], h[:, c::FF], mat(k, "ident"))
                    m.then_inc(h_turned, 1)

                def down(e, b):
                    pe.wait_ge(d_in[b], (e - b) * 8 + 16)
                    pe.wait_ge(h_copied, e + 2)
                    pe.wait_ge(y_kept, e + 1)
                    for half in range(2):
                        for c in range(FF):
                            m = mm(ps_y[:, half, :], ht[:, c, :], w_d[b][:, c, half * HALF:(half + 1) * HALF],
                                   start=(c == 0), stop=(c == FF - 1))
                    m.then_inc(d_done, 1)

                turn_x(0, 0)
                gate_up(0, 0)
                turn_x(1, 1)
                turn_h(0, 0)

                def body(e, b):
                    gate_up(e, b)
                    turn_x(e + 1, 1 - b)
                    down(e - 1, 1 - b)
                    turn_h(e, b)

                pairs(pe, body, 0, E // 2 - 1, 1)
                gate_up(E - 1, 1)
                down(E - 2, 0)
                turn_h(E - 1, 1)
                down(E - 1, 1)

            @block.scalar
            def _(act):
                act.sem_inc(silu_done, 1)
                act.sem_inc(x_copied, 1)
                for b in range(2):
                    act.sem_inc(y_out[b], 16)

                def copy_x(e):
                    act.wait_ge(x_turned, e + 3)
                    act.wait_ge(u_done, e + 2)
                    nc.scalar.copy(xt[:, :, :], ps_x[:, :, :]).then_inc(x_copied, 1)

                def silu(e):
                    act.wait_ge(g_done, e + 3)
                    act.wait_ge(h_ready, e + 1)
                    nc.scalar.activation(gate[:, :], ps_g[:, :], ACT.Silu).then_inc(silu_done, 1)

                def store(e, b):
                    act.wait_ge(y_kept, e + 2)
                    act.dma_start(y_blocks[bass.ds(e, 1)].rearrange("a p d -> (a p) d"), y[b][:, :]).then_inc(y_out[b], 16)

                copy_x(0)
                silu(0)
                copy_x(1)

                def body(e, b):
                    silu(e)
                    copy_x(e + 1)
                    store(e - 1, 1 - b)

                pairs(act, body, 0, E // 2 - 1, 1)
                silu(E - 1)
                store(E - 2, 0)
                store(E - 1, 1)
                for b in range(2):
                    act.wait_ge(y_out[b], 16 + 8 * E)

            @block.vector
            def _(dve):
                dve.sem_inc(h_ready, 1)
                dve.sem_inc(h_copied, 1)
                dve.sem_inc(y_kept, 1)

                def times_up(e):
                    dve.wait_ge(silu_done, e + 2)
                    dve.wait_ge(u_done, e + 3)
                    if not (isinstance(e, int) and e == 0):
                        dve.wait_ge(h_turned, e)
                    nc.vector.tensor_tensor(h[:, :], gate[:, :], ps_u[:, :], ALU.mult).then_inc(h_ready, 1)

                def copy_h(e):
                    dve.wait_ge(h_turned, e + 1)
                    dve.wait_ge(d_done, e + 2)
                    nc.vector.tensor_copy(ht[:, :, :], ps_h[:, :, :]).then_inc(h_copied, 1)

                def keep_y(e, b):
                    dve.wait_ge(d_done, e + 3)
                    dve.wait_ge(y_out[b], (e - b) * 8 + 16)
                    nc.vector.tensor_copy(y[b][:, :], ps_y[:, :, :].rearrange("p a b -> p (a b)")).then_inc(y_kept, 1)

                times_up(0)
                copy_h(0)

                def body(e, b):
                    times_up(e)
                    keep_y(e - 1, 1 - b)
                    copy_h(e)

                pairs(dve, body, 0, E // 2 - 1, 1)
                times_up(E - 1)
                keep_y(E - 2, 0)
                copy_h(E - 1)
                keep_y(E - 1, 1)


def overflow_experts(nc, k):
    with Space(nc, "ov") as s:
        w_g, w_u, w_d = s.sb("w_g", [P, KD, DE]), s.sb("w_u", [P, KD, DE]), s.sb("w_d", [P, FF, D])
        xb, idx, w_idx = s.sb("xb", [P, D]), s.sb("idx", [P, 1], U32), s.sb("w_idx", [P, 1], U32)
        xt, gate, h, ht = s.sb("xt", [P, KD, P]), s.sb("gate", [P, DE]), s.sb("h", [P, DE]), s.sb("ht", [P, FF, P])
        y = s.sb("y", [P, D])
        ps_x, ps_y = s.ps("x", [P, KD, P]), s.ps("y", [P, 2, HALF])
        ps_g, ps_u, ps_h = s.ps("g", [P, DE]), s.ps("u", [P, DE]), s.ps("h", [P, FF, P])
        (idx_ready, loaded, x_turned, x_copied, gu_done, silu_done, h_ready, h_turned, h_copied, d_done, y_kept, stored,
         idx_stood) = (
            s.sem(n) for n in ("idx_ready", "loaded", "x_turned", "x_copied", "gu_done", "silu_done", "h_ready", "h_turned",
                               "h_copied", "d_done", "y_kept", "stored", "idx_stood"))
        rows = [w.rearrange("e (p k) f -> (e p) (k f)", p=P) for w in (k.exp_gate, k.exp_up, k.exp_down)]
        y_blocks = k.y_slots.rearrange("(b p) d -> b p d", p=P)

        def blocks(eng, body):
            with eng.Fori(0, OVER) as j:
                unused = eng.value_load(k.unused[0:1, bass.ds(j, 1)], min_val=0, max_val=1)
                with eng.If(unused < 1):
                    body(j)
                with eng.Else():
                    pass

        with s.block() as block:
            @block.gpsimd
            def _(pool):
                def body(j):
                    nc.gpsimd.tensor_copy(idx[:, :], k.slot_token[:, bass.ds(j + E, 1)]).then_inc(idx_ready, 1)
                    nc.gpsimd.tensor_copy(w_idx[:, :], k.over_rows[:, bass.ds(j, 1)]).then_inc(idx_ready, 1)
                    wait_apart(pool, idx_ready, 2 * j + 2, idx_stood)
                    pool.indirect_dma_start(xb[:, :], None, k.x1_d, bass.IndirectOffsetOnAxis(ap=idx[:, :], axis=0)
                                            ).then_inc(loaded, 16)
                    for w, src in ((w_g, rows[0]), (w_u, rows[1]), (w_d, rows[2])):
                        pool.indirect_dma_start(w[:, :, :].rearrange("p k f -> p (k f)"), None, src,
                                                bass.IndirectOffsetOnAxis(ap=w_idx[:, :], axis=0)).then_inc(loaded, 16)
                    pool.wait_ge(y_kept, j + 1)
                    pool.dma_start(y_blocks[bass.ds(j + E, 1)].rearrange("a p d -> (a p) d"), y[:, :]).then_inc(stored, 16)
                    pool.wait_ge(stored, 16 * j + 16)

                blocks(pool, body)

            @block.tensor
            def _(pe):
                mm = nc.tensor.matmul

                def body(j):
                    pe.wait_ge(loaded, 64 * j + 64)
                    for c in range(KD):
                        m = nc.tensor.transpose(ps_x[:, c, :], xb[:, c::KD], mat(k, "ident"))
                    m.then_inc(x_turned, 1)
                    pe.wait_ge(x_copied, j + 1)
                    for w, ps in ((w_g, ps_g), (w_u, ps_u)):
                        for c in range(KD):
                            m = mm(ps[:, :], xt[:, c, :], w[:, c, :], start=(c == 0), stop=(c == KD - 1))
                        m.then_inc(gu_done, 1)
                    pe.wait_ge(h_ready, j + 1)
                    for c in range(FF):
                        m = nc.tensor.transpose(ps_h[:, c, :], h[:, c::FF], mat(k, "ident"))
                    m.then_inc(h_turned, 1)
                    pe.wait_ge(h_copied, j + 1)
                    for half in range(2):
                        for c in range(FF):
                            m = mm(ps_y[:, half, :], ht[:, c, :], w_d[:, c, half * HALF:(half + 1) * HALF], start=(c == 0),
                                   stop=(c == FF - 1))
                    m.then_inc(d_done, 1)

                blocks(pe, body)

            @block.scalar
            def _(act):
                def body(j):
                    act.wait_ge(x_turned, j + 1)
                    nc.scalar.copy(xt[:, :, :], ps_x[:, :, :]).then_inc(x_copied, 1)
                    act.wait_ge(gu_done, 2 * j + 1)
                    nc.scalar.activation(gate[:, :], ps_g[:, :], ACT.Silu).then_inc(silu_done, 1)

                blocks(act, body)

            @block.vector
            def _(dve):
                def body(j):
                    dve.wait_ge(silu_done, j + 1)
                    dve.wait_ge(gu_done, 2 * j + 2)
                    nc.vector.tensor_tensor(h[:, :], gate[:, :], ps_u[:, :], ALU.mult).then_inc(h_ready, 1)
                    dve.wait_ge(h_turned, j + 1)
                    nc.vector.tensor_copy(ht[:, :, :], ps_h[:, :, :]).then_inc(h_copied, 1)
                    dve.wait_ge(d_done, j + 1)
                    nc.vector.tensor_copy(y[:, :], ps_y[:, :, :].rearrange("p a b -> p (a b)")).then_inc(y_kept, 1)

                blocks(dve, body)


def combine(nc, k):
    with Space(nc, "cb") as s:
        ln = s.sb("ln", [P, 2, D])
        idx = [[s.sb(f"idx{n}{b}", [P, 1], U32) for b in range(2)] for n in range(2)]
        y1, y2 = ([s.sb(f"y{n}{b}", [P, D]) for b in range(2)] for n in "12")
        x1, res = ([s.sb(f"{n}{b}", [P, D]) for b in range(2)] for n in ("x1", "res"))
        stats, mv, sd, eps = s.sb("stats", [P, 2, 6]), s.sb("mv", [P, 2]), s.sb("sd", [P, 1]), s.sb("eps", [P, 1])
        y_in, x_in, stored = ([s.sem(f"{n}{b}") for b in range(2)] for n in ("y_in", "x_in", "stored"))
        ln_in, idx_ready, weighted, aggregated, root_done, normed, eps_set, last, halves, stood, idx_stood = (s.sem(n) for n in (
            "ln_in", "idx_ready", "weighted", "aggregated", "root_done", "normed", "eps_set", "last",
            "halves", "stood", "idx_stood"))
        x1_rows = k.x1_d.rearrange("(n p) d -> n p d", p=P)
        out_rows = k.out.rearrange("a (n p) d -> (a n) p d", p=P)

        def tiles(eng, body):
            with eng.Fori(0, NT // 2) as i:
                for b in range(2):
                    body(2 * i + b, b)

        def tile_of(t, i):
            return t[:, bass.ds(i, 1), :].rearrange("p a d -> p (a d)")

        with s.block() as block:
            @block.sync
            def _(sp):
                for b in range(2):
                    sp.sem_inc(stored[b], 16)
                for n in range(2):
                    sp.dma_start(ln[:, n, :], k.ln2[n:n + 1, :].partition_broadcast(P)).then_inc(ln_in, 16)

                def load(t, b):
                    sp.wait_ge(normed, t + 1)
                    sp.dma_start(x1[b][:, :], x1_rows[bass.ds(t, 1)].rearrange("a p d -> (a p) d")).then_inc(x_in[b], 16)

                def store(t, b):
                    sp.wait_ge(normed, t + 3)
                    sp.dma_start(out_rows[bass.ds(t, 1)].rearrange("a p d -> (a p) d"), res[b][:, :]
                                 ).then_inc(stored[b], 16)

                load(0, 0)
                load(1, 1)
                with sp.Fori(0, NT // 2 - 1) as i:
                    for b in range(2):
                        store(2 * i + b, b)
                        load(2 * i + b + 2, b)
                for b in range(2):
                    store(NT - 2 + b, b)
                for b in range(2):
                    sp.wait_ge(stored[b], 16 + 8 * NT)

            @block.gpsimd
            def _(pool):
                def gather(t, b):
                    pool.wait_ge(normed, t + 1)
                    for n, y in ((0, y1), (1, y2)):
                        nc.gpsimd.tensor_copy(idx[n][b][:, :], tile_of(k.dest, t)[:, n:n + 1]).then_inc(idx_ready, 1)
                    wait_apart(pool, idx_ready, 2 * t + 2, idx_stood)
                    for n, y in ((0, y1), (1, y2)):
                        pool.indirect_dma_start(y[b][:, :], None, k.y_slots, bass.IndirectOffsetOnAxis(
                            ap=idx[n][b][:, :], axis=0)).then_inc(y_in[b], 16)

                tiles(pool, gather)

            @block.scalar
            def _(act):
                act.wait_ge(eps_set, 1)

                def body(t, b):
                    act.wait_ge(y_in[b], (t - b) * 16 + 32)
                    nc.scalar.activation(y1[b][:, :], y1[b][:, :], ACT.Copy, scale=tile_of(k.gates, t)[:, 0:1]
                                         ).then_inc(weighted, 1)
                    act.wait_ge(aggregated, t + 1)
                    nc.scalar.activation(sd[:, :], mv[:, 1:2], ACT.Sqrt, bias=eps[:, :]).then_inc(root_done, 1)

                tiles(act, body)

            @block.vector
            def _(dve):
                v = nc.vector
                dve.sem_inc(normed, 2)
                v.memset(eps[:, :], LN_EPS).then_inc(eps_set, 1)
                dve.wait_ge(ln_in, 32)

                def body(t, b):
                    link = Chain(dve, last)
                    link.base = t * 5
                    dve.wait_ge(weighted, t + 1)
                    link(v.scalar_tensor_tensor(y2[b][:, :], y2[b][:, :], tile_of(k.gates, t)[:, 1:2], y1[b][:, :], ALU.mult,
                                                ALU.add))
                    dve.wait_ge(x_in[b], (t - b) * 8 + 16)
                    link(v.scalar_tensor_tensor(y2[b][:, :], x1[b][:, :], ALPHA, y2[b][:, :], ALU.mult, ALU.add))
                    dve.wait_ge(stored[b], (t - b) * 8 + 16)
                    layer_norm(nc, dve, link, y2[b], res[b][:, :], ln, mv, stats, sd, halves, stood, (aggregated, 1, t + 1),
                               lambda: dve.wait_ge(root_done, t + 1)).then_inc(normed, 1)

                tiles(dve, body)


class Trunk:

    def __init__(self, a):
        self.x, self.mats_d, self.head_rows_d, self.cols_d, self.w_tiles = (
            a["x"], a["mats_d"], a["head_rows_d"], a["cols_d"], a["w_tiles"])
        self.w_fox_v, self.w_small, self.rwkv_w_up, self.rwkv_a_up, self.rwkv_g_up = (
            a["w_fox_v"], a["w_small"], a["rwkv_w_up"], a["rwkv_a_up"], a["rwkv_g_up"])
        self.f_bias, self.dt_bias, self.a_log, self.w_br, self.w_out = (
            a["f_bias"], a["dt_bias"], a["a_log"], a["w_br"], a["w_out"])
        self.ln1, self.ln2, self.router_w, self.router_b, self.exp_gate = (
            a["ln1"], a["ln2"], a["router_w"], a["router_b"], a["exp_gate"])
        self.exp_up, self.exp_down, self.out = (
            a["exp_up"], a["exp_down"], a["out"])


def trunk(nc, aps, stages=None):
    k = Trunk(aps)
    with ExitStack() as ctx:
        def sb(name, shape, dt=F32):
            return ctx.enter_context(nc.sbuf_tensor(name, shape, dt))

        k.mats = sb("mats", [P, N_MATS])
        k.cols = sb("cols", [P, N_COLS])
        room = sb("room", [P, NCONV - SG, T])
        def scratch(name, shape):
            return nc.dram_tensor(name, shape, F32, kind="Internal").ap()

        k.chunk_ch = scratch("chunk_ch", (NT, P, RT, 4, P))
        k.chunk_tok = scratch("chunk_tok", (3, NT, P, RT, P))
        k.fox_qk = scratch("fox_qk", (2 * FH, HD, T))
        k.fox_c = scratch("fox_c", (2, FH, T))
        k.x1_d = scratch("x1_d", (T, D))
        k.buf_tok = scratch("buf_tok", (N_BLOCKS * P, 1))
        k.y_slots = scratch("y_slots", (N_BLOCKS * P, D))

        def run(*every):
            for stage in every:
                if stages is None or stage.__name__ in stages:
                    stage(nc, k)

        with ExitStack() as mixers:
            def mixer_sb(name, shape):
                return mixers.enter_context(nc.sbuf_tensor(name, shape, F32))

            k.xT, k.rwkv_oT = mixer_sb("xT", [P, KD, T]), mixer_sb("rwkv_oT", [P, RT, T])
            run(transpose_x)
            k.bonus, k.gate_in = room[:, 0:RT, :], room[:, RT, :]
            k.spare = room[:, RT + 1:2 * RT + 1, :]
            k.decays = mixer_sb("decays", [P, RT, NT])
            run(rwkv_inputs, rwkv_chunks, rwkv_outputs)
            k.fox_oT, k.dt_raw = mixer_sb("fox_oT", [P, RT, T]), mixer_sb("dt_raw", [SH, T])
            k.fox_v = room[:, 0:4, :].rearrange("p a (b c) -> p (a b) c", c=FH * HD)
            run(fox_project, fox_attend)
            k.ssm = mixer_sb("ssm", [P, NCONV, T])
            k.ssm_tok = room[:, :, :].rearrange("p a t -> p (a t)").rearrange("p (c d) -> p c d", c=NT)
            run(ssm_inputs, ssm_scan, ssm_outputs)
            k.merged, k.spare = room[:, 0:KD, :], room[:, KD:, :]
            run(merge)
        k.aff, k.sel = sb("aff", [P, NT, E]), sb("sel", [P, NT, E])
        k.gates = sb("gates", [P, NT, 2])
        k.dest = sb("dest", [P, NT, 2], U32)
        k.slot_token = sb("slot_token", [P, N_BLOCKS], U32)
        k.over_rows = sb("over_rows", [P, 16], U32)
        k.unused = sb("unused", [P, 16], I32)
        run(out_project, route, experts, overflow_experts, combine)


def lay_out(inputs):
    a = {n: np.asarray(v) for n, v in inputs.items()}
    w_in = a["w_in"][0]
    fox, ssm = 1792, 1792 + 1544
    gate = ssm + 2576
    main = np.concatenate([w_in[:, :fox], w_in[:, fox:fox + 1024], w_in[:, ssm:ssm + 1024 + 1536], w_in[:, gate:]], axis=1)

    def tiles(w):
        kk, n = w.shape
        return np.ascontiguousarray(w.reshape(kk // P, P, n // P, P).transpose(2, 1, 0, 3))

    def rows(w):
        return np.ascontiguousarray(w.reshape(w.shape[0] // P, P, w.shape[1]).transpose(1, 0, 2))

    def per_channel(v):
        return v.reshape(-1, P).T

    cols = np.concatenate([
        per_channel(a["rwkv_mu"][0]), per_channel(a["rwkv_w0"][0]), per_channel(a["rwkv_a0"][0]),
        per_channel(a["rwkv_k_k"][0]), per_channel(a["rwkv_k_a"][0]), per_channel(a["rwkv_r_k"][0]),
        per_channel(a["rwkv_gn_g"][0]), per_channel(a["rwkv_gn_b"][0]), per_channel(a["ssm_conv_w"][0]),
        per_channel(a["ssm_conv_b"][0]), per_channel(np.repeat(a["ssm_d"][0], HD)), per_channel(a["ssm_norm_g"][0]),
        per_channel(a["gate_bias"][0])], axis=1)
    return {
        "x": a["x"],
        "mats_d": constant_matrices(),
        "head_rows_d": head_rows(),
        "cols_d": np.ascontiguousarray(cols),
        "w_tiles": tiles(main),
        "w_fox_v": rows(w_in[:, fox + 1024:fox + 1536]),
        "w_small": rows(np.concatenate([w_in[:, fox + 1536:fox + 1544], np.zeros((D, 24), np.float32),
                                        w_in[:, gate - SH:gate]], axis=1)),
        "rwkv_w_up": a["rwkv_w_up"][0], "rwkv_a_up": a["rwkv_a_up"][0], "rwkv_g_up": a["rwkv_g_up"][0],
        "f_bias": np.ascontiguousarray(a["fox_f_bias"].reshape(FH, 1)),
        "dt_bias": np.ascontiguousarray(a["ssm_dt_bias"].reshape(SH, 1)),
        "a_log": np.ascontiguousarray(a["ssm_a_log"].reshape(SH, 1)),
        "w_br": np.concatenate([tiles(a["w_br_rwkv"][0]), tiles(a["w_br_fox"][0]), tiles(a["w_br_ssm"][0])], axis=2),
        "w_out": rows(a["w_out"][0]),
        "ln1": np.concatenate([a["ln1_g"], a["ln1_b"]]), "ln2": np.concatenate([a["ln2_g"], a["ln2_b"]]),
        "router_w": rows(a["router_w"]),
        "router_b": a["router_bias"].reshape(1, E),
        "exp_gate": a["exp_w_gate"][0], "exp_up": a["exp_w_up"][0], "exp_down": a["exp_w_down"][0],
    }


def kernel(**inputs):
    import concourse.bacc as bacc
    from concourse.bass_utils import run_bass_kernel_spmd

    nc = bacc.Bacc("TRN2", target_bir_lowering=False, num_devices=1)
    arrays = lay_out(inputs)
    aps = {n: nc.dram_tensor(n, v.shape, mybir.dt.from_np(v.dtype), kind="ExternalInput").ap() for n, v in arrays.items()}
    aps["out"] = nc.dram_tensor("out", (1, T, D), F32, kind="ExternalOutput").ap()
    trunk(nc, aps)
    r = run_bass_kernel_spmd(nc, [arrays], core_ids=[0])
    return r.results[0]["out"]
```

```python
from contextlib import ExitStack

import numpy as np
import concourse.bass as bass
from concourse import mybir

F32 = mybir.dt.float32
F32R = mybir.dt.float32r
BF16 = mybir.dt.bfloat16
I32 = mybir.dt.int32
U32 = mybir.dt.uint32
ALU = mybir.AluOpType
ACT = mybir.ActivationFunctionType
AX = mybir.AxisListType

P = 128
D = 1024
T = 1024
KD = D // P
NT = T // P
HALF = 512
RH, HD = 8, 64
RT = RH * HD // P
FH = 8
SH, SG, SN = 16, 2, 128
ST = SH * HD // P
NCONV = 12
TAPS = 4
E, EG, EPG = 32, 4, 8
DE = 512
FF = DE // P
OVER = 15
N_BLOCKS = E + OVER
KAPPA = float(np.exp(-0.5))
RWKV_EPS, NORM_EPS, LN_EPS = 64e-5, 1e-5, 1e-5
ALPHA = 2.0 ** 0.25
NEG = -1.0e30

T_R, T_K, T_V, T_WA, T_G = 0, 4, 8, 12, 13
T_FQ, T_FK = 14, 18
T_Z, T_XBC = 22, 30
T_GATE = 42
N_TILES = 66

COLS = {}
_at = 0
for _name, _n in (("mu", 14), ("w0", RT), ("a0", RT), ("k_k", RT), ("k_a", RT), ("r_k", RT), ("gn_g", RT), ("gn_b", RT),
                  ("conv_w", TAPS * NCONV), ("conv_b", NCONV), ("ssm_d", ST), ("norm_g", ST), ("gate_bias", 3 * KD)):
    COLS[_name] = _at
    _at += _n
N_COLS = _at

MATS = {}
_at = 0
for _name, _n in (("ident", P), ("ones", P), ("before", P), ("before_or_at", P), ("reset", T), ("head_ones", P), ("experts", E),
                  ("group_of", E), ("slot0", E), ("row0", 16), ("over_ids", 16),
                  ("after", P), ("levels", 7 * P), ("level0_t", P)):
    MATS[_name] = _at
    _at += _n
RWKV_MATS = MATS["after"]
N_MATS = _at


def constant_matrices():
    m = np.zeros((P, N_MATS), np.float32)
    i, j = np.arange(P)[:, None], np.arange(P)[None, :]

    def put(name, what):
        m[:, MATS[name]:MATS[name] + what.shape[1]] = what

    put("ident", (i == j) * 1.0)
    put("ones", np.ones((P, P)))
    put("head_ones", (i // HD == j // HD) * 1.0)
    put("before", (i < j) * 1.0)
    put("before_or_at", (i <= j) * 1.0)
    put("after", (i > j) * 1.0)
    for n in range(7):
        b = 1 << n
        level = (i // (2 * b) == j // (2 * b)) & (i % (2 * b) >= b) & (j % (2 * b) < b)
        m[:, MATS["levels"] + n * P:MATS["levels"] + (n + 1) * P] = level if n == 0 else level + (i == j)
        if n == 0:
            put("level0_t", level.T * 1.0)
    put("reset", np.broadcast_to(np.arange(T) % P != 0, (P, T)) * 1.0)
    e = np.broadcast_to(np.arange(E), (P, E))
    put("experts", e * 1.0)
    put("group_of", e // EPG * 1.0)
    put("slot0", e * float(P))
    put("row0", np.broadcast_to(i, (P, 16)) * 1.0)
    put("over_ids", np.broadcast_to(np.arange(16), (P, 16)) * 1.0)
    return m


def head_rows():
    return np.ascontiguousarray(np.broadcast_to(np.eye(SH, dtype=np.float32)[:, :, None], (SH, SH, P)))


class Chain:

    def __init__(self, eng, sem, per_round=0):
        self.eng, self.sem, self.n, self.base, self.per_round = eng, sem, 0, 0, per_round

    def round(self, i):
        assert self.n in (0, self.per_round) or self.base is None, (self.n, self.per_round)
        self.base, self.n = i * self.per_round, 0

    def __call__(self, ins):
        self.n += 1
        ins.then_inc(self.sem, 1)
        self.eng.wait_ge(self.sem, self.base + self.n)

    def done(self):
        assert self.n == self.per_round, (self.n, self.per_round)


class Space:

    def __init__(self, nc, stage):
        self.nc, self.stage, self.ctx, self.sems = nc, stage, ExitStack(), []

    def __enter__(self):
        return self

    def __exit__(self, *a):
        if a[0] is None:
            self.nc.clear_and_free_semaphores(self.sems)
            self.nc.all_engine_barrier()
        return self.ctx.__exit__(*a)

    def sb(self, name, shape, dt=F32):
        return self.ctx.enter_context(self.nc.sbuf_tensor(f"{self.stage}_sb_{name}", shape, dt))

    def ps(self, name, shape, dt=F32):
        return self.ctx.enter_context(self.nc.psum_tensor(f"{self.stage}_ps_{name}", shape, dt))

    def sem(self, name):
        self.sems.append(self.nc.alloc_semaphore(f"{self.stage}_{name}"))
        return self.sems[-1]

    def block(self):
        return self.nc.Block()


def wait_apart(eng, sem, value, stood):
    eng.wait_ge(sem, value)
    eng.sem_inc(stood, 1)


def col(k, name, i=0):
    return k.cols[:, bass.ds(i + COLS[name], 1)]


def mat(k, name, n=P, at=0):
    m, at = (k.rwkv_mats, at - RWKV_MATS) if MATS[name] >= RWKV_MATS else (k.mats, at)
    return m[:, MATS[name] + at:MATS[name] + at + n]


def times(nc, out, lhs, rhs, start, stop):
    nc.tensor.matmul(out, lhs[0], rhs[0], start=start, stop=False)
    nc.tensor.matmul(out, lhs[0], rhs[1], start=False, stop=False)
    return nc.tensor.matmul(out, lhs[1], rhs[0], start=False, stop=stop)


def project(nc, out, w, xT, halves=(0, 1)):
    for half in halves:
        for k in range(KD):
            last = nc.tensor.matmul(out[:, half, :], w[:, k, :], xT[:, k, half * HALF:(half + 1) * HALF],
                                    start=(k == 0), stop=(k == KD - 1))
    return last


def project_parts(nc, out, w, x, halves=(0, 1)):
    for half in halves:
        at = slice(half * HALF, (half + 1) * HALF)
        for k in range(KD):
            last = times(nc, out[:, half, :], (w[0][:, k, :], w[1][:, k, :]), (x[0][:, k, at], x[1][:, k, at]), k == 0,
                         k == KD - 1)
    return last


def split(eng, high, low, full, rounded, count, done, stood):
    eng.sem_inc(stood, 1)
    eng.tensor_copy(high, full).then_inc(rounded, 1)
    wait_apart(eng, rounded, count, stood)
    eng.tensor_tensor(low, full, high, ALU.subtract).then_inc(done, 1)


class SplitWeights:

    def __init__(self, s, used):
        self.full = s.sb("w", [P, KD, P])
        self.high, self.low = ([s.sb(f"{n}{b}", [P, KD, P], F32R) for b in range(2)] for n in ("w_high", "w_low"))
        self.loaded, self.rounded, self.ready, self.stood = (s.sem(n) for n in (
            "w_loaded", "w_rounded", "w_ready", "w_stood"))
        self.used = used

    def start(self, eng):
        eng.sem_inc(self.ready, 1)

    def load(self, eng, k, t, tile):
        eng.wait_ge(self.ready, t + 1)
        eng.dma_start(self.full[:, :, :], k.w_tiles[bass.ds(tile, 1)].rearrange("a p k c -> (a p) k c")
                      ).then_inc(self.loaded, 16)

    def cut(self, pool, t, b):
        pool.wait_ge(self.used, t + 1)
        pool.wait_ge(self.loaded, t * 16 + 16)
        split(pool, self.high[b][:, :, :], self.low[b][:, :, :], self.full[:, :, :], self.rounded, t + 1, self.ready,
              self.stood)

    def project(self, nc, k, out, t, b):
        nc.tensor.wait_ge(self.ready, t + 2)
        return project_parts(nc, out, (self.high[b], self.low[b]), (k.x_high, k.x_low))


def transpose_x(nc, k):
    with Space(nc, "xt") as s:
        xs = [s.sb(f"x{b}", [P, D]) for b in range(2)]
        ps = [s.ps(f"t{b}", [P, KD, P]) for b in range(2)]
        consts_in = s.sem("consts_in")
        x_in = [s.sem(f"x_in{b}") for b in range(2)]
        turned = s.sem("turned")
        copied = [s.sem(f"copied{h}") for h in range(2)]
        x_rows = k.x.rearrange("a (n p) d -> (a n) p d", p=P)
        with s.block() as block:
            @block.sync
            def _(sp):
                sp.dma_start(k.mats[:, :], k.mats_d[:, 0:RWKV_MATS]).then_inc(consts_in, 16)
                sp.dma_start(k.rwkv_mats[:, :], k.mats_d[:, RWKV_MATS:]).then_inc(consts_in, 16)
                sp.dma_start(k.cols[:, :], k.cols_d).then_inc(consts_in, 16)
                with sp.Fori(0, NT // 2) as i:
                    for b in range(2):
                        sp.wait_ge(turned, 2 * i + b + 1)
                        sp.dma_start(xs[b][:, :], x_rows[bass.ds(2 * i + b, 1)].rearrange("a p d -> (a p) d")
                                     ).then_inc(x_in[b], 16)
                sp.wait_ge(consts_in, 48)

            @block.tensor
            def _(pe):
                pe.sem_inc(turned, 2)
                pe.wait_ge(consts_in, 48)
                with pe.Fori(0, NT // 2) as i:
                    for b in range(2):
                        pe.wait_ge(x_in[b], 16 * i + 16)
                        for h in range(2):
                            pe.wait_ge(copied[h], 2 * i + b + 1)
                        for c in range(KD):
                            last = nc.tensor.transpose(ps[b][:, c, :], xs[b][:, c * P:(c + 1) * P], mat(k, "ident"))
                        last.then_inc(turned, 1)

            def copy_half(eng, op, half):
                eng.sem_inc(copied[half], 2)
                with eng.Fori(0, NT // 2) as i:
                    for b in range(2):
                        eng.wait_ge(turned, 2 * i + b + 3)
                        op(k.xT[:, half * 4:half * 4 + 4, bass.ts(2 * i + b, P)],
                           ps[b][:, half * 4:half * 4 + 4, :]).then_inc(copied[half], 1)

            @block.scalar
            def _(act):
                copy_half(act, nc.scalar.copy, 0)

            @block.vector
            def _(dve):
                copy_half(dve, nc.vector.tensor_copy, 1)


def rwkv_inputs(nc, k):
    with Space(nc, "ri") as s:
        w_k, w_v, w_r = s.sb("w_k", [P, KD, P]), s.sb("w_v", [P, KD, P]), s.sb("w_r", [P, KD, P])
        w_up = s.sb("w_up", [P, P])
        raw_k, raw_v, raw_r = (s.sb(f"raw_{n}", [P, T + 4]) for n in "kvr")
        diff = s.sb("diff", [P, T])
        wa = s.sb("wa", [P, T])
        kx, vx, rx = s.sb("kx", [P, T]), s.sb("vx", [P, T]), s.sb("rx", [P, T])
        kk, sq, norm = s.sb("kk", [P, T]), s.sb("sq", [P, T]), s.sb("norm", [P, T])
        sg, cum, cc, cx = (k.mixer_oT[:, c, :] for c in range(4))
        rate, k2, b, rkk = s.sb("rate", [P, T]), s.sb("k2", [P, T]), s.sb("b", [P, T]), s.sb("rkk", [P, T])
        e_pos, e_neg, e_ex = k.slab[:, 7, :], cc, cx
        ch = k.slab[:, 0:4, :].rearrange("p a t -> p (a t)").rearrange("p (c n t) -> p c n t", c=NT, n=4)
        tok = k.slab[:, 4:7, :].rearrange("p a (n t) -> p a n t", t=P)
        span = s.sb("span", [P, NT])
        ka1 = s.sb("ka1", [P, RT])
        ps_a, ps_b = s.ps("a", [P, 2, HALF]), s.ps("b", [P, 2, HALF])
        ps_x, ps_t = s.ps("x", [P, 2, HALF]), s.ps("t", [P, NT, P])
        (k_loaded, v_loaded, r_loaded, up_loaded, ch_out, tok_out) = (
            s.sem(n) for n in ("k_loaded", "v_loaded", "r_loaded", "up_loaded", "ch_out", "tok_out"))
        (inner_proj, k_proj, v_proj, r_proj, lora_w, lora_a, norm_sum, bonus_sum, turned) = (
            s.sem(n) for n in ("inner_proj", "k_proj", "v_proj", "r_proj", "lora_w", "lora_a", "norm_sum", "bonus_sum",
                               "turned"))
        (inner_raw, inner_done, k_raw, v_raw, r_raw, sg_ready, rate_ready, sq_ready, norm_ready, exps_ready, tok_ready) = (
            s.sem(n) for n in ("inner_raw", "inner_done", "k_raw", "v_raw", "r_raw", "sg_ready", "rate_ready",
                               "sq_ready", "norm_ready", "exps_ready", "tok_ready"))
        (inner_mixed, pads, k_mixed, v_mixed, r_mixed, kk_ready, cc_ready, ch_ready, rkk_ready, bonus_ready, dve_last) = (
            s.sem(n) for n in ("inner_mixed", "pads", "k_mixed", "v_mixed", "r_mixed", "kk_ready", "cc_ready",
                               "ch_ready", "rkk_ready", "bonus_ready", "dve_last"))
        norm_floored, tok_free = s.sem("norm_floored"), s.sem("tok_free")

        def w_tile(i):
            return k.w_tiles[bass.ds(i, 1)].rearrange("a p k c -> (a p) k c")

        def up_tile(w, i):
            return w[:, bass.ts(i, P)]

        def rounds(eng, body):
            body(0, True)
            with eng.Fori(1, RT) as i:
                body(i, False)

        x_out = s.sem("x_out")
        with s.block() as block:
            @block.sync
            def _(sp):
                sp.dma_start(w_k[:, :, :], k.w_tiles[T_WA]).then_inc(k_loaded, 16)
                sp.dma_start(w_v[:, :, :], k.w_tiles[T_G]).then_inc(v_loaded, 16)

                def load(i, first):
                    sp.wait_ge(inner_proj, 1) if first else sp.wait_ge(k_proj, i)
                    sp.dma_start(w_k[:, :, :], w_tile(i + T_K)).then_inc(k_loaded, 16)
                    sp.wait_ge(inner_proj, 2) if first else sp.wait_ge(v_proj, i)
                    sp.dma_start(w_v[:, :, :], w_tile(i + T_V)).then_inc(v_loaded, 16)
                    if not first:
                        sp.wait_ge(lora_a, i)
                    sp.dma_start(w_up[0:HD, :], up_tile(k.rwkv_w_up, i)).then_inc(up_loaded, 16)
                    sp.dma_start(w_up[HD:P, :], up_tile(k.rwkv_a_up, i)).then_inc(up_loaded, 16)
                    if not first:
                        sp.wait_ge(r_proj, i)
                    sp.dma_start(w_r[:, :, :], w_tile(i + T_R)).then_inc(r_loaded, 16)

                rounds(sp, load)

            @block.gpsimd
            def _(pool):
                def store(i, first):
                    if not first:
                        pool.wait_ge(tok_out, 48 * i)
                    pool.sem_inc(tok_free, 1)
                    pool.wait_ge(ch_ready, i + 1)
                    pool.dma_start(k.chunk_ch[:, :, bass.ds(i, 1)].rearrange("c p o a b -> p c (o a b)"),
                                   ch[:, :, :, :].rearrange("p c a b -> p c (a b)")).then_inc(ch_out, 16)
                    for n in range(3):
                        pool.wait_ge(tok_ready, 3 * i + n + 2)
                        pool.dma_start(k.chunk_tok[n, :, :, bass.ds(i, 1)].rearrange("c p o b -> p c (o b)"),
                                       tok[:, n, :, :]).then_inc(tok_out, 16)

                pool.dma_start(k.xT_d.rearrange("i p t -> p i t"), k.xT[:, :, :]).then_inc(x_out, 16)
                rounds(pool, store)
                pool.wait_ge(x_out, 16)
                pool.wait_ge(ch_out, 16 * RT)
                pool.wait_ge(tok_out, 48 * RT)

            @block.tensor
            def _(pe):
                pe.wait_ge(k_loaded, 16)
                project(nc, ps_a, w_k, k.xT).then_inc(inner_proj, 1)
                pe.wait_ge(v_loaded, 16)
                project(nc, ps_b, w_v, k.xT).then_inc(inner_proj, 1)

                def both(out, lhsT, rhs, lo=0, hi=P):
                    for h in range(2):
                        last = nc.tensor.matmul(out[:, h, :], lhsT, rhs[lo:hi, h * HALF:(h + 1) * HALF],
                                                start=True, stop=True)
                    return last

                def finish(i):
                    pe.wait_ge(rkk_ready, i)
                    pe.wait_ge(norm_ready, i)
                    both(ps_x, mat(k, "head_ones"), rkk).then_inc(bonus_sum, 1)
                    pe.wait_ge(ch_ready, i)
                    pe.wait_ge(v_mixed, i)
                    for n in range(3):
                        pe.wait_ge(tok_ready, 3 * i + n - 3 + 1)
                        for c in range(NT):
                            src = vx[:, c * P:(c + 1) * P] if n == 0 else ch[:, c, 1 + n, :]
                            last = nc.tensor.transpose(ps_t[:, c, :], src, mat(k, "ident"))
                        last.then_inc(turned, 1)

                def body(i, first):
                    pe.wait_ge(k_loaded, 16 * i + 32)
                    if first:
                        pe.wait_ge(inner_raw, 1)
                    else:
                        pe.wait_ge(r_raw, i)
                    project(nc, ps_a, w_k, k.xT).then_inc(k_proj, 1)
                    if not first:
                        finish(i)
                    pe.wait_ge(v_loaded, 16 * i + 32)
                    if first:
                        pe.wait_ge(inner_raw, 2)
                    else:
                        pe.wait_ge(v_raw, i)
                    project(nc, ps_b, w_v, k.xT).then_inc(v_proj, 1)
                    pe.wait_ge(up_loaded, 32 * i + 32)
                    if first:
                        pe.wait_ge(inner_done, 3)
                    else:
                        pe.wait_ge(bonus_ready, i)
                    both(ps_x, w_up[0:HD, :], wa, 0, HD).then_inc(lora_w, 1)
                    pe.wait_ge(sg_ready, i + 1)
                    both(ps_x, w_up[HD:P, :], wa, HD, P).then_inc(lora_a, 1)
                    pe.wait_ge(rate_ready, i + 1)
                    pe.wait_ge(sq_ready, i + 1)
                    both(ps_x, mat(k, "head_ones"), sq).then_inc(norm_sum, 1)
                    pe.wait_ge(r_loaded, 16 * i + 16)
                    pe.wait_ge(k_raw, i + 1)
                    project(nc, ps_a, w_r, k.xT).then_inc(r_proj, 1)

                rounds(pe, body)
                finish(RT)

            @block.scalar
            def _(act):
                act.sem_inc(tok_ready, 1)
                flat = lambda ps: ps[:, :, :].rearrange("p a b -> p (a b)")
                act.wait_ge(pads, 3)
                act.wait_ge(inner_proj, 1)
                nc.scalar.copy(raw_k[:, 1:T + 1], flat(ps_a)).then_inc(inner_raw, 1)
                act.wait_ge(inner_proj, 2)
                nc.scalar.copy(raw_v[:, 1:T + 1], flat(ps_b)).then_inc(inner_raw, 1)
                act.wait_ge(inner_mixed, 2)
                nc.scalar.activation(wa[0:HD, :], kx[0:HD, :], ACT.Tanh).then_inc(inner_done, 1)
                nc.scalar.copy(wa[HD:P, :], kx[HD:P, :]).then_inc(inner_done, 1)
                nc.scalar.activation(k.gate_in[:, :], vx[:, :], ACT.Sigmoid).then_inc(inner_done, 1)

                def turn_out(i):
                    for n in range(3):
                        act.wait_ge(turned, 3 * i - 3 + n + 1)
                        act.wait_ge(tok_free, i)
                        nc.scalar.copy(tok[:, n, :, :], ps_t[:, :, :]).then_inc(tok_ready, 1)

                def body(i, first):
                    if first:
                        act.wait_ge(inner_mixed, 1)
                    else:
                        act.wait_ge(k_mixed, i)
                    act.wait_ge(k_proj, i + 1)
                    nc.scalar.copy(raw_k[:, 1:T + 1], flat(ps_a)).then_inc(k_raw, 1)
                    if not first:
                        turn_out(i)
                    if first:
                        act.wait_ge(inner_mixed, 2)
                    else:
                        act.wait_ge(v_mixed, i)
                    act.wait_ge(v_proj, i + 1)
                    nc.scalar.copy(raw_v[:, 1:T + 1], flat(ps_b)).then_inc(v_raw, 1)
                    act.wait_ge(lora_w, i + 1)
                    if not first:
                        act.wait_ge(ch_ready, i)
                    nc.scalar.activation(sg[:, :], flat(ps_x), ACT.Sigmoid, bias=col(k, "w0", i)).then_inc(sg_ready, 1)
                    act.wait_ge(lora_a, i + 1)
                    nc.scalar.activation(rate[:, :], flat(ps_x), ACT.Sigmoid, bias=col(k, "a0", i)).then_inc(rate_ready, 1)
                    act.wait_ge(kk_ready, i + 1)
                    if not first:
                        act.wait_ge(norm_sum, i)
                    nc.scalar.activation(sq[:, :], kk[:, :], ACT.Square).then_inc(sq_ready, 1)
                    act.wait_ge(norm_floored, i + 1)
                    nc.scalar.activation(norm[:, :], norm[:, :], ACT.Sqrt).then_inc(norm_ready, 1)
                    if not first:
                        act.wait_ge(r_mixed, i)
                    act.wait_ge(r_proj, i + 1)
                    nc.scalar.copy(raw_r[:, 1:T + 1], flat(ps_a)).then_inc(r_raw, 1)
                    act.wait_ge(cc_ready, i + 1)
                    nc.scalar.activation(e_pos[:, :], cc[:, :], ACT.Exp, scale=-KAPPA).then_inc(exps_ready, 1)
                    act.wait_ge(exps_ready, 4 * i + 1)
                    nc.scalar.activation(e_neg[:, :], cc[:, :], ACT.Exp, scale=KAPPA).then_inc(exps_ready, 1)
                    nc.scalar.activation(e_ex[:, :], cx[:, :], ACT.Exp, scale=-KAPPA).then_inc(exps_ready, 1)
                    nc.scalar.activation(k.decays[:, bass.ds(i, 1), :].rearrange("p a c -> p (a c)"), span[:, :],
                                         ACT.Exp, scale=-KAPPA).then_inc(exps_ready, 1)

                rounds(act, body)
                turn_out(RT)

            @block.vector
            def _(dve):
                then = Chain(dve, dve_last)
                for raw in (raw_k, raw_v, raw_r):
                    nc.vector.memset(raw[:, 0:1], 0.0).then_inc(pads, 1)
                then(nc.vector.tensor_scalar(ka1[:, :], k.cols[:, COLS["k_a"]:COLS["k_a"] + RT], -1.0, 1.0, ALU.mult,
                                             ALU.add))
                dve.wait_ge(pads, 3)

                def mix(out, raw, mu_tile, sem, link):
                    link(nc.vector.tensor_tensor(diff[:, :], raw[:, 0:T], raw[:, 1:T + 1], ALU.subtract))
                    return nc.vector.scalar_tensor_tensor(out[:, :], diff[:, :], col(k, "mu", mu_tile), raw[:, 1:T + 1],
                                                          ALU.mult, ALU.add).then_inc(sem, 1)

                dve.wait_ge(inner_raw, 1)
                mix(kx, raw_k, T_WA, inner_mixed, then)
                dve.wait_ge(inner_raw, 2)
                dve.wait_ge(inner_mixed, 1)
                mix(vx, raw_v, T_G, inner_mixed, then)
                dve.wait_ge(inner_done, 3)
                start = then.n
                chunks = lambda t: t[:, :].rearrange("p (c t) -> p c t", t=P)

                def body(i, first):
                    link = Chain(dve, dve_last, 14)
                    link.base = i * 14 + start
                    if not first:
                        finish(i)
                    dve.wait_ge(k_raw, i + 1)
                    mix(kx, raw_k, i + T_K, k_mixed, link)
                    dve.wait_ge(k_mixed, i + 1)
                    nc.vector.tensor_scalar(kk[:, :], kx[:, :], col(k, "k_k", i), None, ALU.mult).then_inc(kk_ready, 1)
                    dve.wait_ge(sg_ready, i + 1)
                    link(nc.vector.tensor_tensor_scan(cum[:, :], mat(k, "reset", T), sg[:, :], 0.0, ALU.mult, ALU.add))
                    link(nc.vector.tensor_tensor(chunks(cc), chunks(cum),
                                                 chunks(cum)[:, :, P // 2 - 1:P // 2].to_broadcast([P, NT, P]),
                                                 ALU.subtract))
                    link(nc.vector.tensor_tensor(cx[:, :], cc[:, :], sg[:, :], ALU.subtract))
                    link(nc.vector.tensor_copy(span[:, :], chunks(cc)[:, :, P - 1]))
                    nc.vector.tensor_tensor(span[:, 0:NT - 1], span[:, 0:NT - 1], chunks(cum)[:, 1:NT, P // 2 - 1],
                                            ALU.add).then_inc(cc_ready, 1)
                    dve.wait_ge(norm_sum, i + 1)
                    nc.vector.tensor_scalar(norm[:, :], ps_x[:, :, :].rearrange("p a b -> p (a b)"), 1e-24, None,
                                            ALU.max).then_inc(norm_floored, 1)
                    dve.wait_ge(norm_ready, i + 1)
                    link(nc.vector.reciprocal(norm[:, :], norm[:, :]))
                    dve.wait_ge(kk_ready, i + 1)
                    link(nc.vector.tensor_tensor(kk[:, :], kk[:, :], norm[:, :], ALU.mult))
                    dve.wait_ge(rate_ready, i + 1)
                    link(nc.vector.tensor_scalar(k2[:, :], rate[:, :], col(k, "k_a", i), ka1[:, bass.ds(i, 1)], ALU.mult,
                                                 ALU.add))
                    link(nc.vector.tensor_tensor(k2[:, :], k2[:, :], kx[:, :], ALU.mult))
                    link(nc.vector.tensor_tensor(b[:, :], kk[:, :], rate[:, :], ALU.mult))
                    dve.wait_ge(r_raw, i + 1)
                    mix(rx, raw_r, i + T_R, r_mixed, link)
                    dve.wait_ge(r_mixed, i + 1)
                    if not first:
                        dve.wait_ge(bonus_sum, i)
                    nc.vector.scalar_tensor_tensor(rkk[:, :], rx[:, :], col(k, "r_k", i), k2[:, :], ALU.mult,
                                                   ALU.mult).then_inc(rkk_ready, 1)
                    dve.wait_ge(exps_ready, 4 * i + 4)
                    if not first:
                        dve.wait_ge(ch_out, 16 * i)
                        dve.wait_ge(turned, 3 * i)
                    link(nc.vector.scalar_tensor_tensor(ch[:, :, 0, :], chunks(kk), -1.0, chunks(e_ex), ALU.mult, ALU.mult))
                    nc.vector.tensor_tensor(ch[:, :, 1, :], chunks(rx), chunks(e_pos), ALU.mult)
                    nc.vector.tensor_tensor(ch[:, :, 2, :], chunks(b), chunks(e_neg), ALU.mult)
                    link(nc.vector.tensor_tensor(ch[:, :, 3, :], chunks(k2), chunks(e_neg), ALU.mult))
                    dve.sem_inc(ch_ready, 1)
                    dve.wait_ge(v_raw, i + 1)
                    mix(vx, raw_v, i + T_V, v_mixed, link)
                    link.done()

                def finish(i):
                    dve.wait_ge(bonus_sum, i)
                    dve.wait_ge(v_mixed, i)
                    nc.vector.tensor_tensor(k.bonus[:, bass.ds(i - 1, 1), :].rearrange("p a t -> p (a t)"),
                                            ps_x[:, :, :].rearrange("p a b -> p (a b)"), vx[:, :],
                                            ALU.mult).then_inc(bonus_ready, 1)

                rounds(dve, body)
                finish(RT)
                dve.wait_ge(bonus_ready, RT)


LEVELS = 6


def rwkv_chunks(nc, k):
    G = 2
    HG = RH // G
    with Space(nc, "rc") as s:
        ar = [k.slab[:, 2 * b:2 + 2 * b, :].rearrange("p a t -> p (a t)").rearrange("p (r n t) -> p r n t", r=RT, n=2)
              for b in range(2)]
        bk = [k.slab[:, 4 + b, :].rearrange("p (r n t) -> p r n t", r=RT, n=2) for b in range(2)]
        tok = [s.sb(f"tok{b}", [P, 3, RT * P]) for b in range(2)]
        ab = [s.sb(f"ab{b}", [P, RH, 2 * P]) for b in range(2)]
        ak = [s.sb(f"ak{b}", [P, RH, 2 * P]) for b in range(2)]
        low = [s.sb(f"low{g}", [P, HG, P]) for g in range(G)]
        z = [s.sb(f"z{g}", [P, HG, P]) for g in range(G)]
        x = [s.sb(f"x{g}", [P, HG, P]) for g in range(G)]
        xt = [[s.sb(f"xt{b}{g}", [P, HG, P]) for g in range(G)] for b in range(2)]
        tmp = s.sb("tmp", [P, HG, P])
        p1, u = s.sb("p1", [P, RH, HD]), s.sb("u", [P, RH, HD])
        state = s.sb("state", [P, RT, HD])
        eye = s.sb("eye", [P, HG, P], BF16)
        ps_z, ps_x, ps_xt = ([s.ps(f"{n}{g}", [P, HALF]) for g in range(G)] for n in ("z", "x", "xt"))
        ps_p, ps_y = s.ps("p", [P, HALF]), s.ps("y", [P, HALF])
        loaded = [s.sem(f"loaded{b}") for b in range(2)]
        (prod_b, prod_k, prod_l, z_done, x_done, xt_done, b_masked, k_masked, l_masked, z_masked, x0_ready, x_copied,
         xt_copied) = ([s.sem(f"{n}{g}") for g in range(G)] for n in (
             "prod_b", "prod_k", "prod_l", "z_done", "x_done", "xt_done", "b_masked", "k_masked", "l_masked", "z_masked",
             "x0_ready", "x_copied", "xt_copied"))
        p_done, u_done, y_done, s_done, p_copied, u_copied, y_copied, s_scaled, ready, pool_last = (s.sem(n) for n in (
            "p_done", "u_done", "y_done", "s_done", "p_copied", "u_copied", "y_copied", "s_scaled", "ready", "pool_last"))
        zeroed = s.sem("zeroed")
        x_one = [s.sem(f"x_one{g}") for g in range(G)]
        XL, ZL = LEVELS - 1, LEVELS

        def heads(g):
            return range(g * HG, (g + 1) * HG)

        def four(ps):
            return ps[:, :].rearrange("p (h t) -> p h t", h=HG)

        def steps(eng, step):
            step((0, 0, True), None)
            step((1, 1, True), (0, 0, True))
            with eng.Fori(1, NT // 2) as i:
                for b in range(2):
                    step((2 * i + b, b, False), (2 * i + b - 1, 1 - b, False))
            step(None, (NT - 1, 1, False))

        with s.block() as block:
            @block.sync
            def _(sp):
                sp.wait_ge(zeroed, 2)

                def step(front, back):
                    if front is None:
                        return
                    c, b, early = front
                    if not early:
                        sp.wait_ge(s_done, c - 1)
                        sp.wait_ge(y_done, c - 1)
                    src = k.chunk_ch[bass.ds(c, 1)].rearrange("o p r a t -> (o p) r (a t)")
                    for n in range(2):
                        q = slice(n * HD, n * HD + HD)
                        sp.dma_start(ar[b][q, :, n, :], src[q, :, 0:2 * P]).then_inc(loaded[b], 16)
                    sp.dma_start(bk[b][:, :, :, :].rearrange("p r a t -> p r (a t)"), src[:, :, 2 * P:]
                                 ).then_inc(loaded[b], 16)
                    for n in range(3):
                        sp.dma_start(tok[b][:, n, :], k.chunk_tok[n, bass.ds(c, 1)].rearrange("o p r t -> (o p) (r t)")
                                     ).then_inc(loaded[b], 16)

                steps(sp, step)

            @block.tensor
            def _(pe):
                mm = nc.tensor.matmul
                pe.wait_ge(ready, 2)

                def products(front):
                    c, b, early = front
                    pe.wait_ge(loaded[b], (c - b) * 48 + 96)
                    for g in range(G):
                        if not isinstance(c, int) or c > 0:
                            pe.wait_ge(xt_copied[g], ZL * c)
                            pe.wait_ge(x_copied[g], XL * c)
                            pe.wait_ge(z_masked[g], ZL * c)
                        for j, h in enumerate(heads(g)):
                            t, o = h // 2, h % 2
                            last = mm(four(ps_xt[g])[:, j, :], ar[b][:, t, o, 0:P], bk[b][:, t, 0, :], start=True, stop=True)
                        last.then_inc(prod_l[g], 1)
                        for n, sem in ((0, prod_b), (1, prod_k)):
                            if n == 1:
                                pe.wait_ge(b_masked[g], c + 1)
                            for j, h in enumerate(heads(g)):
                                t, o = h // 2, h % 2
                                out = (ps_z, ps_x)[j // 2][g][:, (j % 2) * 2 * P:(j % 2 + 1) * 2 * P]
                                last = mm(out, bk[b][:, t, n, :], ar[b][:, t, o, :], start=True, stop=True)
                            last.then_inc(sem[g], 1)

                def level(front, n):
                    c, b, early = front
                    for g in range(G):
                        if n == 1:
                            pe.wait_ge(x0_ready[g], c + 1)
                            pe.wait_ge(k_masked[g], c + 1)
                        else:
                            pe.wait_ge(x_copied[g], XL * c + n - 1)
                        mm(ps_z[g][:, :], eye[:, 0, :], eye[:, :, :].rearrange("p h t -> p (h t)"), start=True, stop=False,
                           skip_group_check=True)
                        for j, h in enumerate(heads(g)):
                            last = mm(four(ps_z[g])[:, j, :], ab[b][:, h, 0:P], x[g][:, j, :], start=False,
                                      stop=(j == HG - 1), skip_group_check=True)
                        last.then_inc(z_done[g], 1)
                    for g in range(G):
                        pe.wait_ge(z_masked[g], ZL * c + n)
                        if n > 1:
                            pe.wait_ge(xt_copied[g], ZL * c + n - 1)
                        if n < LEVELS:
                            for j in range(HG):
                                last = mm(four(ps_x[g])[:, j, :], xt[b][g][:, j, :], z[g][:, j, :], start=True, stop=True)
                            last.then_inc(x_done[g], 1)
                        if n == 1:
                            pe.wait_ge(l_masked[g], c + 1)
                        for j in range(HG):
                            last = mm(four(ps_xt[g])[:, j, :], z[g][:, j, :], xt[b][g][:, j, :], start=True, stop=True)
                        last.then_inc(xt_done[g], 1)

                def through(back, n):
                    c, b, first = back
                    for h in range(RH) if n < 5 else ():
                        t, o = h // 2, h % 2
                        q, cols = slice(o * HD, o * HD + HD), slice(h * HD, h * HD + HD)
                        g, j = h // HG, h % HG
                        v, bt, kt = (tok[b][:, a, cols] for a in range(3))
                        if n == 1:
                            if h == 0 and not first:
                                pe.wait_ge(s_scaled, c)
                            mm(ps_p[:, cols], ar[b][:, t, o, 0:P], state[:, t, :], start=True, stop=False)
                            last = mm(ps_p[:, cols], ak[b][:, h, 0:P], v, start=False, stop=True)
                        elif n == 2:
                            if h == 0:
                                pe.wait_ge(p_copied, c + 1)
                                if not first:
                                    pe.wait_ge(y_copied, c)
                            if j == 0:
                                pe.wait_ge(xt_copied[g], ZL * c + ZL)
                            last = mm(ps_y[:, cols], xt[b][g][:, j, :], p1[:, h, :], start=True, stop=True)
                        elif n == 3:
                            if h == 0:
                                pe.wait_ge(u_copied, c + 1)
                            out = ps_y[q, t * P:(t + 1) * P]
                            mm(out, state[:, t, :], ar[b][:, t, o, P:2 * P], start=True, stop=False)
                            mm(out, u[:, h, :], ab[b][:, h, P:2 * P], start=False, stop=False)
                            last = mm(out, v, ak[b][:, h, P:2 * P], start=False, stop=True)
                        elif n == 4:
                            out = ps_p[q, t * HD:(t + 1) * HD]
                            mm(out, mat(k, "ident")[:, q], state[:, t, :], start=True, stop=False)
                            mm(out, bt, u[:, h, :], start=False, stop=False)
                            last = mm(out, kt, v, start=False, stop=True)
                    if n < 5:
                        last.then_inc((p_done, u_done, y_done, s_done)[n - 1], 1)

                def step(front, back):
                    if front is not None:
                        products(front)
                    for n in range(1, LEVELS + 1):
                        if front is not None:
                            level(front, n)
                        if back is not None:
                            through(back, n)

                steps(pe, step)

            @block.vector
            def _(dve):
                tt = nc.vector.tensor_tensor
                nc.vector.tensor_copy(eye[:, :, :], mat(k, "ident").unsqueeze(1).to_broadcast([P, HG, P])
                                      ).then_inc(ready, 1)
                nc.vector.memset(state[:, :, :], 0.0).then_inc(ready, 1)
                masks = mat(k, "before", 2 * P).unsqueeze(1).to_broadcast([P, 2, 2 * P])

                def level_mask(n):
                    return mat(k, "levels", P, n * P).unsqueeze(1).to_broadcast([P, HG, P])

                def step(front, back):
                    if front is not None:
                        c, b, early = front
                        if not early:
                            dve.wait_ge(s_done, c - 1)
                            dve.wait_ge(y_done, c - 1)
                        for g in range(G):
                            dve.wait_ge(prod_l[g], c + 1)
                            if not isinstance(c, int) or c > 0:
                                dve.wait_ge(x0_ready[g], c)
                            tt(low[g][:, :, :], four(ps_xt[g]), mat(k, "after").unsqueeze(1).to_broadcast([P, HG, P]),
                               ALU.mult).then_inc(l_masked[g], 1)
                            for sem, done, out in ((prod_b, b_masked, ab), (prod_k, k_masked, ak)):
                                dve.wait_ge(sem[g], c + 1)
                                for n, ps in enumerate((ps_z, ps_x)):
                                    h = g * HG + 2 * n
                                    last = tt(out[b][:, h:h + 2, :], ps[g][:, :].rearrange("p (h t) -> p h t", h=2), masks,
                                              ALU.mult)
                                last.then_inc(done[g], 1)
                    for n in range(1, LEVELS + 1):
                        if front is not None:
                            for g in range(G):
                                dve.wait_ge(z_done[g], ZL * c + n)
                                if n == 1 and (not isinstance(c, int) or c > 0):
                                    dve.wait_ge(xt_done[g], ZL * c)
                                if n > 1:
                                    dve.wait_ge(xt_done[g], ZL * c + n - 1)
                                tt(z[g][:, :, :], four(ps_z[g]), level_mask(n), ALU.mult).then_inc(z_masked[g], 1)
                        if back is not None and n == 4:
                            bc = back[0]
                            dve.wait_ge(s_done, bc + 1)
                            dve.wait_ge(y_done, bc + 1)
                            tt(state[:, :, :], ps_p[:, 0:RT * HD].rearrange("p (t d) -> p t d", d=HD),
                               k.decays[:, :, bass.ds(bc, 1)].to_broadcast([P, RT, HD]), ALU.mult).then_inc(s_scaled, 1)

                steps(dve, step)

            @block.gpsimd
            def _(pool):
                tt = nc.gpsimd.tensor_tensor
                for b in range(2):
                    nc.gpsimd.memset(ar[b][:, :, :, :], 0.0).then_inc(zeroed, 1)
                eye4 = mat(k, "ident").unsqueeze(1).to_broadcast([P, HG, P])

                def step(front, back):
                    if front is None:
                        return
                    c, b, early = front
                    if not early:
                        pool.wait_ge(u_done, c - 1)
                    link = Chain(pool, pool_last, 2 * G)
                    link.base = c * 2 * G
                    for g in range(G):
                        pool.wait_ge(l_masked[g], c + 1)
                        pool.wait_ge(b_masked[g], c + 1)
                        if not isinstance(c, int) or c > 0:
                            pool.wait_ge(z_done[g], ZL * c)
                            pool.wait_ge(x_copied[g], XL * c)
                        for src, name, out in ((low[g][:, :, :], "levels", x[g]),
                                               (ab[b][:, g * HG:(g + 1) * HG, 0:P], "level0_t", xt[b][g])):
                            link(tt(tmp[:, :, :], src, mat(k, name).unsqueeze(1).to_broadcast([P, HG, P]), ALU.mult))
                            last = tt(out[:, :, :], tmp[:, :, :], eye4, ALU.add)
                            if name == "levels":
                                last.then_inc(x_one[g], 1)
                                pool.wait_ge(x_one[g], c + 1)
                        last.then_inc(x0_ready[g], 1)
                        pool.wait_ge(x0_ready[g], c + 1)

                steps(pool, step)

            @block.scalar
            def _(act):
                def step(front, back):
                    for n in range(1, LEVELS + 1):
                        if front is not None:
                            c, b, early = front
                            for g in range(G):
                                if n < LEVELS:
                                    act.wait_ge(x_done[g], XL * c + n)
                                    nc.scalar.copy(x[g][:, :, :], four(ps_x[g])).then_inc(x_copied[g], 1)
                                act.wait_ge(xt_done[g], ZL * c + n)
                                nc.scalar.copy(xt[b][g][:, :, :], four(ps_xt[g])).then_inc(xt_copied[g], 1)
                        if back is not None:
                            bc = back[0]
                            if n == 1:
                                act.wait_ge(p_done, bc + 1)
                                nc.scalar.copy(p1[:, :, :].rearrange("p h d -> p (h d)"), ps_p[:, :]).then_inc(p_copied, 1)
                            elif n == 2:
                                act.wait_ge(u_done, bc + 1)
                                nc.scalar.copy(u[:, :, :].rearrange("p h d -> p (h d)"), ps_y[:, :]).then_inc(u_copied, 1)
                            elif n == 3:
                                act.wait_ge(y_done, bc + 1)
                                nc.scalar.copy(k.rwkv_oT[:, :, bass.ts(bc, P)],
                                               ps_y[:, :].rearrange("p (r t) -> p r t", r=RT)).then_inc(y_copied, 1)

                steps(act, step)


def rwkv_outputs(nc, k):
    with Space(nc, "ro") as s:
        g_up = [s.sb(f"g_up{b}", [P, P]) for b in range(2)]
        yc, sq, sd = ([s.sb(f"{n}{b}", [P, T]) for b in range(2)] for n in ("yc", "sq", "sd"))
        yn = s.sb("yn", [P, T])
        eps = s.sb("eps", [P, 1])
        ps_m = [s.ps(f"m{b}", [P, 2, HALF]) for b in range(2)]
        ps_v, ps_g = (s.ps(n, [P, 2, HALF]) for n in "vg")
        x_full = [s.sb(f"x_full{b}", [P, T]) for b in range(2)]
        x_in = [s.sem(f"x_in{b}") for b in range(2)]
        rounded, x_split, stood = s.sem("rounded"), s.sem("x_split"), s.sem("stood")
        up_loaded = [s.sem(f"up_loaded{b}") for b in range(2)]
        summed, centered, sq_ready, squares_summed, gate_done, eps_set, sd_ready, gated, last = (s.sem(n) for n in (
            "summed", "centered", "sq_ready", "squares_summed", "gate_done", "eps_set", "sd_ready", "gated", "last"))

        def flat(ps):
            return ps[:, :, :].rearrange("p a b -> p (a b)")

        def tile_of(t, i):
            return t[:, bass.ds(i, 1), :].rearrange("p a t -> p (a t)")

        def both(out, lhs, rhs):
            for h in range(2):
                m = nc.tensor.matmul(out[:, h, :], lhs, rhs[:, h * HALF:(h + 1) * HALF], start=True, stop=True)
            return m

        with s.block() as block:
            @block.sync
            def _(sp):
                for i in range(RT):
                    if i >= 2:
                        sp.wait_ge(gate_done, i - 1)
                    sp.dma_start(g_up[i % 2][:, :], k.rwkv_g_up[:, i * P:(i + 1) * P]).then_inc(up_loaded[i % 2], 16)

            @block.tensor
            def _(pe):
                def means(i):
                    if i >= 2:
                        pe.wait_ge(centered, i - 1)
                    both(ps_m[i % 2], mat(k, "head_ones"), k.rwkv_oT[:, i, :]).then_inc(summed, 1)

                means(0)
                for i in range(RT):
                    if i + 1 < RT:
                        means(i + 1)
                    pe.wait_ge(sq_ready, i + 1)
                    if i >= 1:
                        pe.wait_ge(sd_ready, i)
                    both(ps_v, mat(k, "head_ones"), sq[i % 2]).then_inc(squares_summed, 1)
                    pe.wait_ge(up_loaded[i % 2], 16 * (i // 2) + 16)
                    if i >= 1:
                        pe.wait_ge(gated, i)
                    both(ps_g, g_up[i % 2][:, :], k.gate_in).then_inc(gate_done, 1)

            @block.scalar
            def _(act):
                act.wait_ge(eps_set, 1)
                for i in range(RT):
                    act.wait_ge(centered, i + 1)
                    if i >= 2:
                        act.wait_ge(squares_summed, i - 1)
                    nc.scalar.activation(sq[i % 2][:, :], yc[i % 2][:, :], ACT.Square).then_inc(sq_ready, 1)
                    act.wait_ge(squares_summed, i + 1)
                    if i >= 2:
                        act.wait_ge(gated, i - 1)
                    nc.scalar.activation(sd[i % 2][:, :], flat(ps_v), ACT.Sqrt, bias=eps[:, :], scale=1.0 / HD
                                         ).then_inc(sd_ready, 1)

            @block.gpsimd
            def _(pool):
                with pool.Fori(0, KD // 2) as i:
                    for b in range(2):
                        pool.dma_start(x_full[b][:, :], k.xT_d[bass.ds(2 * i + b, 1)].rearrange("a p t -> (a p) t")
                                       ).then_inc(x_in[b], 16)
                    for b in range(2):
                        t = 2 * i + b
                        pool.wait_ge(x_in[b], 16 * i + 16)
                        split(pool, tile_of(k.x_high, t), tile_of(k.x_low, t), x_full[b][:, :], rounded, t + 1, x_split, stood)
                        pool.wait_ge(x_split, t + 1)
                        pool.sem_inc(stood, 1)
                pool.wait_ge(x_split, KD)

            @block.vector
            def _(dve):
                nc.vector.memset(eps[:, :], RWKV_EPS).then_inc(eps_set, 1)
                link = Chain(dve, last)

                def center(i):
                    dve.wait_ge(summed, i + 1)
                    if i >= 2:
                        dve.wait_ge(sq_ready, i - 1)
                    nc.vector.scalar_tensor_tensor(yc[i % 2][:, :], flat(ps_m[i % 2]), -1.0 / HD, k.rwkv_oT[:, i, :],
                                                   ALU.mult, ALU.add).then_inc(centered, 1)

                center(0)
                for i in range(RT):
                    if i + 1 < RT:
                        center(i + 1)
                    y, inv = yc[i % 2][:, :], sd[i % 2][:, :]
                    dve.wait_ge(sd_ready, i + 1)
                    link(nc.vector.reciprocal(inv, inv))
                    dve.wait_ge(centered, i + 1)
                    link(nc.vector.tensor_tensor(yn[:, :], y, inv, ALU.mult))
                    link(nc.vector.tensor_scalar(yn[:, :], yn[:, :], col(k, "gn_g", i), col(k, "gn_b", i), ALU.mult, ALU.add))
                    link(nc.vector.tensor_tensor(yn[:, :], yn[:, :], k.bonus[:, i, :], ALU.add))
                    dve.wait_ge(gate_done, i + 1)
                    nc.vector.tensor_tensor(k.rwkv_oT[:, i, :], yn[:, :], flat(ps_g), ALU.mult).then_inc(gated, 1)
                    dve.wait_ge(gated, i + 1)


SMALL = 48


def fox_project(nc, k):
    with Space(nc, "fp") as s:
        w_v = k.mixer_oT.rearrange("p a (b c) -> p (a b) c", c=HALF)
        high_v, low_v = s.sb("high_v", [P, KD, HALF], F32R), s.sb("low_v", [P, KD, HALF], F32R)
        w_small = s.sb("w_small", [P, KD, SMALL])
        high_small, low_small = (s.sb(f"{n}_small", [P, KD, SMALL], F32R) for n in ("high", "low"))
        qk = [k.room[:, 4 + b, :] for b in range(2)]
        raw, ab, ln, c = (k.room[0:FH, 6 + n, :] for n in range(4))
        one, dt_raw = s.sb("one", [FH, T]), s.sb("dt_raw", [SH, T])
        neg_c = ab
        bias = s.sb("bias", [FH, 1])
        qk_d = k.fox_qk.rearrange("(t two) d s -> t (two d) s", two=2)
        ps = [s.ps(f"t{b}", [P, 2, HALF]) for b in range(2)]
        ps_v = [s.ps(f"v{b}", [P, HALF]) for b in range(2)]
        ps_s = s.ps("s", [SMALL, 2, HALF])
        stored = [s.sem(f"stored{b}") for b in range(2)]
        rounded, v_ready, small_ready, dt_stored, stood = (s.sem(n) for n in (
            "rounded", "v_ready", "small_ready", "dt_stored", "stood"))
        x = (k.x_high, k.x_low)
        (v_loaded, small_loaded, bias_in, projected, small_done, v_done, copied, v_copied, dt_copied, raw_done, abs_done,
         log_done, last, c_ready, c_stored) = (s.sem(n) for n in (
             "v_loaded", "small_loaded", "bias_in", "projected", "small_done", "v_done", "copied", "v_copied", "dt_copied",
             "raw_done", "abs_done", "log_done", "last", "c_ready", "c_stored"))
        w = SplitWeights(s, projected)
        pairs = FH * HD * 2 // P // 2

        with s.block() as block:
            @block.sync
            def _(sp):
                sp.dma_start(w_small[:, :, :], k.w_small).then_inc(small_loaded, 16)
                sp.dma_start(bias[:, :], k.f_bias).then_inc(bias_in, 16)
                for b in range(2):
                    sp.sem_inc(stored[b], 16)

                def store(t, b):
                    sp.wait_ge(copied, t + 3)
                    sp.dma_start(qk_d[bass.ds(t, 1)].rearrange("a p s -> (a p) s"), qk[b][:, :]).then_inc(stored[b], 16)

                w.start(sp)
                w.load(sp, k, 0, T_FQ)
                w.load(sp, k, 1, 1 + T_FQ)
                sp.dma_start(w_v[:, :, :], k.w_fox_v).then_inc(v_loaded, 16)
                with sp.Fori(0, pairs - 1) as i:
                    for b in range(2):
                        w.load(sp, k, 2 * i + b + 2, 2 * i + b + 2 + T_FQ)
                        store(2 * i + b, b)
                for b in range(2):
                    store(2 * pairs - 2 + b, b)
                for b in range(2):
                    sp.wait_ge(stored[b], 16 + 16 * pairs)
                sp.wait_ge(dt_copied, 1)
                sp.dma_start(k.dt_d, dt_raw[:, :]).then_inc(dt_stored, 16)
                sp.wait_ge(dt_stored, 16)
                sp.wait_ge(c_ready, 2)
                sp.dma_start(k.fox_c[0], c[:, :]).then_inc(c_stored, 16)
                sp.dma_start(k.fox_c[1], neg_c[:, :]).then_inc(c_stored, 16)
                sp.wait_ge(c_stored, 32)

            @block.tensor
            def _(pe):
                pe.sem_inc(projected, 2)
                pe.wait_ge(small_ready, 1)
                project_parts(nc, ps_s, (high_small, low_small), x).then_inc(small_done, 1)
                with pe.Fori(0, pairs) as i:
                    for b in range(2):
                        pe.wait_ge(copied, 2 * i + b + 1)
                        w.project(nc, k, ps[b], 2 * i + b, b).then_inc(projected, 1)
                pe.wait_ge(v_ready, 1)
                for n in range(NT):
                    if n >= 2:
                        pe.wait_ge(v_copied, n - 1)
                    for d in range(KD):
                        m = times(nc, ps_v[n % 2][:, :], [t[:, d, n * P:(n + 1) * P] for t in x],
                                  (high_v[:, d, :], low_v[:, d, :]), d == 0, d == KD - 1)
                    m.then_inc(v_done, 1)

            @block.scalar
            def _(act):
                act.sem_inc(copied, 2)
                act.wait_ge(raw_done, 1)
                nc.scalar.activation(ln[:, :], ab[:, :], ACT.Exp).then_inc(log_done, 1)
                act.wait_ge(log_done, 1)
                nc.scalar.activation(ln[:, :], ln[:, :], ACT.Ln, bias=1.0).then_inc(log_done, 1)
                for part, scale in ((0, HD ** -0.5), (1, 1.0)):
                    with act.Fori(part * pairs // 2, (part + 1) * pairs // 2) as i:
                        for b in range(2):
                            act.wait_ge(projected, 2 * i + b + 3)
                            act.wait_ge(stored[b], 16 * i + 16)
                            nc.scalar.activation(qk[b][:, :], ps[b][:, :, :].rearrange("p a b -> p (a b)"), ACT.Copy,
                                                 scale=scale).then_inc(copied, 1)
                for n in range(NT):
                    act.wait_ge(v_done, n + 1)
                    nc.scalar.copy(k.fox_v[:, n, :], ps_v[n % 2][:, :]).then_inc(v_copied, 1)

            @block.gpsimd
            def _(pool):
                pool.wait_ge(small_loaded, 16)
                split(pool, high_small[:, :, :], low_small[:, :, :], w_small[:, :, :], rounded, 1, small_ready, stood)
                w.cut(pool, 0, 0)
                w.cut(pool, 1, 1)
                pool.wait_ge(v_loaded, 16)
                split(pool, high_v[:, :, :], low_v[:, :, :], w_v, rounded, 2, v_ready, stood)
                with pool.Fori(1, pairs) as i:
                    for b in range(2):
                        w.cut(pool, 2 * i + b, b)

            @block.vector
            def _(dve):
                link = Chain(dve, last)
                link(nc.vector.memset(one[:, :], 1.0))
                dve.wait_ge(bias_in, 16)
                dve.wait_ge(small_done, 1)
                nc.vector.tensor_copy(dt_raw[:, :], ps_s[32:32 + SH, :, :].rearrange("p a b -> p (a b)")
                                      ).then_inc(dt_copied, 1)
                link(nc.vector.tensor_scalar(raw[:, :], ps_s[0:FH, :, :].rearrange("p a b -> p (a b)"), bias[:, :], None,
                                             ALU.add))
                link(nc.vector.tensor_scalar(ab[:, :], raw[:, :], -1.0, None, ALU.mult))
                nc.vector.tensor_tensor(ab[:, :], ab[:, :], raw[:, :], ALU.min).then_inc(raw_done, 1)
                dve.wait_ge(log_done, 2)
                link(nc.vector.tensor_scalar(raw[:, :], raw[:, :], 0.0, None, ALU.min))
                link(nc.vector.tensor_tensor(raw[:, :], raw[:, :], ln[:, :], ALU.subtract))
                nc.vector.tensor_tensor_scan(c[:, :], one[:, :], raw[:, :], 0.0, ALU.mult, ALU.add).then_inc(c_ready, 1)
                dve.wait_ge(c_ready, 1)
                nc.vector.tensor_scalar(neg_c[:, :], c[:, :], -1.0, None, ALU.mult).then_inc(c_ready, 1)
                dve.wait_ge(dt_copied, 1)


def fox_attend(nc, k):
    with Space(nc, "fa") as s:
        qh = [s.sb(f"q{b}", [HD + 2, T]) for b in range(2)]
        kh = [s.sb(f"k{b}", [HD + 2, T]) for b in range(2)]
        eye, far = s.sb("eye", [P, P], BF16), s.sb("far", [P, P], BF16)
        p = [s.sb(f"p{b}", [P, T]) for b in range(2)]
        pt = [s.sb(f"pt{b}", [P, NT, P]) for b in range(2)]
        neg_max, total, inv = ([s.sb(f"{n}{b}", [P, 1]) for b in range(2)] for n in ("neg_max", "total", "inv"))
        o = k.room[:, 4:8, :].rearrange("p a (b c) -> p (a b) c", c=FH * HD)
        ps_s = [s.ps(f"s{b}", [P, T]) for b in range(2)]
        ps_t = s.ps("t", [P, NT, P])
        ps_o = [s.ps(f"o{b}", [P, HALF]) for b in range(2)]
        loaded = [s.sem(f"loaded{b}") for b in range(2)]
        (consts, scored, max_ready, exp_ready, turned_a, turned_b, a_copied, b_copied, pv_done, inv_ready, o_ready,
         o_turned, o_copied) = (s.sem(n) for n in (
             "consts", "scored", "max_ready", "exp_ready", "turned_a", "turned_b", "a_copied", "b_copied", "pv_done",
             "inv_ready", "o_ready", "o_turned", "o_copied"))

        def units(eng, head):
            head(0, 0)
            head(1, 1)
            with eng.Fori(1, FH // 2 - 1) as r:
                for b in range(2):
                    head(2 * r + b, b)
            head(FH - 2, 0)
            head(FH - 1, 1)

        def before(h, b, i, n):
            return (h, b, i - n) if i >= n else (h - 1, 1 - b, i - n + NT)

        def there(h, i, n):
            return not isinstance(h, int) or NT * h + i >= n

        with s.block() as block:
            @block.sync
            def _(sp):
                sp.wait_ge(consts, 6)
                def load(h, b):
                    sp.dma_start(qh[b][0:HD, :], k.fox_qk[bass.ds(h, 1)].rearrange("o d s -> (o d) s")).then_inc(loaded[b], 16)
                    sp.dma_start(kh[b][0:HD, :], k.fox_qk[bass.ds(h + FH, 1)].rearrange("o d s -> (o d) s")
                                 ).then_inc(loaded[b], 16)
                    sp.dma_start(qh[b][HD:HD + 1, :], k.fox_c[0, bass.ds(h, 1)]).then_inc(loaded[b], 16)
                    sp.dma_start(kh[b][HD + 1:HD + 2, :], k.fox_c[1, bass.ds(h, 1)]).then_inc(loaded[b], 16)

                load(0, 0)
                load(1, 1)
                with sp.Fori(1, FH // 2) as r:
                    for b in range(2):
                        sp.wait_ge(scored, NT * (2 * r + b - 1))
                        load(2 * r + b, b)

            @block.tensor
            def _(pe):
                mm = nc.tensor.matmul
                pe.wait_ge(consts, 6)

                def score(h, b, i):
                    u, q = NT * h + i, i * P
                    if i == 0:
                        pe.wait_ge(loaded[b], (h - b) * 32 + 64)
                    pe.wait_ge(exp_ready, u + 1)
                    n = (i + 1) * P
                    for lo in range(0, n, HALF):
                        hi = min(lo + HALF, n)
                        mm(ps_s[i % 2][:, lo:hi], qh[b][:, q:q + P], kh[b][:, lo:hi], start=True, stop=(hi < n),
                           skip_group_check=True)
                    mm(ps_s[i % 2][:, q:q + P], eye[:, :], far[:, :], start=False, stop=True,
                       skip_group_check=True).then_inc(scored, 1)

                def turn(h, b, i):
                    u = NT * h + i
                    pe.wait_ge(exp_ready, u + 3)
                    pe.wait_ge(a_copied, u + 1)
                    for j in range(min(i + 1, 4)):
                        m = nc.tensor.transpose(ps_t[:, j, :], p[i % 2][:, j * P:(j + 1) * P], mat(k, "ident"))
                    m.then_inc(turned_a, 1)
                    if i >= 4:
                        pe.wait_ge(b_copied, 4 * h + i - 4 + 1)
                        for j in range(4, i + 1):
                            m = nc.tensor.transpose(ps_t[:, j, :], p[i % 2][:, j * P:(j + 1) * P], mat(k, "ident"))
                        m.then_inc(turned_b, 1)

                def times_v(h, b, i):
                    u = NT * h + i
                    pe.wait_ge(o_ready, u + 1)
                    pe.wait_ge(a_copied, u + 2)
                    if i >= 4:
                        pe.wait_ge(b_copied, 4 * h + i - 4 + 2)
                    for j in range(i + 1):
                        m = mm(ps_o[i % 2][:, 0:HD], pt[i % 2][:, j, :], k.fox_v[:, j, bass.ts(h, HD)],
                               start=(j == 0), stop=(j == i))
                    m.then_inc(pv_done, 1)

                def head(h, b):
                    for i in range(NT):
                        if i + 1 < NT:
                            score(h, b, i + 1)
                        elif not (isinstance(h, int) and h == FH - 1):
                            score(h + 1, 1 - b, 0)
                        if there(h, i, 1):
                            times_v(*before(h, b, i, 1))
                        turn(h, b, i)

                score(0, 0, 0)
                units(pe, head)
                times_v(FH - 1, 1, NT - 1)
                for i in range(NT):
                    if i == 0:
                        pe.wait_ge(o_ready, NT * FH + 2)
                        pe.wait_ge(a_copied, NT * FH + 1)
                        pe.wait_ge(b_copied, 4 * FH + 1)
                    if i >= 2:
                        pe.wait_ge(o_copied, i - 1)
                    for t in range(4):
                        m = nc.tensor.transpose(ps_t[:, (i % 2) * 4 + t, :], o[:, i, t * P:(t + 1) * P], mat(k, "ident"))
                    m.then_inc(o_turned, 1)

            @block.scalar
            def _(act):
                act.sem_inc(exp_ready, 2)
                act.sem_inc(b_copied, 1)

                def copy_b(h, b, j):
                    if j >= 4:
                        act.wait_ge(turned_b, 4 * h + j - 4 + 1)
                        nc.scalar.copy(pt[j % 2][:, 4:j + 1, :], ps_t[:, 4:j + 1, :]).then_inc(b_copied, 1)

                def head(h, b):
                    for i in range(NT):
                        u, n = NT * h + i, (i + 1) * P
                        act.wait_ge(max_ready, u + 1)
                        if there(h, i, 2):
                            act.wait_ge(turned_a, u - 1)
                            act.wait_ge(inv_ready, u - 1)
                            g, _, j = before(h, b, i, 2)
                            if j >= 4:
                                act.wait_ge(turned_b, 4 * g + j - 4 + 1)
                        nc.scalar.activation(p[i % 2][:, 0:n], ps_s[i % 2][:, 0:n], ACT.Exp, bias=neg_max[i % 2][:, :],
                                             accum_out=total[i % 2][:, :]).then_inc(exp_ready, 1)
                        if there(h, i, 1):
                            copy_b(*before(h, b, i, 1))

                units(act, head)
                copy_b(FH - 1, 1, NT - 1)

            @block.vector
            def _(dve):
                for b in range(2):
                    nc.vector.memset(qh[b][HD:HD + 2, :], 1.0).then_inc(consts, 1)
                    nc.vector.memset(kh[b][HD:HD + 2, :], 1.0).then_inc(consts, 1)
                nc.vector.tensor_copy(eye[:, :], mat(k, "ident")).then_inc(consts, 1)
                nc.vector.tensor_scalar(far[:, :], mat(k, "before"), NEG, None, ALU.mult).then_inc(consts, 1)
                dve.sem_inc(a_copied, 1)
                dve.sem_inc(o_ready, 2)

                def inverse(h, b, j):
                    dve.wait_ge(exp_ready, NT * h + j + 3)
                    nc.vector.reciprocal(inv[j % 2][:, :], total[j % 2][:, :]).then_inc(inv_ready, 1)

                def copy_a(h, b, j):
                    v = NT * h + j
                    dve.wait_ge(turned_a, v + 1)
                    if there(h, j, 2):
                        dve.wait_ge(pv_done, v - 1)
                    m = min(j + 1, 4)
                    nc.vector.tensor_copy(pt[j % 2][:, 0:m, :], ps_t[:, 0:m, :]).then_inc(a_copied, 1)

                def scale_o(h, b, j):
                    v = NT * h + j
                    dve.wait_ge(inv_ready, v + 1)
                    dve.wait_ge(pv_done, v + 1)
                    nc.vector.tensor_scalar(o[:, j, bass.ts(h, HD)], ps_o[j % 2][:, 0:HD], inv[j % 2][:, :], None, ALU.mult
                                            ).then_inc(o_ready, 1)

                def head(h, b):
                    for i in range(NT):
                        u, n = NT * h + i, (i + 1) * P
                        dve.wait_ge(scored, u + 1)
                        if there(h, i, 2):
                            dve.wait_ge(exp_ready, u + 1)
                        nc.vector.tensor_reduce(neg_max[i % 2][:, :], ps_s[i % 2][:, 0:n], AX.X, ALU.max,
                                                negate=True).then_inc(max_ready, 1)
                        if there(h, i, 2):
                            inverse(*before(h, b, i, 2))
                        if there(h, i, 1):
                            copy_a(*before(h, b, i, 1))
                        if there(h, i, 2):
                            scale_o(*before(h, b, i, 2))

                units(dve, head)
                inverse(FH - 1, 1, NT - 2)
                copy_a(FH - 1, 1, NT - 1)
                scale_o(FH - 1, 1, NT - 2)
                inverse(FH - 1, 1, NT - 1)
                scale_o(FH - 1, 1, NT - 1)
                for i in range(NT):
                    dve.wait_ge(o_turned, i + 1)
                    nc.vector.tensor_copy(k.fox_oT[:, :, i * P:(i + 1) * P], ps_t[:, (i % 2) * 4:(i % 2) * 4 + 4, :]
                                          ).then_inc(o_copied, 1)
                dve.wait_ge(o_copied, NT)


def ssm_inputs(nc, k):
    with Space(nc, "si") as s:
        spare = k.mixer_oT.rearrange("p a t -> p (a t)")
        raw = spare[:, 2 * T:3 * T + 8]
        acc = [spare[:, b * T:(b + 1) * T] for b in range(2)]
        out = [s.sb(f"out{b}", [P, T]) for b in range(2)]
        ps = [s.ps(f"t{b}", [P, 2, HALF]) for b in range(2)]
        ps_t = s.ps("turn", [P, NT, P])
        projected, copied, convolved, silu_done, kept, turned, turn_copied = (s.sem(n) for n in (
            "projected", "copied", "convolved", "silu_done", "kept", "turned", "turn_copied"))
        pads, last = s.sem("pads"), s.sem("last")
        w = SplitWeights(s, projected)
        n_turned = NCONV - SG

        def tiles(eng, body):
            with eng.Fori(0, n_turned // 2) as i:
                for b in range(2):
                    body(2 * i + b, b, True)
            for t in range(n_turned, NCONV):
                body(t, t % 2, False)

        with s.block() as block:
            @block.sync
            def _(sp):
                w.start(sp)
                with sp.Fori(0, NCONV) as t:
                    w.load(sp, k, t, t + T_XBC)

            @block.tensor
            def _(pe):
                pe.sem_inc(projected, 2)

                def turn_tile(t, b):
                    pe.wait_ge(silu_done, t + 3)
                    pe.wait_ge(turn_copied, t + 1)
                    for c in range(NT):
                        m = nc.tensor.transpose(ps_t[:, c, :], out[b][:, c * P:(c + 1) * P], mat(k, "ident"))
                    m.then_inc(turned, 1)

                def body(t, b, turn, first=False):
                    pe.wait_ge(copied, t + 1)
                    w.project(nc, k, ps[b], t, b).then_inc(projected, 1)
                    if not first:
                        turn_tile(t - 1, 1 - b)

                body(0, 0, True, True)
                body(1, 1, True)
                with pe.Fori(1, n_turned // 2) as i:
                    for b in range(2):
                        body(2 * i + b, b, True)
                body(n_turned, 0, True)
                pe.wait_ge(copied, NCONV)
                w.project(nc, k, ps[1], NCONV - 1, 1).then_inc(projected, 1)

            @block.scalar
            def _(act):
                act.sem_inc(copied, 2)
                act.sem_inc(silu_done, 2)
                act.sem_inc(turn_copied, 1)
                act.wait_ge(pads, 1)

                def copy_in(t, b):
                    act.wait_ge(projected, t + 3)
                    act.wait_ge(convolved, t + 2)
                    nc.scalar.copy(raw[:, 8:8 + T], ps[b][:, :, :].rearrange("p a b -> p (a b)")).then_inc(copied, 1)

                def body(t, b, turn):
                    copy_in(t, b)
                    act.wait_ge(convolved, t + 3)
                    act.wait_ge(kept, t + 1)
                    if turn:
                        act.wait_ge(turned, t + 1)
                    nc.scalar.activation(out[b][:, :], acc[b][:, :], ACT.Silu).then_inc(silu_done, 1)
                    if turn:
                        act.wait_ge(turned, t + 3)
                        nc.scalar.copy(k.ssm_tok[:, :, bass.ts(t, P)], ps_t[:, :, :]).then_inc(turn_copied, 1)

                act.sem_inc(turned, 2)
                tiles(act, body)

            @block.gpsimd
            def _(pool):
                pool.sem_inc(kept, 2)

                def keep(t, b):
                    pool.wait_ge(silu_done, t + 3)
                    nc.gpsimd.tensor_copy(k.ssm[:, bass.ds(t, 1), :].rearrange("p a t -> p (a t)"), out[b][:, :]
                                          ).then_inc(kept, 1)

                w.cut(pool, 0, 0)
                w.cut(pool, 1, 1)
                with pool.Fori(0, NCONV // 2 - 1) as i:
                    for b in range(2):
                        w.cut(pool, 2 * i + b + 2, b)
                        keep(2 * i + b, b)
                for b in range(2):
                    keep(NCONV - 2 + b, b)
                pool.wait_ge(kept, NCONV + 2)

            @block.vector
            def _(dve):
                dve.sem_inc(convolved, 2)
                nc.vector.memset(raw[:, 0:8], 0.0).then_inc(pads, 1)
                dve.wait_ge(pads, 1)

                def tap(t, n):
                    return k.cols[:, bass.ds(t + (COLS["conv_w"] + n * NCONV), 1)]

                def body(t, b, turn):
                    link = Chain(dve, last)
                    link.base = t * 3
                    dve.wait_ge(copied, t + 3)
                    dve.wait_ge(silu_done, t + 1)
                    a = acc[b][:, :]
                    link(nc.vector.tensor_scalar(a, raw[:, 8:8 + T], tap(t, 3), col(k, "conv_b", t), ALU.mult, ALU.add))
                    for n in (2, 1):
                        link(nc.vector.scalar_tensor_tensor(a, raw[:, 5 + n:5 + n + T], tap(t, n), a, ALU.mult, ALU.add))
                    nc.vector.scalar_tensor_tensor(a, raw[:, 5:5 + T], tap(t, 0), a, ALU.mult, ALU.add
                                                   ).then_inc(convolved, 1)

                tiles(dve, body)


def ssm_scan(nc, k):
    with Space(nc, "sc") as s:
        row = [s.sb(f"row{b}", [SH, P]) for b in range(2)]
        soft, cums = s.sb("soft", [SH, T]), s.sb("cums", [SH, T])
        x0, dt = s.sb("x0", [SH, T]), soft
        bias, a_exp = s.sb("bias", [SH, 1]), s.sb("a_exp", [SH, 1])
        dt_tok, cums_tok = s.sb("dt_tok", [P, NT, SH]), s.sb("cums_tok", [P, NT, SH])
        cb = k.ssm[:, ST:ST + SG, :].rearrange("p g (c t) -> p g c t", t=P)
        lm = [k.mixer_oT[:, b, :].rearrange("p (c t) -> p c t", t=P) for b in range(2)]
        ec = [k.mixer_oT[:, 2 + b, :].rearrange("p (c t) -> p c t", t=P) for b in range(2)]
        end = [s.sb(f"end{b}", [P, NT]) for b in range(2)]
        xs = [s.sb(f"xs{b}", [P, NT, HD]) for b in range(2)]
        xd = [s.sb(f"xd{b}", [P, NT, HD]) for b in range(2)]
        st = [s.sb(f"st{b}", [P, NT, HD]) for b in range(2)]
        ps_s = [s.ps(f"s{b}", [P, 2, HALF]) for b in range(2)]
        ps_y = s.ps("y", [P, NT, P])
        ps_d = [s.ps(f"d{b}", [P, NT, HD]) for b in range(2)]
        row_in = [s.sem(f"row_in{b}") for b in range(2)]
        (consts_in, floored, exps_done, log_done, dt_ready, tok_done, tok_copied, cb_done, cb_masked, zeroed, spread,
         arg_ready, e_ready, l_ready, x_ready, m_ready, c_ready, d_done, st_ready, y_done, y_kept, link_a, link_c,
         link_s) = (s.sem(n) for n in (
             "consts_in", "floored", "exps_done", "log_done", "dt_ready", "tok_done", "tok_copied", "cb_done", "cb_masked",
             "zeroed", "spread", "arg_ready", "e_ready", "l_ready", "x_ready", "m_ready", "c_ready", "d_done", "st_ready",
             "y_done", "y_kept", "link_a", "link_c", "link_s"))
        pairs = SH // 2

        def heads(eng, head):
            head(0, 0, 0)
            head(0, 1, 0)
            for lo, hi, g in ((1, pairs // 2, 0), (pairs // 2, pairs - 1, 1)):
                with eng.Fori(lo, hi) as i:
                    for b in range(2):
                        head(i, b, g)
            head(pairs - 1, 0, 1)
            head(pairs - 1, 1, 1)

        def at_first(i, b):
            return isinstance(i, int) and i == 0 and b == 0

        def at_last(i, b):
            return isinstance(i, int) and i == pairs - 1 and b == 1

        def chunks(t):
            return t.rearrange("p a (c t) -> p (a c) t", t=P)

        with s.block() as block:
            @block.sync
            def _(sp):
                sp.dma_start(bias[:, :], k.dt_bias).then_inc(consts_in, 16)
                sp.dma_start(a_exp[:, :], k.a_log).then_inc(consts_in, 16)
                sp.dma_start(x0[:, :], k.dt_d).then_inc(consts_in, 16)

                def head(i, b, g):
                    sp.wait_ge(spread, 2 * i + b + 1)
                    sp.dma_start(row[b][:, :], k.head_rows_d[:, bass.ds(2 * i + b, 1), :].rearrange("h a p -> h (a p)")
                                 ).then_inc(row_in[b], 16)

                heads(sp, head)

            @block.tensor
            def _(pe):
                mm = nc.tensor.matmul
                for sem in (spread, d_done, y_done):
                    pe.sem_inc(sem, 2)
                for g in range(SG):
                    for c in range(NT):
                        q = slice(c * P, (c + 1) * P)
                        m = mm(chunks(ps_s[g][:, :, :])[:, c, :], k.ssm[:, ST + g, q], k.ssm[:, ST + SG + g, q],
                               start=True, stop=True)
                    m.then_inc(cb_done, 1)
                pe.wait_ge(dt_ready, 2)
                for n, t in ((0, dt), (1, cums)):
                    for c in range(NT):
                        m = nc.tensor.transpose(ps_y[:, c, n * SH:(n + 1) * SH], t[:, c * P:(c + 1) * P],
                                                mat(k, "ident")[0:SH, 0:SH])
                m.then_inc(tok_done, 1)
                pe.wait_ge(cb_masked, SG)
                pe.wait_ge(tok_copied, 2)

                def outputs(i, b):
                    h = 2 * i + b
                    pe.wait_ge(m_ready, h + 1)
                    pe.wait_ge(c_ready, h + 1)
                    pe.wait_ge(st_ready, h + 3)
                    if b == 0:
                        pe.wait_ge(y_kept, i + 1)
                    for c in range(NT):
                        y = ps_y[b * HD:(b + 1) * HD, c, :]
                        mm(y, xs[b][:, c, :], lm[b][:, c, :], start=True, stop=False)
                        m = mm(y, st[b][:, c, :], ec[b][:, c, :], start=False, stop=True)
                    m.then_inc(y_done, 1)

                def spread_s(i, b):
                    h = 2 * i + b
                    pe.wait_ge(row_in[b], 16 * i + 16)
                    pe.wait_ge(e_ready, h + 1)
                    pe.wait_ge(arg_ready, h + 1)
                    for half in range(2):
                        m = mm(ps_s[b][:, half, :], row[b][:, :], cums[:, half * HALF:(half + 1) * HALF], start=True,
                               stop=True)
                    m.then_inc(spread, 1)

                spread_s(0, 0)

                def head(i, b, g):
                    h = 2 * i + b
                    if not at_last(i, b):
                        spread_s(i + b, 1 - b)
                    if b == 1:
                        outputs(i, 0)
                    elif not at_first(i, b):
                        outputs(i - 1, 1)
                    pe.wait_ge(x_ready, h + 1)
                    pe.wait_ge(st_ready, h + 1)
                    for c in range(NT):
                        m = mm(ps_d[b][:, c, :], k.ssm_tok[:, c, SH * HD + g * SN:SH * HD + (g + 1) * SN], xd[b][:, c, :],
                               start=True, stop=True)
                    m.then_inc(d_done, 1)

                heads(pe, head)
                outputs(pairs - 1, 1)

            @block.scalar
            def _(act):
                act.sem_inc(e_ready, 2)
                act.wait_ge(consts_in, 48)
                nc.scalar.activation(a_exp[:, :], a_exp[:, :], ACT.Exp).then_inc(exps_done, 1)
                act.wait_ge(floored, 1)
                nc.scalar.activation(soft[:, :], soft[:, :], ACT.Exp).then_inc(exps_done, 1)
                act.wait_ge(exps_done, 2)
                nc.scalar.activation(soft[:, :], soft[:, :], ACT.Ln, bias=1.0).then_inc(log_done, 1)

                def head(i, b, g):
                    h = 2 * i + b
                    act.wait_ge(spread, h + 3)
                    act.wait_ge(y_done, h + 1)
                    nc.scalar.activation(ec[b][:, :, :], chunks(ps_s[b][:, :, :]), ACT.Exp).then_inc(e_ready, 1)
                    act.wait_ge(arg_ready, h + 3)
                    nc.scalar.activation(lm[b][:, :, :], lm[b][:, :, :], ACT.Exp).then_inc(l_ready, 1)

                heads(act, head)

            @block.gpsimd
            def _(pool):
                tt = nc.gpsimd.tensor_tensor

                def head(i, b, g):
                    pool.wait_ge(x_ready, 2 * i + b + 1)
                    tt(lm[b][:, :, :], lm[b][:, :, :], cb[:, g], ALU.mult).then_inc(m_ready, 1)
                    tt(ec[b][:, :, :], ec[b][:, :, :], k.ssm[:, ST + SG + g, :].rearrange("p (c t) -> p c t", t=P),
                       ALU.mult).then_inc(c_ready, 1)

                heads(pool, head)

            @block.vector
            def _(dve):
                v = nc.vector
                dve.sem_inc(arg_ready, 2)
                dve.sem_inc(st_ready, 2)
                dve.sem_inc(y_kept, 1)
                link = Chain(dve, link_s)
                for b in range(2):
                    v.memset(st[b][:, 0, :], 0.0).then_inc(zeroed, 1)
                dve.wait_ge(consts_in, 48)
                link(v.tensor_scalar(x0[:, :], x0[:, :], bias[:, :], None, ALU.add))
                link(v.tensor_scalar(soft[:, :], x0[:, :], -1.0, None, ALU.mult))
                v.tensor_tensor(soft[:, :], soft[:, :], x0[:, :], ALU.min).then_inc(floored, 1)
                for g in range(SG):
                    dve.wait_ge(cb_done, g + 1)
                    v.tensor_tensor(cb[:, g], chunks(ps_s[g][:, :, :]),
                                    mat(k, "before_or_at").unsqueeze(1).to_broadcast([P, NT, P]), ALU.mult
                                    ).then_inc(cb_masked, 1)
                dve.wait_ge(log_done, 1)
                v.scalar_tensor_tensor(dt[:, :], x0[:, :], 0.0, soft[:, :], ALU.max, ALU.add).then_inc(dt_ready, 1)
                dve.wait_ge(dt_ready, 1)
                dve.wait_ge(exps_done, 1)
                link(v.tensor_scalar(x0[:, :], dt[:, :], a_exp[:, :], -1.0, ALU.mult, ALU.mult))
                v.tensor_tensor_scan(cums[:, :], mat(k, "reset", T)[0:SH, :], x0[:, :], 0.0, ALU.mult, ALU.add
                                     ).then_inc(dt_ready, 1)
                dve.wait_ge(tok_done, 1)
                for n, t in ((0, dt_tok), (1, cums_tok)):
                    v.tensor_copy(t[:, :, :], ps_y[:, :, n * SH:(n + 1) * SH]).then_inc(tok_copied, 1)
                dve.wait_ge(tok_copied, 2)
                dve.wait_ge(zeroed, 2)

                def states(i, b):
                    h = 2 * i + b
                    link = Chain(dve, link_c)
                    link.base = h * (NT - 2)
                    dve.wait_ge(d_done, h + 3)
                    for c in range(NT - 1):
                        m = v.scalar_tensor_tensor(st[b][:, c + 1, :], st[b][:, c, :], end[b][:, c:c + 1], ps_d[b][:, c, :],
                                                   ALU.mult, ALU.add)
                        if c < NT - 2:
                            link(m)
                    m.then_inc(st_ready, 1)

                def keep(i):
                    dve.wait_ge(y_done, 2 * i + 4)
                    x = k.ssm[:, bass.ds(i, 1), :].rearrange("p a t -> p (a t)")
                    v.scalar_tensor_tensor(x, x, col(k, "ssm_d", i), ps_y[:, :, :].rearrange("p a t -> p (a t)"), ALU.mult,
                                           ALU.add).then_inc(y_kept, 1)

                def head(i, b, g):
                    h = 2 * i + b
                    link = Chain(dve, link_a)
                    link.base = h * 3
                    if b == 1 and not at_first(i, 0):
                        keep(i - 1)
                    dve.wait_ge(spread, h + 3)
                    dve.wait_ge(y_done, h + 1)
                    dve.wait_ge(e_ready, h + 3)
                    of_head = lambda t: t[:, :, bass.ds(h, 1)].to_broadcast([P, NT, P])
                    link(v.tensor_tensor(lm[b][:, :, :], chunks(ps_s[b][:, :, :]), of_head(cums_tok), ALU.subtract))
                    v.tensor_scalar(lm[b][:, :, :], lm[b][:, :, :], 0.0, None, ALU.min).then_inc(arg_ready, 1)
                    link(v.tensor_tensor(xs[b][:, :, :], k.ssm_tok[:, :, bass.ts(h, HD)],
                                         dt_tok[:, :, bass.ds(h, 1)].to_broadcast([P, NT, HD]), ALU.mult))
                    if b == 1:
                        states(i, 0)
                    elif not at_first(i, b):
                        states(i - 1, 1)
                    link(v.tensor_copy(end[b][:, :], ec[b][:, :, P - 1]))
                    dve.wait_ge(l_ready, h + 1)
                    dve.wait_ge(d_done, h + 1)
                    v.tensor_tensor(xd[b][:, :, :], xs[b][:, :, :], lm[b][:, :, P - 1:P].to_broadcast([P, NT, HD]),
                                    ALU.mult).then_inc(x_ready, 1)

                heads(dve, head)
                states(pairs - 1, 1)
                keep(pairs - 1)
                dve.wait_ge(y_kept, pairs + 1)


def ssm_outputs(nc, k):
    with Space(nc, "so") as s:
        zs = [k.mixer_oT[:, b, :] for b in range(2)]
        sq = [k.mixer_oT[:, 2 + b, :] for b in range(2)]
        inv = s.sb("inv", [P, T])
        eps = s.sb("eps", [P, 1])
        ps = [s.ps(f"t{b}", [P, 2, HALF]) for b in range(2)]
        ps_q = s.ps("q", [P, 2, HALF])
        projected, silu_done, gated, squared, summed, root_done, inv_done, normed, eps_set = (s.sem(n) for n in (
            "projected", "silu_done", "gated", "squared", "summed", "root_done", "inv_done", "normed", "eps_set"))
        per = ST // SG
        w = SplitWeights(s, projected)

        def flat(p):
            return p[:, :, :].rearrange("p a b -> p (a b)")

        def y(t):
            return k.ssm[:, bass.ds(t, 1), :].rearrange("p a t -> p (a t)")

        with s.block() as block:
            @block.sync
            def _(sp):
                w.start(sp)
                with sp.Fori(0, ST) as t:
                    w.load(sp, k, t, t + T_Z)

            @block.tensor
            def _(pe):
                pe.sem_inc(projected, 2)
                pe.sem_inc(summed, 2)

                def sums(t, b, j):
                    pe.wait_ge(squared, t + 1)
                    for half in range(2):
                        m = nc.tensor.matmul(ps_q[:, half, :], mat(k, "ones"), sq[b][:, half * HALF:(half + 1) * HALF],
                                             start=(j == 0), stop=(j == per - 1), skip_group_check=True)
                    m.then_inc(summed, 1)

                with pe.Fori(0, SG) as g:
                    for j in range(per):
                        t, b = per * g + j, j % 2
                        pe.wait_ge(silu_done, t + 1)
                        w.project(nc, k, ps[b], t, b).then_inc(projected, 1)
                        if j > 0:
                            if j == 1:
                                pe.wait_ge(root_done, g + 1)
                            sums(t - 1, 1 - b, j - 1)
                    sums(per * g + per - 1, 1, per - 1)

            @block.scalar
            def _(act):
                act.sem_inc(silu_done, 2)
                act.sem_inc(root_done, 1)
                act.wait_ge(eps_set, 1)

                def square(t, b):
                    act.wait_ge(gated, t + 3)
                    act.wait_ge(summed, t + 1)
                    nc.scalar.activation(sq[b][:, :], y(t), ACT.Square).then_inc(squared, 1)

                with act.Fori(0, SG) as g:
                    for j in range(per):
                        t, b = per * g + j, j % 2
                        act.wait_ge(projected, t + 3)
                        act.wait_ge(gated, t + 1)
                        nc.scalar.activation(zs[b][:, :], flat(ps[b]), ACT.Silu).then_inc(silu_done, 1)
                        square(t, b)
                    act.wait_ge(summed, per * g + per + 2)
                    act.wait_ge(normed, per * g + 1)
                    nc.scalar.activation(inv[:, :], flat(ps_q), ACT.Sqrt, bias=eps[:, :], scale=1.0 / (per * P)
                                         ).then_inc(root_done, 1)

            @block.gpsimd
            def _(pool):
                with pool.Fori(0, ST // 2) as i:
                    for b in range(2):
                        w.cut(pool, 2 * i + b, b)

            @block.vector
            def _(dve):
                dve.sem_inc(gated, 2)
                dve.sem_inc(normed, 1)
                nc.vector.memset(eps[:, :], NORM_EPS).then_inc(eps_set, 1)
                with dve.Fori(0, SG) as g:
                    for j in range(per):
                        t, b = per * g + j, j % 2
                        dve.wait_ge(silu_done, t + 3)
                        nc.vector.tensor_tensor(y(t), y(t), zs[b][:, :], ALU.mult).then_inc(gated, 1)
                    dve.wait_ge(root_done, g + 2)
                    nc.vector.reciprocal(inv[:, :], inv[:, :]).then_inc(inv_done, 1)
                    dve.wait_ge(inv_done, g + 1)
                    dve.wait_ge(squared, per * g + per)
                    for j in range(per):
                        t = per * g + j
                        nc.vector.scalar_tensor_tensor(y(t), y(t), col(k, "norm_g", t), inv[:, :], ALU.mult, ALU.mult
                                                       ).then_inc(normed, 1)
                dve.wait_ge(normed, ST + 1)


def merge_branch(nc, k, n, first, last_one):
    n_c, at, o = (ST, 2 * RT, k.ssm) if last_one else (RT, n * RT, k.mixer_oT)
    with Space(nc, f"mg{n}") as s:
        w_b = [s.sb(f"w_b{b}", [P, n_c, P]) for b in range(2)]
        gate = k.room[:, KD, :]
        ps_g = [s.ps(f"g{b}", [P, 2, HALF]) for b in range(2)]
        ps_b = [s.ps(f"b{b}", [P, 2, HALF]) for b in range(2)]
        b_in = [s.sem(f"b_in{b}") for b in range(2)]
        g_done, b_done, g_ready, merged, termed, summing, before_in, stored = (s.sem(m) for m in (
            "g_done", "b_done", "g_ready", "merged", "termed", "summing", "before_in", "stored"))
        w = SplitWeights(s, g_done)

        def flat(p):
            return p[:, :, :].rearrange("p a b -> p (a b)")

        def tile_of(t, i):
            return t[:, bass.ds(i, 1), :].rearrange("p a t -> p (a t)")

        def tiles(eng, body):
            with eng.Fori(0, KD // 2) as i:
                for b in range(2):
                    body(2 * i + b, b)

        with s.block() as block:
            @block.sync
            def _(sp):
                def load(i, b):
                    w.load(sp, k, i, i + (T_GATE + n * KD))
                    sp.wait_ge(b_done, i + 1)
                    sp.dma_start(w_b[b][:, :, :], k.w_br[bass.ds(i, 1), :, at:at + n_c, :].rearrange(
                        "a p k c -> (a p) k c")).then_inc(b_in[b], 16)

                w.start(sp)
                tiles(sp, load)
                if not last_one:
                    with sp.Fori(0, KD) as i:
                        sp.wait_ge(merged, i + 3)
                        sp.dma_start(k.merged_d[bass.ds(i, 1)].rearrange("a p t -> (a p) t"), tile_of(k.merged, i)
                                     ).then_inc(stored, 16)
                    sp.wait_ge(stored, 16 * KD)

            @block.gpsimd
            def _(pool):
                tiles(pool, lambda i, b: w.cut(pool, i, b))

            @block.tensor
            def _(pe):
                pe.sem_inc(g_done, 2)
                pe.sem_inc(b_done, 2)

                with pe.Fori(0, KD // 2) as r:
                    for b in range(2):
                        i = 2 * r + b
                        pe.wait_ge(g_ready, i + 1)
                        w.project(nc, k, ps_g[b], i, b).then_inc(g_done, 1)
                        pe.wait_ge(b_in[b], 16 * r + 16)
                        pe.wait_ge(termed, i + 1)
                        for half in range(2):
                            for c in range(n_c):
                                last = nc.tensor.matmul(ps_b[b][:, half, :], w_b[b][:, c, :],
                                                        o[:, c, half * HALF:(half + 1) * HALF], start=(c == 0),
                                                        stop=(c == n_c - 1))
                        last.then_inc(b_done, 1)

            @block.scalar
            def _(act):
                act.sem_inc(g_ready, 2)
                if not first:
                    act.dma_start(k.merged[:, :, :], k.merged_d.rearrange("i p t -> p i t")).then_inc(before_in, 16)

                def sigmoid(i, b):
                    act.wait_ge(g_done, i + 3)
                    act.wait_ge(termed, i + 2)
                    nc.scalar.activation(gate, flat(ps_g[b]), ACT.Sigmoid, bias=col(k, "gate_bias", i + n * KD)
                                         ).then_inc(g_ready, 1)

                tiles(act, sigmoid)

            @block.vector
            def _(dve):
                dve.sem_inc(termed, 2)
                dve.sem_inc(merged, 2)
                if not first:
                    dve.wait_ge(before_in, 16)

                def term(i, b):
                    dve.wait_ge(g_ready, i + 3)
                    dve.wait_ge(b_done, i + 3)
                    to = tile_of(k.merged, i) if first else gate
                    m = nc.vector.tensor_tensor(to, gate, flat(ps_b[b]), ALU.mult)
                    if not first:
                        m.then_inc(summing, 1)
                        dve.wait_ge(summing, i + 1)
                        m = nc.vector.tensor_tensor(tile_of(k.merged, i), tile_of(k.merged, i), gate, ALU.add)
                    m.then_inc(merged, 1)
                    dve.wait_ge(merged, i + 3)
                    dve.sem_inc(termed, 1)

                tiles(dve, term)
                dve.wait_ge(merged, KD + 2)


def merge_rwkv(nc, k):
    merge_branch(nc, k, 0, True, False)


def merge_fox(nc, k):
    merge_branch(nc, k, 1, False, False)


def merge_ssm(nc, k):
    merge_branch(nc, k, 2, False, True)


def layer_norm(nc, dve, link, r, out, ln, mv, stats, sd, halves, stood, aggregated, wait_root):
    v = nc.vector
    link(v.bn_stats(stats[:, 0, :], r[:, 0:HALF]))
    v.bn_stats(stats[:, 1, :], r[:, HALF:D]).then_inc(halves, 1)
    wait_apart(dve, halves, aggregated[2], stood)
    v.bn_aggr(mv[:, :], stats[:, :, :]).then_inc(*aggregated[:2])
    dve.wait_ge(aggregated[0], aggregated[2])
    link(v.scalar_tensor_tensor(r[:, :], r[:, :], mv[:, 0:1], ln[:, 0, :], ALU.subtract, ALU.mult))
    wait_root()
    link(v.reciprocal(sd[:, :], sd[:, :]))
    return v.scalar_tensor_tensor(out, r[:, :], sd[:, :], ln[:, 1, :], ALU.mult, ALU.add)


def out_project(nc, k):
    with Space(nc, "op") as s:
        w = s.sb("w", [P, KD, D])
        lhs = [s.sb(f"lhs{b}", [P, KD, P]) for b in range(2)]
        r = [s.sb(f"r{b}", [P, D]) for b in range(2)]
        x1 = [s.sb(f"x1{b}", [P, D]) for b in range(2)]
        ln = s.sb("ln", [P, 2, D])
        w_r, b_r = s.sb("w_r", [P, KD, E]), s.sb("b_r", [P, E])
        xt = [s.sb(f"xt{b}", [P, KD, P]) for b in range(2)]
        zeros = s.sb("zeros", [P, D])
        stats, mv, sd, eps = s.sb("stats", [P, 2, 6]), s.sb("mv", [P, 2]), s.sb("sd", [P, 1]), s.sb("eps", [P, 1])
        ps = [s.ps(f"t{b}", [P, 2, HALF]) for b in range(2)]
        ps_t = s.ps("turn", [P, KD, P])
        ps_l = [s.ps(f"l{b}", [P, HALF]) for b in range(2)]
        x_in = [s.sem(f"x_in{b}") for b in range(2)]
        stored = [s.sem(f"stored{b}") for b in range(2)]
        zeroed, slots_zeroed = s.sem("zeroed"), s.sem("slots_zeroed")
        (w_in, ln_in, router_in, lhs_ready, projected, mixed, aggregated, root_done, x1_ready, turned, turn_copied,
         logits_done, logits_copied, aff_ready, sel_ready, eps_set, last, halves, stood) = (s.sem(n) for n in (
             "w_in", "ln_in", "router_in", "lhs_ready", "projected", "mixed", "aggregated", "root_done", "x1_ready", "turned",
             "turn_copied", "logits_done", "logits_copied", "aff_ready", "sel_ready", "eps_set", "last",
             "halves", "stood"))
        x_rows = k.x.rearrange("a (n p) d -> (a n) p d", p=P)
        x1_rows = k.x1_d.rearrange("(n p) d -> n p d", p=P)

        def tiles(eng, body):
            with eng.Fori(0, NT // 2) as i:
                for b in range(2):
                    body(2 * i + b, b)

        with s.block() as block:
            @block.sync
            def _(sp):
                for b in range(2):
                    sp.sem_inc(stored[b], 16)
                for h in range(2):
                    sp.dma_start(w[:, h * 4:h * 4 + 4, :], k.w_out[:, h * 4:h * 4 + 4, :]).then_inc(w_in, 16)
                for n in range(2):
                    sp.dma_start(ln[:, n, :], k.ln1[n:n + 1, :].partition_broadcast(P)).then_inc(ln_in, 16)
                sp.dma_start(w_r[:, :, :], k.router_w).then_inc(router_in, 16)
                sp.dma_start(b_r[:, :], k.router_b.partition_broadcast(P)).then_inc(router_in, 16)

                def load(t, b):
                    sp.dma_start(r[b][:, :], x_rows[bass.ds(t, 1)].rearrange("a p d -> (a p) d")).then_inc(x_in[b], 16)

                def store(t, b):
                    sp.wait_ge(x1_ready, t + 3)
                    sp.dma_start(x1_rows[bass.ds(t, 1)].rearrange("a p d -> (a p) d"), x1[b][:, :]).then_inc(stored[b], 16)

                load(0, 0)
                load(1, 1)
                with sp.Fori(0, NT // 2 - 1) as i:
                    for b in range(2):
                        store(2 * i + b, b)
                        load(2 * i + b + 2, b)
                for b in range(2):
                    store(NT - 2 + b, b)
                for b in range(2):
                    sp.wait_ge(stored[b], 16 + 8 * NT)

            @block.gpsimd
            def _(pool):
                nc.gpsimd.memset(zeros[:, :], 0.0).then_inc(zeroed, 1)
                pool.wait_ge(zeroed, 1)
                pool.dma_start(k.buf_tok.rearrange("(b p) o -> b (p o)", p=P), zeros[0:N_BLOCKS, 0:P]).then_inc(slots_zeroed, 16)
                with pool.Fori(E, N_BLOCKS) as n:
                    pool.dma_start(k.y_slots.rearrange("(b p) d -> b p d", p=P)[bass.ds(n, 1)].rearrange("a p d -> (a p) d"),
                                   zeros[:, :]).then_inc(slots_zeroed, 16)

                def copy(t, b):
                    pool.wait_ge(projected, t + 1)
                    nc.gpsimd.tensor_copy(lhs[b][:, :, :], k.merged[:, :, bass.ts(t, P)]).then_inc(lhs_ready, 1)

                tiles(pool, copy)
                pool.wait_ge(slots_zeroed, 16 * (1 + OVER))

            @block.tensor
            def _(pe):
                mm = nc.tensor.matmul
                pe.sem_inc(projected, 2)

                def mix(t, b):
                    pe.wait_ge(lhs_ready, t + 1)
                    pe.wait_ge(mixed, t + 1)
                    for h in range(2):
                        for d in range(KD):
                            m = mm(ps[b][:, h, :], lhs[b][:, d, :], w[:, d, h * HALF:(h + 1) * HALF], start=(d == 0),
                                   stop=(d == KD - 1))
                    m.then_inc(projected, 1)

                def turn(t, b):
                    pe.wait_ge(x1_ready, t + 3)
                    pe.wait_ge(turn_copied, t + 2)
                    for c in range(KD):
                        m = nc.tensor.transpose(ps_t[:, c, :], x1[b][:, c * P:(c + 1) * P], mat(k, "ident"))
                    m.then_inc(turned, 1)

                def logits(t, b):
                    pe.wait_ge(turn_copied, t + 3)
                    pe.wait_ge(logits_copied, t + 1)
                    for c in range(KD):
                        m = mm(ps_l[b][:, 0:E], xt[b][:, c, :], w_r[:, c, :], start=(c == 0), stop=(c == KD - 1))
                    m.then_inc(logits_done, 1)

                pe.wait_ge(w_in, 32)
                mix(0, 0)
                mix(1, 1)
                turn(0, 0)
                pe.wait_ge(router_in, 32)
                with pe.Fori(1, NT // 2) as i:
                    for b in range(2):
                        mix(2 * i + b, b)
                        turn(2 * i + b - 1, 1 - b)
                        logits(2 * i + b - 2, b)
                turn(NT - 1, 1)
                logits(NT - 2, 0)
                logits(NT - 1, 1)

            @block.scalar
            def _(act):
                act.sem_inc(turn_copied, 2)
                act.sem_inc(logits_copied, 2)
                act.sem_inc(logits_done, 2)
                act.wait_ge(eps_set, 1)

                def root(t):
                    act.wait_ge(aggregated, t + 1)
                    nc.scalar.activation(sd[:, :], mv[:, 1:2], ACT.Sqrt, bias=eps[:, :]).then_inc(root_done, 1)

                def out_of_psum(t, b):
                    act.wait_ge(turned, t + 3)
                    act.wait_ge(logits_done, t + 1)
                    nc.scalar.copy(xt[b][:, :, :], ps_t[:, :, :]).then_inc(turn_copied, 1)

                def keep_logits(t, b):
                    act.wait_ge(logits_done, t + 3)
                    nc.scalar.copy(k.aff[:, bass.ds(t, 1), :].rearrange("p a e -> p (a e)"), ps_l[b][:, 0:E]
                                   ).then_inc(logits_copied, 1)

                root(0)
                root(1)
                out_of_psum(0, 0)
                with act.Fori(1, NT // 2) as i:
                    for b in range(2):
                        root(2 * i + b)
                        out_of_psum(2 * i + b - 1, 1 - b)
                        keep_logits(2 * i + b - 2, b)
                out_of_psum(NT - 1, 1)
                keep_logits(NT - 2, 0)
                keep_logits(NT - 1, 1)
                act.wait_ge(logits_copied, NT + 2)
                nc.scalar.activation(k.aff[:, :, :], k.aff[:, :, :], ACT.Sigmoid).then_inc(aff_ready, 1)
                act.wait_ge(aff_ready, 1)

            @block.vector
            def _(dve):
                v = nc.vector
                v.memset(eps[:, :], LN_EPS).then_inc(eps_set, 1)
                dve.sem_inc(mixed, 2)
                dve.sem_inc(x1_ready, 2)
                dve.sem_inc(turned, 2)
                dve.wait_ge(ln_in, 32)

                def norm(t, b):
                    link = Chain(dve, last)
                    link.base = t * 3
                    dve.wait_ge(x_in[b], (t - b) * 8 + 16)
                    dve.wait_ge(projected, t + 3)
                    v.scalar_tensor_tensor(r[b][:, :], r[b][:, :], ALPHA, ps[b][:, :, :].rearrange("p a b -> p (a b)"),
                                           ALU.mult, ALU.add).then_inc(mixed, 1)
                    dve.wait_ge(mixed, t + 3)
                    dve.wait_ge(stored[b], (t - b) * 8 + 16)
                    dve.wait_ge(turned, t + 1)
                    layer_norm(nc, dve, link, r[b], x1[b][:, :], ln, mv, stats, sd, halves, stood, (aggregated, 1, t + 1),
                               lambda: dve.wait_ge(root_done, t + 1)).then_inc(x1_ready, 1)

                tiles(dve, norm)
                dve.wait_ge(router_in, 32)
                dve.wait_ge(aff_ready, 1)
                v.tensor_tensor(k.sel[:, :, :], k.aff[:, :, :], b_r[:, :].unsqueeze(1).to_broadcast([P, NT, E]), ALU.add
                                ).then_inc(sel_ready, 1)
                dve.wait_ge(sel_ready, 1)


def route(nc, k):
    with Space(nc, "rt") as s:
        def grid(name):
            return s.sb(name, [P, NT, E])

        eq, idx_of, cand, oh1, oh2, both, pos = (grid(n) for n in ("eq", "idx_of", "cand", "oh1", "oh2", "both", "pos"))
        best, first, score = (s.sb(n, [P, NT * EG]) for n in ("best", "first", "score"))
        g1, g2 = s.sb("g1", [P, NT]), s.sb("g2", [P, NT])
        before = s.sb("before", [P, NT + 1, E])
        over = s.sb("over", [P, E])
        over_end, over_slot, one_e = s.sb("over_end", [P, E]), s.sb("over_slot", [P, E]), s.sb("one_e", [P, E])
        ended = s.sb("ended", [P, 16, E])
        block_expert, rows = s.sb("block_expert", [P, 16]), s.sb("rows", [P, 16])
        token = s.sb("token", [P, NT])
        dest = s.sb("dest", [P, NT, 2])
        slots = s.sb("slots", [N_BLOCKS, P])
        ps_rank, ps_count, ps_slots = s.ps("rank", [P, NT, E]), s.ps("count", [P, HALF]), s.ps("slots", [P, HALF])
        (last, picked, ranked, dest_ready, scattered, slots_in, slots_turned, done) = (s.sem(n) for n in (
            "last", "picked", "ranked", "dest_ready", "scattered", "slots_in", "slots_turned", "done"))

        with s.block() as block:
            @block.vector
            def _(dve):
                v, link = nc.vector, Chain(dve, last)
                tt, ts = v.tensor_tensor, v.tensor_scalar

                def spread(t, shape):
                    return t.unsqueeze(2).to_broadcast(shape)

                def first_of_max(values, index, n, width, one_hot, value, take_out=None):
                    shape = [P, n, width]
                    link(v.tensor_reduce(value, values, AX.X, ALU.max))
                    link(tt(one_hot, values, spread(value, shape), ALU.is_lt))
                    link(v.scalar_tensor_tensor(one_hot, one_hot, float(P), index, ALU.mult, ALU.add))
                    link(v.tensor_reduce(first[:, 0:n], one_hot, AX.X, ALU.min))
                    link(tt(one_hot, index, spread(first[:, 0:n], shape), ALU.is_equal))
                    if take_out is not None:
                        link(v.scalar_tensor_tensor(take_out, one_hot, NEG, values, ALU.mult, ALU.add))

                def by_group(t):
                    return t[:, :, :].rearrange("p n (g e) -> p (n g) e", e=EPG)

                experts = mat(k, "experts", E).unsqueeze(1).to_broadcast([P, NT, E])
                link(v.tensor_copy(idx_of[:, :, :], experts))
                first_of_max(by_group(k.sel), by_group(idx_of), NT * EG, EPG, by_group(oh1), best[:, :], by_group(cand))
                link(v.tensor_reduce(score[:, :], by_group(cand), AX.X, ALU.max))
                link(tt(score[:, :], score[:, :], best[:, :], ALU.add))
                scores = score[:, :].rearrange("p (n g) -> p n g", g=EG)
                eq_g = eq[:, :, 0:EG]
                first_of_max(scores, idx_of[:, :, 0:EG], NT, EG, eq_g, g1[:, :])
                link(v.tensor_copy(score[:, :].rearrange("p (n g) -> p n g", g=EG), eq_g))
                in_group = score[:, :].unsqueeze(2).to_broadcast([P, NT * EG, EPG])
                link(v.tensor_copy(by_group(eq), in_group))
                link(tt(cand[:, :, :], k.sel[:, :, :], eq[:, :, :], ALU.mult))
                link(ts(eq[:, :, :], eq[:, :, :], 1.0, -NEG, ALU.subtract, ALU.mult))
                link(tt(cand[:, :, :], cand[:, :, :], eq[:, :, :], ALU.add))
                first_of_max(cand[:, :, :], idx_of[:, :, :], NT, E, oh1[:, :, :], g1[:, :], cand[:, :, :])
                first_of_max(cand[:, :, :], idx_of[:, :, :], NT, E, oh2[:, :, :], g2[:, :])
                tt(both[:, :, :], oh1[:, :, :], oh2[:, :, :], ALU.add).then_inc(picked, 1)
                dve.wait_ge(picked, 1)
                link(v.memset(before[:, 0, :], 0.0))
                for n in range(NT):
                    m = tt(before[:, n + 1, :], before[:, n, :], both[:, n, :], ALU.add)
                    if n < NT - 1:
                        link(m)
                m.then_inc(picked, 1)
                for g, oh in ((g1, oh1), (g2, oh2)):
                    link(tt(eq[:, :, :], k.aff[:, :, :], oh[:, :, :], ALU.mult))
                    link(v.tensor_reduce(g[:, :], eq[:, :, :], AX.X, ALU.add))
                link(tt(k.gates[:, :, 0], g1[:, :], g2[:, :], ALU.add))
                link(v.reciprocal(k.gates[:, :, 1], k.gates[:, :, 0]))
                link(tt(k.gates[:, :, 0], g1[:, :], k.gates[:, :, 1], ALU.mult))
                link(tt(k.gates[:, :, 1], g2[:, :], k.gates[:, :, 1], ALU.mult))
                dve.wait_ge(ranked, 2)
                link(ts(over[:, :], ps_count[:, 0:E], float(P), None, ALU.is_gt))
                for j in range(2, T // P):
                    link(v.scalar_tensor_tensor(over[:, :], ps_count[:, 0:E], float(j * P), over[:, :], ALU.is_gt, ALU.add))
                link(v.memset(one_e[:, :], 1.0))
                link(v.tensor_tensor_scan(over_end[:, :], one_e[:, :], over[:, :], 0.0, ALU.mult, ALU.add))
                link(tt(ended[:, :, :], over_end[:, :].unsqueeze(1).to_broadcast([P, 16, E]),
                        mat(k, "over_ids", 16).unsqueeze(2).to_broadcast([P, 16, E]), ALU.is_le))
                link(v.tensor_reduce(block_expert[:, :], ended[:, :, :], AX.X, ALU.add))
                link(ts(k.unused[:, :], block_expert[:, :], float(E), None, ALU.is_ge))
                link(ts(rows[:, :], block_expert[:, :], float(E - 1), float(P), ALU.min, ALU.mult))
                link(tt(k.over_rows[:, :], rows[:, :], mat(k, "row0", 16), ALU.add))
                link(tt(over_slot[:, :], over_end[:, :], over[:, :], ALU.subtract))
                link(ts(over_slot[:, :], over_slot[:, :], float(P), float((E - 1) * P), ALU.mult, ALU.add))
                link(tt(over_slot[:, :], over_slot[:, :], mat(k, "slot0", E), ALU.subtract))
                link(ts(pos[:, :, :], ps_rank[:, :, :], float(P), None, ALU.is_ge))
                link(tt(pos[:, :, :], pos[:, :, :], over_slot[:, :].unsqueeze(1).to_broadcast([P, NT, E]), ALU.mult))
                link(tt(pos[:, :, :], pos[:, :, :], ps_rank[:, :, :], ALU.add))
                link(tt(pos[:, :, :], pos[:, :, :], mat(k, "slot0", E).unsqueeze(1).to_broadcast([P, NT, E]), ALU.add))
                for n, oh in ((0, oh1), (1, oh2)):
                    link(tt(eq[:, :, :], pos[:, :, :], oh[:, :, :], ALU.mult))
                    link(v.tensor_reduce(dest[:, :, n], eq[:, :, :], AX.X, ALU.add))
                link(ts(token[:, :], mat(k, "slot0", NT), mat(k, "row0", 1), None, ALU.add))
                v.tensor_copy(k.dest[:, :, :], dest[:, :, :]).then_inc(dest_ready, 1)
                dve.wait_ge(dest_ready, 1)
                dve.wait_ge(slots_turned, 1)
                v.tensor_copy(k.slot_token[:, :], ps_slots[:, 0:N_BLOCKS]).then_inc(done, 1)
                dve.wait_ge(done, 1)

            @block.tensor
            def _(pe):
                mm = nc.tensor.matmul
                pe.wait_ge(picked, 2)
                mm(ps_rank[:, :, :], mat(k, "before"), both[:, :, :], start=True, stop=False)
                mm(ps_rank[:, :, :], mat(k, "ones"), before[:, 0:NT, :], start=False, stop=True).then_inc(ranked, 1)
                mm(ps_count[:, 0:E], mat(k, "ones"), before[:, NT, :], start=True, stop=True).then_inc(ranked, 1)
                pe.wait_ge(slots_in, 16)
                nc.tensor.transpose(ps_slots[:, 0:N_BLOCKS], slots[:, :], mat(k, "ident")[0:N_BLOCKS, 0:N_BLOCKS]
                                    ).then_inc(slots_turned, 1)

            @block.gpsimd
            def _(pool):
                pool.wait_ge(dest_ready, 1)
                for n in range(NT):
                    for j in range(2):
                        pool.indirect_dma_start(k.buf_tok, bass.IndirectOffsetOnAxis(ap=k.dest[:, n, j:j + 1], axis=0),
                                                token[:, n:n + 1], None).then_inc(scattered, 16)

            @block.scalar
            def _(act):
                for part in range(3):
                    load_expert(act, k, 0, part)

            @block.sync
            def _(sp):
                sp.wait_ge(scattered, 16 * 2 * NT)
                sp.dma_start(slots[:, :], k.buf_tok.rearrange("(b p) o -> b (p o)", p=P)).then_inc(slots_in, 16)
                sp.wait_ge(slots_in, 16)


def load_expert(eng, k, e, part):
    src = (k.exp_gate, k.exp_up, k.exp_down)[part].rearrange("e (p k) f -> e p (k f)", p=P)
    eng.dma_start(k.landed[part][:, :], src[bass.ds(e, 1)].rearrange("a p f -> (a p) f")).then_inc(k.landing[part], 16)


def experts(nc, k):
    with Space(nc, "ex") as s:
        high, low = ([s.sb(f"{m}{n}", [P, KD * DE], F32R) for n in range(3)] for m in ("high", "low"))
        xb = [s.sb(f"xb{b}", [P, D]) for b in range(2)]
        idx = [s.sb(f"idx{b}", [P, 1], U32) for b in range(2)]
        gate, h = s.sb("gate", [P, DE]), s.sb("h", [P, DE])
        xt, ht = ([s.sb(f"{n}{i}", [P, c, P], F32R) for i in range(2)] for n, c in (("xt", KD), ("ht", FF)))
        y = [s.sb(f"y{b}", [P, D]) for b in range(2)]
        ps_x, ps_y = s.ps("x", [P, KD, P]), s.ps("y", [P, 2, HALF])
        ps_g, ps_u, ps_h = s.ps("g", [P, DE]), s.ps("u", [P, DE]), s.ps("h", [P, FF, P])
        x_in, y_out = ([s.sem(f"{n}{b}") for b in range(2)] for n in ("x_in", "y_out"))
        high_ready, low_ready = ([s.sem(f"{n}{i}") for i in range(3)] for n in ("high_ready", "low_ready"))
        used = [s.sem(f"used{i}") for i in range(3)]
        (idx_ready, x_turned, x_high_ready, x_low_ready, silu_done, h_ready, h_turned, h_high_ready, h_low_ready, y_kept,
         idx_stood) = (s.sem(n) for n in (
             "idx_ready", "x_turned", "x_high_ready", "x_low_ready", "silu_done", "h_ready", "h_turned", "h_high_ready",
             "h_low_ready", "y_kept", "idx_stood"))
        y_blocks = k.y_slots.rearrange("(b p) d -> b p d", p=P)

        def pairs(eng, body, lo=0, hi=E // 2, first=0):
            with eng.Fori(lo, hi) as i:
                for n in range(2):
                    body(2 * i + n + first, (n + first) % 2)

        with s.block() as block:
            @block.sync
            def _(sp):
                def load(e, part):
                    sp.wait_ge(low_ready[part], e)
                    load_expert(sp, k, e, part)

                load(1, 0)
                load(1, 1)
                with sp.Fori(1, E - 1) as e:
                    load(e + 1, 0)
                    load(e + 1, 1)
                    load(e, 2)
                load(E - 1, 2)

            @block.gpsimd
            def _(pool):
                def gather(e, b):
                    pool.wait_ge(x_turned, e + 1)
                    nc.gpsimd.tensor_copy(idx[b][:, :], k.slot_token[:, bass.ds(e, 1)]).then_inc(idx_ready, 1)
                    wait_apart(pool, idx_ready, e + 1, idx_stood)
                    pool.indirect_dma_start(xb[b][:, :], None, k.x1_d, bass.IndirectOffsetOnAxis(ap=idx[b][:, :], axis=0)
                                            ).then_inc(x_in[b], 16)

                pairs(pool, gather)

            @block.tensor
            def _(pe):
                pe.sem_inc(x_turned, 2)
                for sem in used:
                    pe.sem_inc(sem, 1)

                def product(e, b, part, ps, lhs, c, rhs_at, n_c):
                    rhs = (high[part][:, rhs_at:rhs_at + HALF], low[part][:, rhs_at:rhs_at + HALF])
                    return times(nc, ps, (lhs[0][:, c, :], lhs[1][:, c, :]), rhs, c == 0, c == n_c - 1)

                def turn_x(e, b):
                    pe.wait_ge(x_in[b], (e - b) * 8 + 16)
                    pe.wait_ge(x_low_ready, e + 1)
                    for c in range(KD):
                        m = nc.tensor.transpose(ps_x[:, c, :], xb[b][:, c::KD], mat(k, "ident"))
                    m.then_inc(x_turned, 1)

                def gate_up(e, b):
                    pe.wait_ge(x_low_ready, e + 2)
                    for part, ps, read in ((0, ps_g, silu_done), (1, ps_u, h_ready)):
                        pe.wait_ge(low_ready[part], e + 1)
                        pe.wait_ge(read, e + 1)
                        for c in range(KD):
                            m = product(e, b, part, ps[:, :], xt, c, c * DE, KD)
                        m.then_inc(used[part], 1)

                def turn_h(e, b):
                    pe.wait_ge(h_ready, e + 2)
                    pe.wait_ge(h_low_ready, e + 1)
                    for c in range(FF):
                        m = nc.tensor.transpose(ps_h[:, c, :], h[:, c::FF], mat(k, "ident"))
                    m.then_inc(h_turned, 1)

                def down(e, b):
                    pe.wait_ge(low_ready[2], e + 1)
                    pe.wait_ge(h_low_ready, e + 2)
                    pe.wait_ge(y_kept, e + 1)
                    for half in range(2):
                        for c in range(FF):
                            m = product(e, b, 2, ps_y[:, half, :], ht, c, c * D + half * HALF, FF)
                    m.then_inc(used[2], 1)

                turn_x(0, 0)
                gate_up(0, 0)
                turn_x(1, 1)
                turn_h(0, 0)

                def body(e, b):
                    gate_up(e, b)
                    turn_x(e + 1, 1 - b)
                    down(e - 1, 1 - b)
                    turn_h(e, b)

                pairs(pe, body, 0, E // 2 - 1, 1)
                gate_up(E - 1, 1)
                down(E - 2, 0)
                turn_h(E - 1, 1)
                down(E - 1, 1)

            @block.scalar
            def _(act):
                act.sem_inc(silu_done, 1)
                act.sem_inc(y_kept, 1)
                for b in range(2):
                    act.sem_inc(y_out[b], 16)

                def high_x(e):
                    act.wait_ge(x_turned, e + 3)
                    act.wait_ge(used[1], e + 1)
                    nc.scalar.copy(xt[0][:, :, :], ps_x[:, :, :]).then_inc(x_high_ready, 1)

                def high_w(e, b, part):
                    act.wait_ge(k.landing[part], e * 16 + 16)
                    act.wait_ge(used[part], e + 1)
                    nc.scalar.copy(high[part][:, :], k.landed[part][:, :]).then_inc(high_ready[part], 1)

                def silu(e):
                    act.wait_ge(used[0], e + 2)
                    act.wait_ge(h_ready, e + 1)
                    nc.scalar.activation(gate[:, :], ps_g[:, :], ACT.Silu).then_inc(silu_done, 1)

                def high_h(e):
                    act.wait_ge(h_turned, e + 1)
                    act.wait_ge(used[2], e + 1)
                    nc.scalar.copy(ht[0][:, :, :], ps_h[:, :, :]).then_inc(h_high_ready, 1)

                def keep_y(e, b):
                    act.wait_ge(used[2], e + 2)
                    act.wait_ge(y_out[b], (e - b) * 8 + 16)
                    nc.scalar.copy(y[b][:, :], ps_y[:, :, :].rearrange("p a b -> p (a b)")).then_inc(y_kept, 1)
                    act.wait_ge(y_kept, e + 2)
                    act.dma_start(y_blocks[bass.ds(e, 1)].rearrange("a p d -> (a p) d"), y[b][:, :]).then_inc(y_out[b], 16)

                high_w(0, 0, 0)
                high_x(0)
                high_w(0, 0, 1)
                silu(0)
                high_w(1, 1, 0)
                high_x(1)
                high_w(1, 1, 1)
                high_w(0, 0, 2)
                high_h(0)

                def body(e, b):
                    silu(e)
                    high_w(e + 1, 1 - b, 0)
                    high_x(e + 1)
                    high_w(e + 1, 1 - b, 1)
                    keep_y(e - 1, 1 - b)
                    high_w(e, b, 2)
                    high_h(e)

                pairs(act, body, 0, E // 2 - 1, 1)
                silu(E - 1)
                keep_y(E - 2, 0)
                high_w(E - 1, 1, 2)
                high_h(E - 1)
                keep_y(E - 1, 1)
                for b in range(2):
                    act.wait_ge(y_out[b], 16 + 8 * E)

            @block.vector
            def _(dve):
                dve.sem_inc(h_ready, 1)
                dve.sem_inc(h_low_ready, 1)
                dve.sem_inc(x_low_ready, 1)

                def low_x(e):
                    dve.wait_ge(x_high_ready, e + 1)
                    nc.vector.tensor_tensor(xt[1][:, :, :], ps_x[:, :, :], xt[0][:, :, :], ALU.subtract
                                            ).then_inc(x_low_ready, 1)

                def low_w(e, b, part):
                    dve.wait_ge(high_ready[part], e + 1)
                    nc.vector.tensor_tensor(low[part][:, :], k.landed[part][:, :], high[part][:, :], ALU.subtract
                                            ).then_inc(low_ready[part], 1)

                def times_up(e):
                    dve.wait_ge(silu_done, e + 2)
                    dve.wait_ge(used[1], e + 2)
                    if not (isinstance(e, int) and e == 0):
                        dve.wait_ge(h_turned, e)
                    nc.vector.tensor_tensor(h[:, :], gate[:, :], ps_u[:, :], ALU.mult).then_inc(h_ready, 1)

                def low_h(e):
                    dve.wait_ge(h_high_ready, e + 1)
                    nc.vector.tensor_tensor(ht[1][:, :, :], ps_h[:, :, :], ht[0][:, :, :], ALU.subtract
                                            ).then_inc(h_low_ready, 1)

                low_w(0, 0, 0)
                low_x(0)
                low_w(0, 0, 1)
                low_w(1, 1, 0)
                times_up(0)
                low_x(1)
                low_w(1, 1, 1)
                low_w(0, 0, 2)
                low_h(0)

                def body(e, b):
                    low_w(e + 1, 1 - b, 0)
                    times_up(e)
                    low_x(e + 1)
                    low_w(e + 1, 1 - b, 1)
                    low_w(e, b, 2)
                    low_h(e)

                pairs(dve, body, 0, E // 2 - 1, 1)
                times_up(E - 1)
                low_w(E - 1, 1, 2)
                low_h(E - 1)


def overflow_experts(nc, k):
    with Space(nc, "ov") as s:
        w_g, w_u, w_d = s.sb("w_g", [P, KD, DE]), s.sb("w_u", [P, KD, DE]), s.sb("w_d", [P, FF, D])
        xb, idx, w_idx = s.sb("xb", [P, D]), s.sb("idx", [P, 1], U32), s.sb("w_idx", [P, 1], U32)
        xt, gate, h, ht = s.sb("xt", [P, KD, P]), s.sb("gate", [P, DE]), s.sb("h", [P, DE]), s.sb("ht", [P, FF, P])
        y = s.sb("y", [P, D])
        ps_x, ps_y = s.ps("x", [P, KD, P]), s.ps("y", [P, 2, HALF])
        ps_g, ps_u, ps_h = s.ps("g", [P, DE]), s.ps("u", [P, DE]), s.ps("h", [P, FF, P])
        (idx_ready, loaded, x_turned, x_copied, gu_done, silu_done, h_ready, h_turned, h_copied, d_done, y_kept, stored,
         idx_stood) = (
            s.sem(n) for n in ("idx_ready", "loaded", "x_turned", "x_copied", "gu_done", "silu_done", "h_ready", "h_turned",
                               "h_copied", "d_done", "y_kept", "stored", "idx_stood"))
        rows = [w.rearrange("e (p k) f -> (e p) (k f)", p=P) for w in (k.exp_gate, k.exp_up, k.exp_down)]
        y_blocks = k.y_slots.rearrange("(b p) d -> b p d", p=P)

        def blocks(eng, body):
            none = eng.value_load(k.unused[0:1, 0:1], min_val=0, max_val=1)
            with eng.If(none < 1):
                with eng.Fori(0, OVER) as j:
                    unused = eng.value_load(k.unused[0:1, bass.ds(j, 1)], min_val=0, max_val=1)
                    with eng.If(unused < 1):
                        body(j)
                    with eng.Else():
                        pass
            with eng.Else():
                pass

        with s.block() as block:
            @block.gpsimd
            def _(pool):
                def body(j):
                    nc.gpsimd.tensor_copy(idx[:, :], k.slot_token[:, bass.ds(j + E, 1)]).then_inc(idx_ready, 1)
                    nc.gpsimd.tensor_copy(w_idx[:, :], k.over_rows[:, bass.ds(j, 1)]).then_inc(idx_ready, 1)
                    wait_apart(pool, idx_ready, 2 * j + 2, idx_stood)
                    pool.indirect_dma_start(xb[:, :], None, k.x1_d, bass.IndirectOffsetOnAxis(ap=idx[:, :], axis=0)
                                            ).then_inc(loaded, 16)
                    for w, src in ((w_g, rows[0]), (w_u, rows[1]), (w_d, rows[2])):
                        pool.indirect_dma_start(w[:, :, :].rearrange("p k f -> p (k f)"), None, src,
                                                bass.IndirectOffsetOnAxis(ap=w_idx[:, :], axis=0)).then_inc(loaded, 16)
                    pool.wait_ge(y_kept, j + 1)
                    pool.dma_start(y_blocks[bass.ds(j + E, 1)].rearrange("a p d -> (a p) d"), y[:, :]).then_inc(stored, 16)
                    pool.wait_ge(stored, 16 * j + 16)

                blocks(pool, body)

            @block.tensor
            def _(pe):
                mm = nc.tensor.matmul

                def body(j):
                    pe.wait_ge(loaded, 64 * j + 64)
                    for c in range(KD):
                        m = nc.tensor.transpose(ps_x[:, c, :], xb[:, c::KD], mat(k, "ident"))
                    m.then_inc(x_turned, 1)
                    pe.wait_ge(x_copied, j + 1)
                    for w, ps in ((w_g, ps_g), (w_u, ps_u)):
                        for c in range(KD):
                            m = mm(ps[:, :], xt[:, c, :], w[:, c, :], start=(c == 0), stop=(c == KD - 1))
                        m.then_inc(gu_done, 1)
                    pe.wait_ge(h_ready, j + 1)
                    for c in range(FF):
                        m = nc.tensor.transpose(ps_h[:, c, :], h[:, c::FF], mat(k, "ident"))
                    m.then_inc(h_turned, 1)
                    pe.wait_ge(h_copied, j + 1)
                    for half in range(2):
                        for c in range(FF):
                            m = mm(ps_y[:, half, :], ht[:, c, :], w_d[:, c, half * HALF:(half + 1) * HALF], start=(c == 0),
                                   stop=(c == FF - 1))
                    m.then_inc(d_done, 1)

                blocks(pe, body)

            @block.scalar
            def _(act):
                def body(j):
                    act.wait_ge(x_turned, j + 1)
                    nc.scalar.copy(xt[:, :, :], ps_x[:, :, :]).then_inc(x_copied, 1)
                    act.wait_ge(gu_done, 2 * j + 1)
                    nc.scalar.activation(gate[:, :], ps_g[:, :], ACT.Silu).then_inc(silu_done, 1)

                blocks(act, body)

            @block.vector
            def _(dve):
                def body(j):
                    dve.wait_ge(silu_done, j + 1)
                    dve.wait_ge(gu_done, 2 * j + 2)
                    nc.vector.tensor_tensor(h[:, :], gate[:, :], ps_u[:, :], ALU.mult).then_inc(h_ready, 1)
                    dve.wait_ge(h_turned, j + 1)
                    nc.vector.tensor_copy(ht[:, :, :], ps_h[:, :, :]).then_inc(h_copied, 1)
                    dve.wait_ge(d_done, j + 1)
                    nc.vector.tensor_copy(y[:, :], ps_y[:, :, :].rearrange("p a b -> p (a b)")).then_inc(y_kept, 1)

                blocks(dve, body)


def combine(nc, k):
    with Space(nc, "cb") as s:
        ln = s.sb("ln", [P, 2, D])
        x1, y1, y2 = (s.sb(n, [P, NT, D]) for n in ("x1", "y1", "y2"))
        r = s.sb("r", [P, D])
        res = [s.sb(f"res{b}", [P, D]) for b in range(2)]
        stats, mv, sd, eps = s.sb("stats", [P, 2, 6]), s.sb("mv", [P, 2]), s.sb("sd", [P, 1]), s.sb("eps", [P, 1])
        stored = [s.sem(f"stored{b}") for b in range(2)]
        y_in, x_in = ([s.sem(f"{n}{t}") for t in range(NT)] for n in ("y_in", "x_in"))
        scaled, summed, ln_in, weighted, aggregated, root_done, normed, eps_set, last, halves, stood = (s.sem(n) for n in (
            "scaled", "summed", "ln_in", "weighted", "aggregated", "root_done", "normed", "eps_set", "last", "halves", "stood"))
        out_rows = k.out.rearrange("a (n p) d -> (a n) p d", p=P)

        def tiles(eng, body):
            with eng.Fori(0, NT // 2) as i:
                for b in range(2):
                    body(2 * i + b, b)

        def tile_of(t, i):
            return t[:, bass.ds(i, 1), :].rearrange("p a d -> p (a d)")

        with s.block() as block:
            @block.sync
            def _(sp):
                for b in range(2):
                    sp.sem_inc(stored[b], 16)
                for n in range(2):
                    sp.dma_start(ln[:, n, :], k.ln2[n:n + 1, :].partition_broadcast(P)).then_inc(ln_in, 16)

                def load(t):
                    sp.dma_start(x1[:, t, :], k.x1_d[t * P:(t + 1) * P, :]).then_inc(x_in[t], 16)

                load(0)
                load(1)
                for t in range(2, NT):
                    sp.wait_ge(y_in[t - 2], 32)
                    load(t)

                def store(t, b):
                    sp.wait_ge(normed, t + 3)
                    sp.dma_start(out_rows[bass.ds(t, 1)].rearrange("a p d -> (a p) d"), res[b][:, :]
                                 ).then_inc(stored[b], 16)

                tiles(sp, store)
                for b in range(2):
                    sp.wait_ge(stored[b], 16 + 8 * NT)

            @block.gpsimd
            def _(pool):
                for t in range(NT):
                    for n, y in ((0, y1), (1, y2)):
                        pool.indirect_dma_start(y[:, t, :], None, k.y_slots, bass.IndirectOffsetOnAxis(
                            ap=k.dest[:, t, n:n + 1], axis=0)).then_inc(y_in[t], 16)
                for t in range(NT):
                    pool.wait_ge(scaled, t + 1)
                    pool.wait_ge(weighted, t + 1)
                    nc.gpsimd.tensor_tensor(y1[:, t, :], y1[:, t, :], x1[:, t, :], ALU.add).then_inc(summed, 1)

            @block.scalar
            def _(act):
                act.wait_ge(eps_set, 1)

                def weigh(t):
                    act.wait_ge(x_in[t], 16)
                    nc.scalar.activation(x1[:, t, :], x1[:, t, :], ACT.Copy, scale=ALPHA).then_inc(scaled, 1)
                    act.wait_ge(y_in[t], 32)
                    nc.scalar.activation(y1[:, t, :], y1[:, t, :], ACT.Copy, scale=k.gates[:, t, 0:1]).then_inc(weighted, 1)

                weigh(0)
                for t in range(NT):
                    if t + 1 < NT:
                        weigh(t + 1)
                    act.wait_ge(aggregated, t + 1)
                    nc.scalar.activation(sd[:, :], mv[:, 1:2], ACT.Sqrt, bias=eps[:, :]).then_inc(root_done, 1)

            @block.vector
            def _(dve):
                v = nc.vector
                dve.sem_inc(normed, 2)
                v.memset(eps[:, :], LN_EPS).then_inc(eps_set, 1)
                dve.wait_ge(ln_in, 32)

                def body(t, b):
                    link = Chain(dve, last)
                    link.base = t * 4
                    dve.wait_ge(summed, t + 1)
                    dve.wait_ge(normed, t + 2)
                    link(v.scalar_tensor_tensor(r[:, :], tile_of(y2, t), tile_of(k.gates, t)[:, 1:2], tile_of(y1, t),
                                                ALU.mult, ALU.add))
                    dve.wait_ge(stored[b], (t - b) * 8 + 16)
                    layer_norm(nc, dve, link, r, res[b][:, :], ln, mv, stats, sd, halves, stood, (aggregated, 1, t + 1),
                               lambda: dve.wait_ge(root_done, t + 1)).then_inc(normed, 1)

                tiles(dve, body)


class Trunk:

    def __init__(self, a):
        self.x, self.mats_d, self.head_rows_d, self.cols_d, self.w_tiles = (
            a["x"], a["mats_d"], a["head_rows_d"], a["cols_d"], a["w_tiles"])
        self.w_fox_v, self.w_small, self.rwkv_w_up, self.rwkv_a_up, self.rwkv_g_up = (
            a["w_fox_v"], a["w_small"], a["rwkv_w_up"], a["rwkv_a_up"], a["rwkv_g_up"])
        self.f_bias, self.dt_bias, self.a_log, self.w_br, self.w_out = (
            a["f_bias"], a["dt_bias"], a["a_log"], a["w_br"], a["w_out"])
        self.ln1, self.ln2, self.router_w, self.router_b, self.exp_gate = (
            a["ln1"], a["ln2"], a["router_w"], a["router_b"], a["exp_gate"])
        self.exp_up, self.exp_down, self.out = (
            a["exp_up"], a["exp_down"], a["out"])


def trunk(nc, aps, stages=None):
    k = Trunk(aps)
    with ExitStack() as ctx:
        def sb(name, shape, dt=F32):
            return ctx.enter_context(nc.sbuf_tensor(name, shape, dt))

        k.mats = sb("mats", [P, RWKV_MATS])
        k.cols = sb("cols", [P, N_COLS])
        k.aff, k.sel = sb("aff", [P, NT, E]), sb("sel", [P, NT, E])
        k.gates = sb("gates", [P, NT, 2])
        k.dest = sb("dest", [P, NT, 2], U32)
        k.slot_token = sb("slot_token", [P, N_BLOCKS], U32)
        k.over_rows = sb("over_rows", [P, 16], U32)
        k.unused = sb("unused", [P, 16], I32)
        early = ctx.enter_context(ExitStack())
        room = early.enter_context(nc.sbuf_tensor("room", [P, NCONV - SG, T], F32))

        def scratch(name, shape):
            return nc.dram_tensor(name, shape, F32, kind="Internal").ap()

        k.chunk_ch = scratch("chunk_ch", (NT, P, RT, 4, P))
        k.chunk_tok = scratch("chunk_tok", (3, NT, P, RT, P))
        k.fox_qk = scratch("fox_qk", (2 * FH, HD, T))
        k.fox_c = scratch("fox_c", (2, FH, T))
        k.dt_d = scratch("dt_d", (SH, T))
        k.xT_d = scratch("xT_d", (KD, P, T))
        k.merged_d = scratch("merged_d", (KD, P, T))
        k.x1_d = scratch("x1_d", (T, D))
        k.buf_tok = scratch("buf_tok", (N_BLOCKS * P, 1))
        k.y_slots = scratch("y_slots", (N_BLOCKS * P, D))

        def run(*every):
            for stage in every:
                if stages is None or stage.__name__ in stages:
                    stage(nc, k)

        with ExitStack() as mixers:
            def mixer_sb(name, shape, dt=F32):
                return mixers.enter_context(nc.sbuf_tensor(name, shape, dt))

            k.mixer_oT = k.rwkv_oT = k.fox_oT = mixer_sb("mixer_oT", [P, RT, T])[:, :, :]
            k.room = room
            k.bonus, k.gate_in = room[:, 0:RT, :], room[:, RT, :]
            with ExitStack() as rwkv:
                k.xT, k.slab, k.rwkv_mats, k.decays = (rwkv.enter_context(nc.sbuf_tensor(n, shape, F32)) for n, shape in (
                    ("xT", [P, KD, T]), ("slab", [P, KD, T]), ("rwkv_mats", [P, N_MATS - RWKV_MATS]),
                    ("decays", [P, RT, NT])))
                run(transpose_x, rwkv_inputs, rwkv_chunks)
            k.x_high, k.x_low = mixer_sb("x_high", [P, KD, T], F32R), mixer_sb("x_low", [P, KD, T], F32R)
            run(rwkv_outputs)
            k.merged = room[:, 0:KD, :]
            run(merge_rwkv)
            k.fox_v = room[:, 0:4, :].rearrange("p a (b c) -> p (a b) c", c=FH * HD)
            run(fox_project, fox_attend, merge_fox)
            k.ssm = mixer_sb("ssm", [P, NCONV, T])
            k.ssm_tok = room[:, :, :].rearrange("p a t -> p (a t)").rearrange("p (c d) -> p c d", c=NT)
            run(ssm_inputs, ssm_scan, ssm_outputs, merge_ssm)
        run(out_project)
        early.close()
        with ExitStack() as landing:
            k.landed = [landing.enter_context(nc.sbuf_tensor(f"landed{n}", [P, KD * DE], F32)) for n in range(3)]
            k.landing = [landing.enter_context(nc.semaphore(f"landing{n}")) for n in range(3)]
            run(route, experts)
        run(overflow_experts, combine)


def lay_out(inputs):
    a = {n: np.asarray(v) for n, v in inputs.items()}
    w_in = a["w_in"][0]
    fox, ssm = 1792, 1792 + 1544
    gate = ssm + 2576
    main = np.concatenate([w_in[:, :fox], w_in[:, fox:fox + 1024], w_in[:, ssm:ssm + 1024 + 1536], w_in[:, gate:]], axis=1)

    def tiles(w):
        kk, n = w.shape
        return np.ascontiguousarray(w.reshape(kk // P, P, n // P, P).transpose(2, 1, 0, 3))

    def rows(w):
        return np.ascontiguousarray(w.reshape(w.shape[0] // P, P, w.shape[1]).transpose(1, 0, 2))

    def per_channel(v):
        return v.reshape(-1, P).T

    cols = np.concatenate([
        per_channel(a["rwkv_mu"][0]), per_channel(a["rwkv_w0"][0]), per_channel(a["rwkv_a0"][0]),
        per_channel(a["rwkv_k_k"][0]), per_channel(a["rwkv_k_a"][0]), per_channel(a["rwkv_r_k"][0]),
        per_channel(a["rwkv_gn_g"][0]), per_channel(a["rwkv_gn_b"][0]), per_channel(a["ssm_conv_w"][0]),
        per_channel(a["ssm_conv_b"][0]), per_channel(np.repeat(a["ssm_d"][0], HD)), per_channel(a["ssm_norm_g"][0]),
        per_channel(a["gate_bias"][0])], axis=1)
    return {
        "x": a["x"],
        "mats_d": constant_matrices(),
        "head_rows_d": head_rows(),
        "cols_d": np.ascontiguousarray(cols),
        "w_tiles": tiles(main),
        "w_fox_v": rows(w_in[:, fox + 1024:fox + 1536]),
        "w_small": rows(np.concatenate([w_in[:, fox + 1536:fox + 1544], np.zeros((D, 24), np.float32),
                                        w_in[:, gate - SH:gate]], axis=1)),
        "rwkv_w_up": a["rwkv_w_up"][0], "rwkv_a_up": a["rwkv_a_up"][0], "rwkv_g_up": a["rwkv_g_up"][0],
        "f_bias": np.ascontiguousarray(a["fox_f_bias"].reshape(FH, 1)),
        "dt_bias": np.ascontiguousarray(a["ssm_dt_bias"].reshape(SH, 1)),
        "a_log": np.ascontiguousarray(a["ssm_a_log"].reshape(SH, 1)),
        "w_br": np.concatenate([tiles(a["w_br_rwkv"][0]), tiles(a["w_br_fox"][0]), tiles(a["w_br_ssm"][0])], axis=2),
        "w_out": rows(a["w_out"][0]),
        "ln1": np.concatenate([a["ln1_g"], a["ln1_b"]]), "ln2": np.concatenate([a["ln2_g"], a["ln2_b"]]),
        "router_w": rows(a["router_w"]),
        "router_b": a["router_bias"].reshape(1, E),
        "exp_gate": a["exp_w_gate"][0], "exp_up": a["exp_w_up"][0], "exp_down": a["exp_w_down"][0],
    }


def kernel(**inputs):
    import concourse.bacc as bacc
    from concourse.bass_utils import run_bass_kernel_spmd

    nc = bacc.Bacc("TRN2", target_bir_lowering=False, num_devices=1)
    arrays = lay_out(inputs)
    aps = {n: nc.dram_tensor(n, v.shape, mybir.dt.from_np(v.dtype), kind="ExternalInput").ap() for n, v in arrays.items()}
    aps["out"] = nc.dram_tensor("out", (1, T, D), F32, kind="ExternalOutput").ap()
    trunk(nc, aps)
    r = run_bass_kernel_spmd(nc, [arrays], core_ids=[0])
    return r.results[0]["out"]
```
